# Optimizing a Trainium2 kernel written in Bass

```python
import math
import jax
import jax.numpy as jnp
from jax import lax
import numpy as np

D_MODEL = 1024
BATCH = 1
SEQ = 256
DEPTH = 1

N_BRANCH = 3
SSM_GROUP_WIDTH = 16
SSM_GROUPS = 16
D_SSM = SSM_GROUP_WIDTH * SSM_GROUPS
SSM_STATE = 64
SSM_DT_MIN = 1e-3
SSM_DT_MAX = 1e-1
HGRN_HEADS = 4
HGRN_KDIM = 64
HGRN_VDIM = 64
D_HGRN_K = HGRN_HEADS * HGRN_KDIM
D_HGRN_V = HGRN_HEADS * HGRN_VDIM
HGRN_CHUNK = 64
MOBA_HEADS = 4
MOBA_HEAD_DIM = 64
D_MOBA = MOBA_HEADS * MOBA_HEAD_DIM
MOBA_BLOCK = 256
MOBA_TOPK = 3
MOBA_QUERY_BLOCK = 32
IN_WIDTHS = (D_SSM, D_HGRN_K, D_HGRN_K, D_HGRN_V, D_HGRN_V, D_MOBA, D_MOBA, D_MOBA, N_BRANCH * D_MODEL)
D_IN = sum(IN_WIDTHS)
N_EXPERTS = 64
TOP_K = 6
D_EXPERT = 256
D_SHARED = 256
ROUTED_SCALE = 2.5
MOE_ROW_BLOCK = 256
N_MOD = 6
EPS = 1e-6

kernel_name = 'hybrid_s5_hgrn2_moba_moe_adaln'

def rms_norm(x, gain):
    xf = x.astype(jnp.float32)
    y = xf * lax.rsqrt(jnp.mean(xf * xf, axis=-1, keepdims=True) + EPS)
    return y * gain.astype(jnp.float32)

def _complex_affine_combine(earlier, later):
    a1r, a1i, b1r, b1i = earlier
    a2r, a2i, b2r, b2i = later
    return (a2r * a1r - a2i * a1i,
            a2r * a1i + a2i * a1r,
            a2r * b1r - a2i * b1i + b2r,
            a2r * b1i + a2i * b1r + b2i)

def s5_mixer(u, log_dt, lam_re, lam_im, b_re, b_im, c_re, c_im, d_skip, w_glu):
    bsz, seq, _ = u.shape
    f32 = jnp.float32
    ug = u.astype(f32).reshape(bsz, seq, SSM_GROUPS, SSM_GROUP_WIDTH)
    dt = jnp.exp(log_dt.astype(f32))[:, None]
    lr, li = lam_re.astype(f32), lam_im.astype(f32)
    mag = jnp.exp(lr * dt)
    abar_r, abar_i = mag * jnp.cos(li * dt), mag * jnp.sin(li * dt)
    inv = 1.0 / (lr * lr + li * li)
    coef_r = ((abar_r - 1.0) * lr + abar_i * li) * inv
    coef_i = (abar_i * lr - (abar_r - 1.0) * li) * inv
    br, bi = b_re.astype(f32), b_im.astype(f32)
    bbar_r = coef_r[..., None] * br - coef_i[..., None] * bi
    bbar_i = coef_r[..., None] * bi + coef_i[..., None] * br
    bu_r = jnp.einsum('blgh,gph->blgp', ug, bbar_r)
    bu_i = jnp.einsum('blgh,gph->blgp', ug, bbar_i)
    shp = (1, seq, SSM_GROUPS, SSM_STATE)
    a_r = jnp.broadcast_to(abar_r, shp)
    a_i = jnp.broadcast_to(abar_i, shp)
    _, _, s_r, s_i = lax.associative_scan(_complex_affine_combine, (a_r, a_i, bu_r, bu_i), axis=1)
    y = (jnp.einsum('blgp,ghp->blgh', s_r, c_re.astype(f32))
         - jnp.einsum('blgp,ghp->blgh', s_i, c_im.astype(f32)))
    y = (y + d_skip.astype(f32).reshape(SSM_GROUPS, SSM_GROUP_WIDTH) * ug).reshape(bsz, seq, D_SSM)
    z = (jax.nn.gelu(y).astype(u.dtype) @ w_glu).astype(f32)
    return z[..., :D_MODEL] * jax.nn.sigmoid(z[..., D_MODEL:])

def hgrn2_mixer(q, f_raw, inp, g, lower_bound, norm_g, w_o):
    bsz, seq, _ = q.shape
    f32 = jnp.float32
    n_chunks = seq // HGRN_CHUNK
    lb = lower_bound.astype(f32)
    forget = lb + (1.0 - lb) * jax.nn.sigmoid(f_raw.astype(f32))
    log_f = jnp.log(forget)
    key = 1.0 - forget

    def chunks(t, dim):
        return t.astype(f32).reshape(bsz, n_chunks, HGRN_CHUNK, HGRN_HEADS, dim).transpose(1, 0, 3, 2, 4)

    xs = (chunks(q, HGRN_KDIM), chunks(log_f, HGRN_KDIM), chunks(key, HGRN_KDIM), chunks(inp, HGRN_VDIM))
    causal = jnp.tril(jnp.ones((HGRN_CHUNK, HGRN_CHUNK), dtype=bool))[:, :, None]

    def step(state, xc):
        qc, lfc, kc, ic = xc
        cum = jnp.cumsum(lfc, axis=2)
        rel = cum[:, :, :, None, :] - cum[:, :, None, :, :]
        decay = jnp.exp(jnp.where(causal, rel, -jnp.inf))
        scores = jnp.einsum('bhtk,bhtsk,bhsk->bhts', qc, decay, kc)
        out = (jnp.einsum('bhts,bhsv->bhtv', scores, ic)
               + jnp.einsum('bhtk,bhkv->bhtv', qc * jnp.exp(cum), state))
        last = cum[:, :, -1, :]
        state = (jnp.exp(last)[..., None] * state
                 + jnp.einsum('bhsk,bhsv->bhkv', kc * jnp.exp(last[:, :, None, :] - cum), ic))
        return state, out

    s0 = jnp.zeros((bsz, HGRN_HEADS, HGRN_KDIM, HGRN_VDIM), f32)
    _, o = lax.scan(step, s0, xs)
    o = o.transpose(1, 0, 3, 2, 4).reshape(bsz, seq, HGRN_HEADS, HGRN_VDIM)
    o = rms_norm(o, norm_g) * jax.nn.silu(g.astype(f32).reshape(bsz, seq, HGRN_HEADS, HGRN_VDIM))
    return o.reshape(bsz, seq, D_HGRN_V).astype(q.dtype) @ w_o

def moba_mixer(q, k, v, q_norm_g, k_norm_g, w_o):
    bsz, seq, _ = q.shape
    f32 = jnp.float32
    hs = (bsz, seq, MOBA_HEADS, MOBA_HEAD_DIM)
    qh = rms_norm(q.reshape(hs), q_norm_g).transpose(0, 2, 1, 3) * (MOBA_HEAD_DIM ** -0.5)
    kh = rms_norm(k.reshape(hs), k_norm_g).transpose(0, 2, 1, 3)
    vh = v.astype(f32).reshape(hs).transpose(0, 2, 1, 3)
    n_blocks = -(-seq // MOBA_BLOCK)
    pad = ((0, 0), (0, 0), (0, n_blocks * MOBA_BLOCK - seq), (0, 0))
    kb = jnp.pad(kh, pad).reshape(bsz, MOBA_HEADS, n_blocks, MOBA_BLOCK, MOBA_HEAD_DIM)
    vb = jnp.pad(vh, pad).reshape(bsz, MOBA_HEADS, n_blocks, MOBA_BLOCK, MOBA_HEAD_DIM)
    kmean = jnp.mean(kb, axis=3)
    n_sel = min(MOBA_TOPK, n_blocks)
    b_ix = jnp.arange(bsz)[:, None, None, None]
    h_ix = jnp.arange(MOBA_HEADS)[None, :, None, None]
    block_ids = jnp.arange(n_blocks)
    key_offs = jnp.arange(MOBA_BLOCK)
    q_offs = jnp.arange(MOBA_QUERY_BLOCK)

    def query_block(qi):
        t0 = qi * MOBA_QUERY_BLOCK
        qc = lax.dynamic_slice_in_dim(qh, t0, MOBA_QUERY_BLOCK, axis=2)
        qpos = t0 + q_offs
        own = t0 // MOBA_BLOCK
        k_own = lax.dynamic_index_in_dim(kb, own, axis=2, keepdims=False)
        v_own = lax.dynamic_index_in_dim(vb, own, axis=2, keepdims=False)
        s_own = jnp.einsum('bhqd,bhnd->bhqn', qc, k_own)
        s_own = jnp.where((own * MOBA_BLOCK + key_offs)[None, :] <= qpos[:, None], s_own, -jnp.inf)
        gate = jnp.einsum('bhqd,bhjd->bhqj', qc, kmean)
        gate = jnp.where(block_ids < own, gate, -jnp.inf)
        _, sel = lax.top_k(gate, n_sel)
        valid = sel < own
        k_sel = kb[b_ix, h_ix, sel]
        v_sel = vb[b_ix, h_ix, sel]
        s_sel = jnp.einsum('bhqd,bhqjnd->bhqjn', qc, k_sel)
        s_sel = jnp.where(valid[..., None], s_sel, -jnp.inf)
        s = jnp.concatenate(
            [s_own, s_sel.reshape(bsz, MOBA_HEADS, MOBA_QUERY_BLOCK, n_sel * MOBA_BLOCK)], axis=-1)
        p = jax.nn.softmax(s, axis=-1)
        p_own = p[..., :MOBA_BLOCK]
        p_sel = p[..., MOBA_BLOCK:].reshape(bsz, MOBA_HEADS, MOBA_QUERY_BLOCK, n_sel, MOBA_BLOCK)
        return (jnp.einsum('bhqn,bhnd->bhqd', p_own, v_own)
                + jnp.einsum('bhqjn,bhqjnd->bhqd', p_sel, v_sel))

    o = lax.map(query_block, jnp.arange(seq // MOBA_QUERY_BLOCK))
    o = o.transpose(1, 0, 3, 2, 4).reshape(bsz, seq, D_MOBA)
    return o.astype(q.dtype) @ w_o

def moe_ffn(h, router_w, router_bias, w_gate, w_up, w_down, s_gate, s_up, s_down):
    bsz, seq, dm = h.shape
    f32 = jnp.float32
    n_tok = bsz * seq
    hf = h.reshape(n_tok, dm)
    scores = jax.nn.sigmoid((hf @ router_w).astype(f32))
    _, top_idx = lax.top_k(scores + router_bias.astype(f32), TOP_K)
    top_s = jnp.take_along_axis(scores, top_idx, axis=-1)
    top_w = top_s / jnp.sum(top_s, axis=-1, keepdims=True) * ROUTED_SCALE
    n_assign = n_tok * TOP_K
    e_flat = top_idx.reshape(n_assign)
    t_flat = jnp.repeat(jnp.arange(n_tok, dtype=jnp.int32), TOP_K)
    w_flat = top_w.reshape(n_assign)
    order = jnp.argsort(e_flat)
    e_sorted = e_flat[order]
    counts = jnp.bincount(e_flat, length=N_EXPERTS)
    starts = jnp.cumsum(counts) - counts
    padded = (counts + MOE_ROW_BLOCK - 1) // MOE_ROW_BLOCK * MOE_ROW_BLOCK
    padded_end = jnp.cumsum(padded)
    dest = (padded_end - padded)[e_sorted] + jnp.arange(n_assign) - starts[e_sorted]
    n_blocks = -(-n_assign // MOE_ROW_BLOCK) + N_EXPERTS
    n_rows = n_blocks * MOE_ROW_BLOCK
    row_tok = jnp.full((n_rows,), n_tok, jnp.int32).at[dest].set(t_flat[order])
    row_w = jnp.zeros((n_rows,), f32).at[dest].set(w_flat[order])
    block_expert = jnp.minimum(
        jnp.searchsorted(padded_end, jnp.arange(n_blocks) * MOE_ROW_BLOCK, side='right'), N_EXPERTS - 1)

    def block(acc, bi):
        rows = lax.dynamic_slice_in_dim(row_tok, bi * MOE_ROW_BLOCK, MOE_ROW_BLOCK)
        wts = lax.dynamic_slice_in_dim(row_w, bi * MOE_ROW_BLOCK, MOE_ROW_BLOCK)
        e = block_expert[bi]
        xb = jnp.take(hf, rows, axis=0, mode='fill', fill_value=0)
        hid = jax.nn.silu(xb @ w_gate[e]) * (xb @ w_up[e])
        yb = (hid @ w_down[e]).astype(f32) * wts[:, None]
        return acc.at[rows].add(yb, mode='drop'), None

    routed, _ = lax.scan(block, jnp.zeros((n_tok, dm), f32), jnp.arange(n_blocks))
    shared = (jax.nn.silu(hf @ s_gate) * (hf @ s_up)) @ s_down
    return (routed + shared.astype(f32)).reshape(bsz, seq, dm)

def setup_inputs(seed: int = 0) -> dict:
    key = jax.random.key(seed)
    k = jax.random.split(key, 32)
    f32 = jnp.float32

    def normal(kk, shape, scale):
        return jax.random.normal(kk, shape, f32) * scale

    def gain(kk, shape):
        return 1.0 + normal(kk, shape, 0.02)

    L, D, G, P, GW = DEPTH, D_MODEL, SSM_GROUPS, SSM_STATE, SSM_GROUP_WIDTH
    lam_im_base = jnp.pi * jnp.arange(P, dtype=f32)
    return {
        'x': normal(k[0], (BATCH, SEQ, D), 1.0),
        'c': normal(k[1], (BATCH, D), 1.0),
        'ada_w': normal(k[2], (L, D, N_MOD * D), 0.5 * D ** -0.5),
        'ada_b': normal(k[3], (L, N_MOD * D), 0.02),
        'norm1_g': gain(k[4], (L, D)),
        'w_in': normal(k[5], (L, D, D_IN), D ** -0.5),
        'ssm_log_dt': jax.random.uniform(k[6], (L, G), f32, math.log(SSM_DT_MIN), math.log(SSM_DT_MAX)),
        'ssm_lambda_re': -0.5 + normal(k[7], (L, G, P), 0.01),
        'ssm_lambda_im': lam_im_base + normal(k[8], (L, G, P), 0.01),
        'ssm_b_re': normal(k[9], (L, G, P, GW), (2 * GW) ** -0.5),
        'ssm_b_im': normal(k[10], (L, G, P, GW), (2 * GW) ** -0.5),
        'ssm_c_re': normal(k[11], (L, G, GW, P), (2 * P) ** -0.5),
        'ssm_c_im': normal(k[12], (L, G, GW, P), (2 * P) ** -0.5),
        'ssm_d': normal(k[13], (L, D_SSM), 1.0),
        'ssm_w_glu': normal(k[14], (L, D_SSM, 2 * D), D_SSM ** -0.5),
        'hgrn_lb_logits': normal(k[15], (L, D_HGRN_K), 1.0),
        'hgrn_norm_g': gain(k[16], (L, HGRN_VDIM)),
        'hgrn_w_o': normal(k[17], (L, D_HGRN_V, D), D_HGRN_V ** -0.5),
        'moba_q_norm_g': gain(k[18], (L, MOBA_HEAD_DIM)),
        'moba_k_norm_g': gain(k[19], (L, MOBA_HEAD_DIM)),
        'moba_w_o': normal(k[20], (L, D_MOBA, D), D_MOBA ** -0.5),
        'w_out': normal(k[21], (L, D, D), D ** -0.5),
        'norm2_g': gain(k[22], (L, D)),
        'router_w': normal(k[23], (L, D, N_EXPERTS), D ** -0.5),
        'router_bias': normal(k[24], (L, N_EXPERTS), 0.01),
        'exp_w_gate': normal(k[25], (L, N_EXPERTS, D, D_EXPERT), D ** -0.5),
        'exp_w_up': normal(k[26], (L, N_EXPERTS, D, D_EXPERT), D ** -0.5),
        'exp_w_down': normal(k[27], (L, N_EXPERTS, D_EXPERT, D), D_EXPERT ** -0.5),
        'shared_w_gate': normal(k[28], (L, D, D_SHARED), D ** -0.5),
        'shared_w_up': normal(k[29], (L, D, D_SHARED), D ** -0.5),
        'shared_w_down': normal(k[30], (L, D_SHARED, D), D_SHARED ** -0.5),
    }

def reference(x, c, ada_w, ada_b, norm1_g, w_in, ssm_log_dt, ssm_lambda_re, ssm_lambda_im,
              ssm_b_re, ssm_b_im, ssm_c_re, ssm_c_im, ssm_d, ssm_w_glu, hgrn_lb_logits,
              hgrn_norm_g, hgrn_w_o, moba_q_norm_g, moba_k_norm_g, moba_w_o, w_out, norm2_g,
              router_w, router_bias, exp_w_gate, exp_w_up, exp_w_down, shared_w_gate,
              shared_w_up, shared_w_down):
    f32 = jnp.float32
    bsz, seq, _ = x.shape
    lb_cum = jnp.cumsum(jax.nn.softmax(hgrn_lb_logits.astype(f32), axis=0), axis=0)
    lower_bounds = lb_cum - lb_cum[0:1]
    cond = jax.nn.silu(c.astype(f32))
    splits = np.cumsum(IN_WIDTHS)[:-1].tolist()
    for l in range(DEPTH):
        mod = cond @ ada_w[l].astype(f32) + ada_b[l].astype(f32)
        shift1, scale1, gate1, shift2, scale2, gate2 = [m[:, None, :] for m in jnp.split(mod, N_MOD, axis=-1)]
        h = (rms_norm(x, norm1_g[l]) * (1.0 + scale1) + shift1).astype(x.dtype)
        proj = h @ w_in[l]
        u, hq, hf, hi, hg, mq, mk, mv, gl = jnp.split(proj, splits, axis=-1)
        y_a = s5_mixer(u, ssm_log_dt[l], ssm_lambda_re[l], ssm_lambda_im[l], ssm_b_re[l], ssm_b_im[l],
                       ssm_c_re[l], ssm_c_im[l], ssm_d[l], ssm_w_glu[l])
        y_b = hgrn2_mixer(hq, hf, hi, hg, lower_bounds[l], hgrn_norm_g[l], hgrn_w_o[l])
        y_c = moba_mixer(mq, mk, mv, moba_q_norm_g[l], moba_k_norm_g[l], moba_w_o[l])
        gates = jax.nn.sigmoid(gl.astype(f32)).reshape(bsz, seq, N_BRANCH, D_MODEL)
        merged = gates[:, :, 0] * y_a + gates[:, :, 1] * y_b + gates[:, :, 2] * y_c
        x = x + (gate1 * (merged.astype(x.dtype) @ w_out[l])).astype(x.dtype)
        h2 = (rms_norm(x, norm2_g[l]) * (1.0 + scale2) + shift2).astype(x.dtype)
        y_ffn = moe_ffn(h2, router_w[l], router_bias[l], exp_w_gate[l], exp_w_up[l], exp_w_down[l],
                        shared_w_gate[l], shared_w_up[l], shared_w_down[l])
        x = x + (gate2 * y_ffn).astype(x.dtype)
    return x


_drawn_inputs = setup_inputs


def setup_inputs(seed=0):
    import zlib

    import numpy as np

    out = dict(_drawn_inputs(seed))
    spreads = {}
    factors = {'norm1_g': 3.102,
     'ssm_log_dt': 22.001,
     'ssm_lambda_re': 64.0,
     'ssm_lambda_im': 24.433,
     'ssm_b_re': 35.824,
     'ssm_b_im': 32.809,
     'ssm_c_re': 48.08,
     'ssm_c_im': 28.616,
     'hgrn_norm_g': 4.198,
     'moba_q_norm_g': 7.652,
     'moba_k_norm_g': 8.0,
     'norm2_g': 3.921}
    for name, (base, spread) in spreads.items():
        noise = np.random.default_rng([zlib.crc32(name.encode()), seed]).standard_normal(out[name].shape)
        drawn = base * np.exp(spread * noise) if base else spread * noise
        out[name] = jnp.asarray(drawn.astype(out[name].dtype))
    for name, factor in factors.items():
        out[name] = (out[name] * factor).astype(out[name].dtype)
    return out
```

```python
import math
from contextlib import ExitStack

import concourse.bass as bass
from concourse import mybir

F32 = mybir.dt.float32
BF16 = mybir.dt.bfloat16
I32 = mybir.dt.int32
U8 = mybir.dt.uint8
U32 = mybir.dt.uint32
ALU = mybir.AluOpType
ACT = mybir.ActivationFunctionType
AX = mybir.AxisListType

D = 1024
T = 256
PT = 128
TT = T // PT
KC = D // 128
HEADS = 4
HD = 64
NSTATE_TILES = 8
E = 64
FE = 256
SLOTS = 64
MAX_ROUNDS = T // SLOTS
TOP = 6
WSLOTS = 4
WCOLS = 6144
BLK = WCOLS // KC
EPS = 1e-6
ROUTED_SCALE = 2.5
MAGIC = 12582912.0
TWO_PI = 2 * math.pi
TP1 = 6.28125
TP2 = 0.0019350051879882812
TP3 = TWO_PI - TP1 - TP2
NEG = -1e30

R_C, R_N1, R_N2, R_ADAB = 0, 8, 16, 24
R_D, R_LB, R_QG, R_KG = 72, 74, 76, 77
R_LRE, R_LIM, R_LDT, R_END = 80, 88, 96, 104
SHIFT1, SCALE1, GATE1, SHIFT2, SCALE2, GATE2 = 0, 8, 16, 24, 32, 40

ADA_A = [0, 1, 2]
BLOCKS = ([("ada", n) for n in ADA_A] + [("in", n) for n in range(7)]
          + [("ada", n) for n in range(3, 8)] + [("glu", 0), ("wo", 0)] + [("out", 0), ("out", 1), ("shared", 0)])
assert len(BLOCKS) % WSLOTS == 0

GROUPS = (["vt", "adaA"] + [f"xT{i}" for i in range(4)] + ["bT", "cT", "pu", "pq", "pf", "vg0", "vg1", "mq",
          "kv0", "kv1"])
ORDER = []
for i in range(8):
    ORDER += [f"bu{i}"] + ([f"g{i}"] if i < 6 else [])
ORDER += ["qT", "kT", "g6", "sc0", "sc1", "g7", "sc2", "sc3", "g8", "pT0", "pT1", "g9", "pT2", "pT3", "mo",
          "g10", "L0a", "L0b", "g11"]
LEVELS = [1, 2, 4, 8, 16, 32, 64, 128]
for b in LEVELS[:-1]:
    ORDER += [f"L{b}a", f"L{b}b"]
ORDER += ["L128a", "L128b", "adaB", "ho", "hoT"]
GROUPS += ORDER
for j in range(KC):
    GROUPS += [f"za{j}", f"yb{j}"]
GROUPS += ["g1r0", "g1r1", "a2r0", "a2r1", "b2r0", "b2r1", "wo00", "wo01", "wo10", "wo11", "g2r0", "g2r1"]
GROUPS += [f"hT{i}" for i in range(4)] + ["rt", "sh0", "ps", "sh1"]
ROTATE = 7
AT = {name: (n % ROTATE, n // ROTATE) for n, name in enumerate(GROUPS)}
AT["sy"] = (ROTATE, 0)


def build(nc, a, out):
    ctx = ExitStack()
    with ctx:
        def sb(name, shape, dt=F32):
            return ctx.enter_context(nc.sbuf_tensor(name, shape, dt))

        def sem(name):
            return ctx.enter_context(nc.semaphore(name))

        ring = [sb(f"ring{n}", [128, WCOLS]) for n in range(WSLOTS)]
        ident = sb("ident", [128, 128])
        ones = sb("ones", [128, 128])
        before = sb("before", [128, 128])
        upto = sb("upto", [128, 128])
        causal = sb("causal", [128, 128])
        level_mask = sb("level_mask", [128, 7, 128], U8)
        iota_e = sb("iota_e", [128, E])
        rows = sb("rows", [128, 128])
        log_dt = sb("log_dt", [128, 2])
        eps = sb("eps", [128, 1])
        cols = sb("cols", [128, R_END])
        cond = sb("cond", [128, KC])
        mod = sb("mod", [128, 48])
        a1 = sb("a1", [128, KC])
        a2 = sb("a2", [128, KC])
        bias_row = sb("bias_row", [128, E])
        hg_gain = sb("hg_gain", [128, HD])
        st = sb("st", [128, 64])
        sc = sb("sc", [128, 24, NSTATE_TILES])
        r3 = sb("r3", [128, 1536])
        pools = r3[:, 0:1024].rearrange("p (k r q x) -> p k r q x", k=2, r=2, q=2)
        bsrc = r3[:, 1024:1280].rearrange("p (r i h) -> p r i h", r=2, i=NSTATE_TILES)
        csrc = r3[:, 1280:1536].rearrange("p (r m s) -> p r m s", r=2, m=2)
        bt = sb("bt", [128, 4, 128])
        ct = sb("ct", [128, 4, 128])
        par = sb("par", [128, 4])
        par_i = sb("par_i", [128, 2], I32)
        rounds_i = sb("rounds_i", [128, 1], I32)

        xs = sb("xs", [128, TT, D])
        hT = sb("hT", [128, KC, T])
        merged = hT
        act = sb("act", [128, 24 * 256])
        r1 = sb("r1", [128, 24 * 256])
        r2 = sb("r2", [128, 26 * 256])
        gates = r1[:, :].rearrange("p (g t) -> p g t", g=24)

        row_i, col_i, xor_i = [act[:, 128 * n:128 * (n + 1)].bitcast(I32) for n in range(3)]

        def two(n):
            return act[:, 512 * n:512 * (n + 1)].rearrange("p (m t) -> p m t", m=2)

        uT, qT, key, logf, cum64, cumall, hi, hg, mq, mk, mv, keepm = [two(n) for n in range(12)]
        ogT = logf
        flat = lambda v: v.rearrange("p m t -> p (m t)")
        cosT = r2[:, 0:2048].rearrange("p (i t) -> p i t", i=8)
        sinT = r2[:, 2048:4096].rearrange("p (i t) -> p i t", i=8)
        s5tmp = r2[:, 4096:6656].rearrange("p (n t) -> p n t", n=5)
        expo = r2[:, 0:512]
        qe = r2[:, 512:1024].rearrange("p (m t) -> p m t", m=2)
        ke = r2[:, 1024:1536].rearrange("p (m t) -> p m t", m=2)
        score_h = r2[:, 1536:2560].rearrange("p (n t) -> p n t", n=8)
        score_x = r2[:, 2560:3072].rearrange("p (n t) -> p n t", n=4)
        x1 = r2[:, 4096:6144].rearrange("p (m t) -> p m t", m=2)
        prob = act[:, 4096:4864].rearrange("p (h s) -> p h s", h=2)
        probT = r3[:, :].rearrange("p (h s) -> p h s", h=HEADS)
        qn, kn, mo = [xs[:, 0, 512 * n:512 * n + 512].rearrange("p (m t) -> p m t", m=2) if n < 2
                      else xs[:, 1, 0:512].rearrange("p (m t) -> p m t", m=2) for n in range(3)]
        tmp = sb("tmp", [128, 1024])
        tmp2 = xs[:, 1, 512:1024]
        g1row, a2row, b2row, g2row = [act[:, 1024 * n:1024 * (n + 1)] for n in range(4)]
        diag = r2[:, 0:1024].rearrange("p (c t) -> p c t", c=8)
        hp = xs
        parts = [r1[:, 1024 * n:1024 * (n + 1)].bitcast(BF16).rearrange("p (m t) -> p m t", m=2) for n in range(3)]
        h2T = r1[:, 3072:5120].rearrange("p (c t) -> p c t", c=8)
        hidS = hT[:, 0:2, :]
        silS = hT[:, 2:4, :]
        xe = [hT[:, 0:4, :].rearrange("p c t -> p (c t)").rearrange("p (c s) -> p c s", c=8),
              hT[:, 4:8, :].rearrange("p c t -> p (c t)").rearrange("p (c s) -> p c s", c=8)]
        ysb = r1[:, 5120:6144]
        sel = [act[:, 4096 + 128 * n:4224 + 128 * n].bitcast(BF16).rearrange("p (m s) -> p m s", m=2) for n in range(2)]
        selw = [act[:, 4352 + 256 * n:4608 + 256 * n].rearrange("p (m s) -> p m s", m=2) for n in range(2)]
        swt = act[:, 4864:5120]
        hid = act[:, 5120:5376].rearrange("p (e j s) -> p e j s", e=2, j=2)
        sil = act[:, 5376:5632].rearrange("p (e j s) -> p e j s", e=2, j=2)
        ro = act[:, 0:512]
        router = act[:, 512:1024].rearrange("p (c e) -> p c e", c=KC)
        s_r, b_r, m_r = [ro[:, 128 * n:128 * n + 128].rearrange("p (m e) -> p m e", m=2) for n in range(3)]
        w_r = ro[:, 384:512].rearrange("p (m e) -> p m e", m=2)
        onehot = tmp[:, 0:768].rearrange("p (m e k) -> p m e k", m=2, k=TOP)
        top8 = sb("top8", [128, 2, 8])
        idx8 = sb("idx8", [128, 2, 8], U32)
        idxf = sb("idxf", [128, 2, 8])
        NPOS = MAX_ROUNDS * E + 2
        pos_all, w_all = [r3[:, 2 * NPOS * n:2 * NPOS * (n + 1)].rearrange("p (m e) -> p m e", m=2) for n in range(2)]

        ps = [ctx.enter_context(nc.psum_tensor(f"bank{n}", [128, 512], F32)) for n in range(8)]

        w_full = [sem(f"w_full{n}") for n in range(WSLOTS)]
        w_free = sem("w_free")
        gu_full = [sem(f"gu_full{n}") for n in range(WSLOTS)]
        dn_full = [sem(f"dn_full{n}") for n in range(WSLOTS)]
        bank_full = [sem(f"bank_full{n}") for n in range(8)]
        bank_free = [sem(f"bank_free{n}") for n in range(8)]
        consts = sem("consts")
        small_in = sem("small_in")
        rows_ready = sem("rows_ready")
        x_in = sem("x_in")
        s5_in = sem("s5_in")
        bcast_in = sem("bcast_in")
        router_in = sem("router_in")
        x_again = sem("x_again")
        dve_seq, act_seq, pool_seq = sem("dve_seq"), sem("act_seq"), sem("pool_seq")
        cond_ready, rowsq, xn_ready = sem("cond_ready"), sem("rowsq"), sem("xn_ready")
        theta_ready, trig_ready = sem("theta_ready"), sem("trig_ready")
        bc_ready = sem("bc_ready")
        bct_ready = sem("bct_ready")
        hT_ready, u_ready, f_exp, f_ready, logf_ready = (sem(n) for n in
                                                         ("hT_ready", "u_ready", "f_exp", "f_ready", "logf_ready"))
        vals_ready, qknorm_ready, qkT_ready = sem("vals_ready"), sem("qknorm_ready"), sem("qkT_ready")
        s5_state, s5_y, s5_tanh, s5_ready = sem("s5_state"), sem("s5_y"), sem("s5_tanh"), sem("s5_ready")
        sm_max, sm_exp, prob_ready, probT_ready, mo_ready = (sem(n) for n in
                                                             ("sm_max", "sm_exp", "prob_ready", "probT_ready", "mo_ready"))
        lv_arg, lv_exp, lv_ready, score_ready = (sem(n) for n in ("lv_arg", "lv_exp", "lv_ready", "score_ready"))
        o_sq, o_silu, o_ready = (sem(n) for n in ("o_sq", "o_silu", "o_ready"))
        qk_sq = sem("qk_sq")
        gate_ready, zs_ready, merged_ready = sem("gate_ready"), sem("zs_ready"), sem("merged_ready")
        mod_ready, diag_ready, row_ready = sem("mod_ready"), sem("diag_ready"), sem("row_ready")
        x1_ready, x1_sq, h2_ready, part_ready, h2T_ready = (sem(n) for n in
                                                            ("x1_ready", "x1_sq", "h2_ready", "part_ready", "h2T_ready"))
        part_a = sem("part_a")
        r_exp, mask_ready, route_ready, rounds_ready = (sem(n) for n in
                                                        ("r_exp", "mask_ready", "route_ready", "rounds_ready"))
        sh_silu, sh_hid, acc_init = sem("sh_silu"), sem("sh_hid"), sem("acc_init")
        sel_ready, g_done, xe_full, swt_done, swt_full = (sem(n) for n in
                                                          ("sel_ready", "g_done", "xe_full", "swt_done", "swt_full"))
        gu_done, silu_done, hid_full, y_done, y0_full, y1_full, acc_done = (
            sem(n) for n in ("gu_done", "silu_done", "hid_full", "y_done", "y0_full", "y1_full", "acc_done"))
        outs_ready, stored = sem("outs_ready"), sem("stored")

        block = ctx.enter_context(nc.Block())

        n_dma = {"wo": 2, "shared": 3}
        landed, seen = {}, [0] * WSLOTS
        for s, blk in enumerate(BLOCKS):
            seen[s % WSLOTS] += 16 * n_dma.get(blk[0], 1)
            landed[blk] = (s % WSLOTS, seen[s % WSLOTS])

        def wait_full(eng, name):
            b, n = AT[name]
            eng.wait_ge(bank_full[b], n + 1)
            return ps[b]

        def free_of(name):
            return bank_free[AT[name][0]]

        @block.sync
        def _(sp):
            def w_view(w, lo, n):
                return w[:, lo:lo + n].rearrange("(c p) n -> p c n", p=128)

            def used(blk):
                if blk == ("shared", 0):
                    sp.wait_ge(acc_init, 1)
                elif blk in LAST_GROUP:
                    b, cnt = AT[LAST_GROUP[blk]]
                    sp.wait_ge(bank_full[b], cnt + 1)
                else:
                    sp.wait_ge(w_free, [0, 1, 3, 4, 5, 6].index(blk[1]) + 1)

            ada, win, wout = a["ada_w"][0], a["w_in"][0], a["w_out"][0]
            for s, (kind, n) in enumerate(BLOCKS):
                slot = s % WSLOTS
                if s >= WSLOTS:
                    used(BLOCKS[s - WSLOTS])
                dst = ring[slot]
                if kind in ("ada", "in"):
                    w = ada if kind == "ada" else win
                    lo = BLK * n if kind == "ada" or n < 2 else (1536 if n == 2 else 2048 + BLK * (n - 3))
                    width = 512 if (kind, n) == ("in", 2) else BLK
                    sp.dma_start(dst[:, 0:KC * width].rearrange("p (c n) -> p c n", c=KC),
                                 w_view(w, lo, width)).then_inc(w_full[slot], 16)
                elif kind == "glu":
                    sp.dma_start(dst[:, 0:4096].rearrange("p (c n) -> p c n", c=2),
                                 w_view(a["ssm_w_glu"][0], 0, 2 * D)).then_inc(w_full[slot], 16)
                elif kind == "wo":
                    for k, w in enumerate(("hgrn_w_o", "moba_w_o")):
                        sp.dma_start(dst[:, 2048 * k:2048 * (k + 1)].rearrange("p (c n) -> p c n", c=2),
                                     w_view(a[w][0], 0, D)).then_inc(w_full[slot], 16)
                elif kind == "out":
                    sp.dma_start(dst[:, 0:4096].rearrange("p (c n) -> p c n", c=KC),
                                 w_view(wout, 512 * n, 512)).then_inc(w_full[slot], 16)
                else:
                    for k, w in enumerate(("shared_w_gate", "shared_w_up")):
                        sp.dma_start(dst[:, 2048 * k:2048 * (k + 1)].rearrange("p (c n) -> p c n", c=KC),
                                     a[w][0].rearrange("(p c) n -> p c n", c=KC)).then_inc(w_full[slot], 16)
                    sp.dma_start(dst[:, 4096:6144].rearrange("p (c n) -> p c n", c=2),
                                 w_view(a["shared_w_down"][0], 0, D)).then_inc(w_full[slot], 16)

            gate_w = a["exp_w_gate"][0].rearrange("e (p c) n -> p e (c n)", c=KC)
            up_w = a["exp_w_up"][0].rearrange("e (p c) n -> p e (c n)", c=KC)
            down_w = a["exp_w_down"][0].rearrange("e (c p) n -> p e c n", p=128)

            def load_gate_up(k, e):
                sp.dma_start(ring[k][:, 0:2048].unsqueeze(1), gate_w[:, bass.ds(e, 1), :]).then_inc(gu_full[k], 16)
                sp.dma_start(ring[k][:, 2048:4096].unsqueeze(1), up_w[:, bass.ds(e, 1), :]).then_inc(gu_full[k], 16)

            def load_down(k, e):
                sp.dma_start(ring[k][:, 4096:6144].rearrange("p (e c n) -> p e c n", e=1, c=2),
                             down_w[:, bass.ds(e, 1), :, :]).then_inc(dn_full[k], 16)

            for k in range(WSLOTS):
                used(BLOCKS[len(BLOCKS) - WSLOTS + k])
                load_gate_up(k, k)
                load_down(k, k)

            def load_four(turn, first):
                for k in range(WSLOTS):
                    sp.wait_ge(gu_done, WSLOTS * turn - 3 + k)
                    load_gate_up(k, first + k)
                    if k % 2 == 0:
                        sp.wait_ge(y_done, 4 * turn - 2 + k)
                    load_down(k, first + k)

            with sp.Fori(1, E // WSLOTS) as i:
                load_four(i, i * WSLOTS)
            sp.wait_ge(rounds_ready, 1)
            n_rounds = sp.value_load(rounds_i[0:1, 0:1], min_val=1, max_val=MAX_ROUNDS)
            with sp.If(n_rounds > 1):
                with sp.Fori(1, n_rounds) as rd:
                    with sp.Fori(0, E // WSLOTS) as i:
                        load_four(rd * (E // WSLOTS) + i, i * WSLOTS)
            for q in range(4):
                tt, h = divmod(q, 2)
                sp.wait_ge(outs_ready, q + 1)
                sp.dma_start(out[0, tt * PT:(tt + 1) * PT, 512 * h:512 * (h + 1)],
                             xs[:, tt, 512 * h:512 * (h + 1)]).then_inc(stored, 16)
            sp.wait_ge(stored, 64)
        @block.gpsimd
        def _(pool):
            n = [0]

            def link(ins):
                n[0] += 1
                ins.then_inc(pool_seq, 1)
                pool.wait_ge(pool_seq, n[0])

            link(pool.memset(ident[:, :], 0.0))
            link(pool.affine_select(out=ident[:, :], in_=ident[:, :], compare_op=ALU.not_equal, fill=1.0, base=0,
                                    pattern=[[-1, 128]], channel_multiplier=1))
            link(pool.memset(eps[:, :], EPS))
            pool.memset(ones[:, :], 1.0).then_inc(consts, 1)
            pool.iota(row_i[:, :], pattern=[[0, 128]], base=0, channel_multiplier=1).then_inc(consts, 1)
            pool.iota(col_i[:, :], pattern=[[1, 128]], base=0, channel_multiplier=0).then_inc(consts, 1)
            pool.iota(iota_e[:, :], pattern=[[1, E]], base=0, channel_multiplier=0,
                      allow_small_or_imprecise_dtypes=True).then_inc(consts, 1)
            link(pool.memset(before[:, :], 1.0))
            pool.affine_select(out=before[:, :], in_=before[:, :], compare_op=ALU.is_gt, fill=0.0, base=0,
                               pattern=[[1, 128]], channel_multiplier=-1).then_inc(consts, 1)
            link(pool.memset(upto[:, :], 1.0))
            pool.affine_select(out=upto[:, :], in_=upto[:, :], compare_op=ALU.is_ge, fill=0.0, base=0,
                               pattern=[[1, 128]], channel_multiplier=-1).then_inc(consts, 1)
            link(pool.memset(causal[:, :], 0.0))
            pool.affine_select(out=causal[:, :], in_=causal[:, :], compare_op=ALU.is_ge, fill=NEG, base=0,
                               pattern=[[-1, 128]], channel_multiplier=1).then_inc(consts, 1)
            pool.wait_ge(s5_ready, 1)
            pool.dma_start(x1, a["x"][0].rearrange("(m p) d -> p m d", p=PT)).then_inc(x_again, 16)
            for k, (src, lo, last) in enumerate(((mod, GATE1, "g1r1"), (a2, 0, "a2r1"), (mod, SHIFT2, "b2r1"),
                                                 (mod, GATE2, "g2r1"))):
                if k == 0:
                    pool.wait_ge(mod_ready, 2)
                    pool.wait_ge(score_ready, 1)
                else:
                    prev = ("g1r1", "a2r1", "b2r1")[k - 1]
                    pool.wait_ge(bank_full[AT[prev][0]], AT[prev][1] + 1)
                for c in range(KC):
                    pool.tensor_scalar(out=diag[:, c, :], in0=ident[:, :], scalar1=src[:, lo + c:lo + c + 1],
                                       scalar2=None, op0=ALU.mult).then_inc(diag_ready, 1)
            pool.wait_ge(x1_ready, 4)
            pool.dma_start(router, a["router_w"][0].rearrange("(p c) n -> p c n", c=KC)).then_inc(router_in, 16)

        @block.scalar
        def _(act_e):
            e = nc.scalar
            n = [0]

            def link(ins):
                n[0] += 1
                ins.then_inc(act_seq, 1)
                act_e.wait_ge(act_seq, n[0])

            def vec(name):
                v = a[name][0]
                return v

            def small(lo, cnt, src):
                e.dma_start(rows[lo:lo + cnt, :], src).then_inc(small_in, 16)

            x_t = a["x"][0].rearrange("(m p) d -> p m d", p=PT)
            row = lambda v: v.rearrange("(r p) -> r p", p=128)
            small(R_C, 8, row(a["c"][0]))
            e.dma_start(xs[:, :, :], x_t).then_inc(x_in, 16)
            small(R_ADAB, 48, row(a["ada_b"][0]))
            small(R_N1, 8, row(a["norm1_g"][0]))
            small(R_N2, 8, row(a["norm2_g"][0]))
            small(R_D, 2, row(a["ssm_d"][0]))
            small(R_LB, 2, row(a["hgrn_lb_logits"][0]))
            for r, nm in ((R_QG, "moba_q_norm_g"), (R_KG, "moba_k_norm_g")):
                for k in range(2):
                    e.dma_start(rows[r:r + 1, 64 * k:64 * k + 64], a[nm][0:1, :]).then_inc(small_in, 16)
            e.dma_start(rows[78:80, :], row(a["ssm_d"][0])).then_inc(small_in, 16)
            small(R_LRE, 8, a["ssm_lambda_re"][0].rearrange("(i g) p -> i (g p)", g=2))
            small(R_LIM, 8, a["ssm_lambda_im"][0].rearrange("(i g) p -> i (g p)", g=2))
            e.dma_start(log_dt[R_LDT:R_LDT + 8, :],
                        a["ssm_log_dt"][0].rearrange("(i g) -> i g", g=2)).then_inc(small_in, 16)
            for k, (bn, cn) in enumerate((("ssm_b_re", "ssm_c_re"), ("ssm_b_im", "ssm_c_im"))):
                e.dma_start(bsrc[:, k, :, :], a[bn][0].rearrange("g p h -> (g p) h").rearrange("(i q) h -> q i h", q=128)
                            ).then_inc(s5_in, 16)
                e.dma_start(csrc[:, k, :, :], a[cn][0].rearrange("g h p -> (g h) p").rearrange("(m q) p -> q m p", q=128)
                            ).then_inc(s5_in, 16)
            e.dma_start(bias_row[:, :], a["router_bias"][0:1, :].to_broadcast([128, E])).then_inc(bcast_in, 16)
            e.dma_start(hg_gain[:, :], a["hgrn_norm_g"][0:1, :].to_broadcast([128, HD])).then_inc(bcast_in, 16)

            act_e.wait_ge(x_in, 16)
            for tt in range(TT):
                if tt:
                    act_e.wait_ge(rowsq, tt)
                e.activation(tmp[:, :], xs[:, tt, :], ACT.Square, accum_out=st[:, tt:tt + 1]).then_inc(rowsq, 1)
            act_e.wait_ge(rowsq, 2)
            act_e.wait_ge(consts, 1)
            e.activation(st[:, 4:6], st[:, 0:2], ACT.Sqrt, bias=eps[:, :], scale=1.0 / D).then_inc(rowsq, 1)
            act_e.wait_ge(cond_ready, 1)
            e.activation(cond[:, :], cols[:, R_C:R_C + 8], ACT.Silu).then_inc(cond_ready, 1)
            link(e.activation(sc[:, 0, :], cols[:, R_LDT:R_LDT + 8], ACT.Exp))
            e.activation(st[:, 40:42], cols[:, R_LB:R_LB + 2], ACT.Exp, bias=0.0).then_inc(theta_ready, 1)
            act_e.wait_ge(theta_ready, 3)
            e.activation(sc[:, 4, :], sc[:, 1, :], ACT.Exp).then_inc(trig_ready, 1)
            e.activation(sc[:, 5, :], sc[:, 2, :], ACT.Sin).then_inc(trig_ready, 1)
            e.activation(sc[:, 6, :], sc[:, 3, :], ACT.Sin).then_inc(trig_ready, 1)
            for g, dst in (("bT", bt), ("cT", ct)):
                b = wait_full(act_e, g)
                e.activation(dst[:, :, :].rearrange("p a b -> p (a b)"), b[:, :], ACT.Copy).then_inc(free_of(g), 1)
            b = wait_full(act_e, "pu")
            e.activation(flat(uT), b[:, :], ACT.Copy).then_inc(free_of("pu"), 1)
            b = wait_full(act_e, "pq")
            e.activation(flat(qT), b[:, :], ACT.Copy).then_inc(free_of("pq"), 1)
            b = wait_full(act_e, "pf")
            e.activation(flat(key), b[:, :], ACT.Exp, scale=-1.0).then_inc(free_of("pf"), 1)
            act_e.wait_ge(f_ready, 1)
            e.activation(flat(logf), flat(cum64), ACT.Ln).then_inc(logf_ready, 1)
            for tt in range(TT):
                b = wait_full(act_e, f"vg{tt}")
                e.activation(hi[:, tt, :], b[:, 0:256], ACT.Copy).then_inc(vals_ready, 1)
                e.activation(hg[:, tt, :], b[:, 256:512], ACT.Copy).then_inc(free_of(f"vg{tt}"), 1)
            b = wait_full(act_e, "mq")
            e.activation(flat(mq), b[:, :], ACT.Copy).then_inc(free_of("mq"), 1)
            for tt in range(TT):
                b = wait_full(act_e, f"kv{tt}")
                e.activation(mk[:, tt, :], b[:, 0:256], ACT.Copy).then_inc(vals_ready, 1)
                e.activation(mv[:, tt, :], b[:, 256:512], ACT.Copy).then_inc(free_of(f"kv{tt}"), 1)
            act_e.wait_ge(free_of("mq"), AT["mq"][1] + 1)
            act_e.wait_ge(vals_ready, 4)
            act_e.wait_ge(rowsq, 2)
            e.activation(tmp[:, 0:512], flat(mq), ACT.Square).then_inc(qk_sq, 1)
            e.activation(tmp[:, 512:1024], flat(mk), ACT.Square).then_inc(qk_sq, 1)
            act_e.wait_ge(qk_sq, 4)
            e.activation(st[:, 48:64], st[:, 48:64], ACT.Sqrt, bias=eps[:, :], scale=1.0 / HD).then_inc(qk_sq, 1)

            def gate_tile(k):
                b = wait_full(act_e, f"g{k}")
                e.activation(gates[:, 2 * k:2 * k + 2, :].rearrange("p g t -> p (g t)"), b[:, :], ACT.Tanh,
                             scale=0.5).then_inc(free_of(f"g{k}"), 1)

            def softmax(h):
                act_e.wait_ge(sm_max, 2 * h + 2)
                for tt in range(TT):
                    lo, nn = (0, 128) if tt == 0 else (128, 256)
                    e.activation(prob[:, h % 2, lo:lo + nn], prob[:, h % 2, lo:lo + nn], ACT.Exp,
                                 bias=st[:, 8 + 2 * h + tt:9 + 2 * h + tt],
                                 accum_out=st[:, 16 + 2 * h + tt:17 + 2 * h + tt]).then_inc(sm_exp, 1)

            def level_exp(k):
                act_e.wait_ge(lv_arg, 2 * (k + 1))
                e.activation(expo, expo, ACT.Exp).then_inc(lv_exp, 1)

            for k in range(6):
                gate_tile(k)
            for g, dst, col in (("qT", qn, 2), ("kT", kn, 3)):
                act_e.wait_ge(qknorm_ready, 3)
                b = wait_full(act_e, g)
                e.activation(flat(dst), b[:, :], ACT.Copy, scale=st[:, col:col + 1]).then_inc(free_of(g), 1)
            gate_tile(6)
            act_e.wait_ge(s5_y, 1)
            e.activation(s5tmp[:, 2, :], s5tmp[:, 1, :], ACT.Tanh, scale=math.sqrt(2 / math.pi)).then_inc(s5_tanh, 1)
            softmax(0)
            softmax(1)
            gate_tile(7)
            softmax(2)
            softmax(3)
            gate_tile(8)
            for h in range(HEADS):
                b = wait_full(act_e, f"pT{h}")
                e.activation(probT[:, h, :], b[:, 0:384], ACT.Copy).then_inc(free_of(f"pT{h}"), 1)
                if h == 1:
                    gate_tile(9)
            b = wait_full(act_e, "mo")
            e.activation(flat(mo), b[:, :], ACT.Copy).then_inc(free_of("mo"), 1)
            gate_tile(10)
            level_exp(0)
            gate_tile(11)
            for k in range(1, len(LEVELS)):
                level_exp(k)
            act_e.wait_ge(free_of("vg1"), AT["vg1"][1] + 1)
            e.activation(keepm.rearrange("p m t -> p (m t)"), flat(hg), ACT.Tanh, scale=0.5).then_inc(o_silu, 1)
            b = wait_full(act_e, "ho")
            act_e.wait_ge(qk_sq, 5)
            e.activation(tmp[:, 0:512], b[:, :], ACT.Square).then_inc(o_sq, 1)
            act_e.wait_ge(o_sq, 2)
            e.activation(st[:, 48:56], st[:, 48:56], ACT.Sqrt, bias=eps[:, :], scale=1.0 / HD).then_inc(o_sq, 1)
            b = wait_full(act_e, "hoT")
            e.activation(flat(ogT), b[:, :], ACT.Copy).then_inc(free_of("hoT"), 1)
            for j in range(KC):
                b = wait_full(act_e, f"za{j}")
                if j >= 2:
                    act_e.wait_ge(merged_ready, j - 1)
                e.activation(tmp2[:, 256 * (j % 2):256 * (j % 2) + 256], b[:, 256:512], ACT.Tanh,
                             scale=0.5).then_inc(zs_ready, 1)
            for r, dst in (("g1r", g1row), ("a2r", a2row), ("b2r", b2row)):
                for h in range(2):
                    if r == "g1r" and h == 0:
                        act_e.wait_ge(merged_ready, KC)
                    b = wait_full(act_e, f"{r}{h}")
                    e.activation(dst[:, 512 * h:512 * h + 512], b[:, :], ACT.Copy).then_inc(free_of(f"{r}{h}"), 1)
            for tt in range(TT):
                act_e.wait_ge(x1_ready, 2 * (tt + 1))
                if tt:
                    act_e.wait_ge(x1_sq, tt)
                e.activation(tmp[:, :], x1[:, tt, :], ACT.Square, accum_out=st[:, 32 + tt:33 + tt]).then_inc(x1_sq, 1)
            act_e.wait_ge(x1_sq, 2)
            e.activation(st[:, 34:36], st[:, 32:34], ACT.Sqrt, bias=eps[:, :], scale=1.0 / D).then_inc(x1_sq, 1)
            for h in range(2):
                b = wait_full(act_e, f"g2r{h}")
                e.activation(g2row[:, 512 * h:512 * h + 512], b[:, :], ACT.Copy).then_inc(free_of(f"g2r{h}"), 1)
            for tt in range(TT):
                act_e.wait_ge(h2_ready, tt + 1)
                e.activation(parts[0][:, tt, :], hp[:, tt, :], ACT.Copy).then_inc(part_a, 1)
            for k in range(4):
                b = wait_full(act_e, f"hT{k}")
                e.activation(h2T[:, 2 * k:2 * k + 2, :].rearrange("p c t -> p (c t)"), b[:, :],
                             ACT.Copy).then_inc(free_of(f"hT{k}"), 1)
            b = wait_full(act_e, "rt")
            e.activation(s_r.rearrange("p m e -> p (m e)"), b[:, 0:128], ACT.Exp, scale=-1.0).then_inc(r_exp, 1)
            b = wait_full(act_e, "sh0")
            e.activation(silS.rearrange("p c t -> p (c t)"), b[:, :], ACT.Silu).then_inc(free_of("sh0"), 1)

            def take_half(pair, h, buf):
                act_e.wait_ge(g_done, 2 * pair + h + 1)
                if isinstance(pair, int) and pair == 0:
                    act_e.wait_ge(acc_init, 1)
                e.activation(xe[buf][:, 4 * h:4 * h + 4, :].rearrange("p c s -> p (c s)"), ps[4][:, :],
                             ACT.Copy).then_inc(xe_full, 1)

            take_half(0, 0, 0)
            take_half(0, 1, 0)
            act_e.wait_ge(rounds_ready, 1)
            n_rounds = act_e.value_load(rounds_i[0:1, 0:1], min_val=1, max_val=MAX_ROUNDS)
            with act_e.Fori(0, n_rounds * (E // 4)) as i:
                for k in range(2):
                    p = i * 2 + k
                    for x, bank in enumerate((6, 5)):
                        act_e.wait_ge(gu_done, 2 * p + x + 1)
                        e.activation(sil[:, x, :, :].rearrange("p j s -> p (j s)"), ps[bank][:, 0:128],
                                     ACT.Silu).then_inc(silu_done, 1)
                    take_half(p + 1, 0, 1 - k)
                    act_e.wait_ge(y_done, 2 * p + 1)
                    e.activation(ysb[:, 0:512], ps[7][:, :], ACT.Copy).then_inc(y0_full, 1)
                    take_half(p + 1, 1, 1 - k)

        @block.vector
        def _(dve):
            v = nc.vector
            n = [0]

            def link(ins):
                n[0] += 1
                ins.then_inc(dve_seq, 1)
                dve.wait_ge(dve_seq, n[0])

            def mul(o, x, y):
                link(v.tensor_tensor(o, x, y, ALU.mult))

            def add(o, x, y):
                link(v.tensor_tensor(o, x, y, ALU.add))

            def sub(o, x, y):
                link(v.tensor_tensor(o, x, y, ALU.subtract))

            def ts(o, x, s1, op0, s2=None, op1=None):
                link(v.tensor_scalar(o, x, s1, s2, op0, op1) if op1 is not None
                     else v.tensor_scalar(o, x, s1, None, op0))

            dve.wait_ge(small_in, 16 * 14)
            v.tensor_copy(rows[R_LDT:R_LDT + 8, :].rearrange("i (g p) -> i g p", g=2),
                          log_dt[R_LDT:R_LDT + 8, :].unsqueeze(2).to_broadcast([8, 2, 64])).then_inc(rows_ready, 1)
            b = wait_full(dve, "vt")
            v.tensor_copy(cols[:, :], b[:, 0:R_END]).then_inc(cond_ready, 1)
            dve.wait_ge(cond_ready, 1)
            v.tensor_copy(par[:, 0:1], cols[:, 0:1]).then_inc(free_of("vt"), 1)
            dve.wait_ge(rowsq, 3)
            link(v.reciprocal(st[:, 6:8], st[:, 4:6]))
            for tt in range(TT):
                v.tensor_scalar(xs[:, tt, :], xs[:, tt, :], st[:, 6 + tt:7 + tt], None, ALU.mult).then_inc(xn_ready, 1)
            dve.wait_ge(consts, 7)
            link(v.tensor_tensor(xor_i[:, :], row_i[:, :], col_i[:, :], ALU.bitwise_xor))
            for k, lv in enumerate(LEVELS[:-1]):
                link(v.tensor_scalar(level_mask[:, k, :], xor_i[:, :], float(lv), None, ALU.is_ge))
            link(v.tensor_scalar(par_i[:, 0:1], row_i[:, 0:1], 4, 1, ALU.logical_shift_right, ALU.bitwise_and))
            link(v.tensor_copy(par[:, 1:2], par_i[:, 0:1]))
            ts(par[:, 0:1], par[:, 1:2], -1.0, ALU.mult, 1.0, ALU.add)

            lre, lim = cols[:, R_LRE:R_LRE + 8], cols[:, R_LIM:R_LIM + 8]
            dve.wait_ge(theta_ready, 1)
            mul(sc[:, 1, :], lre, sc[:, 0, :])
            mul(sc[:, 7, :], lim, sc[:, 0, :])
            ts(sc[:, 8, :], sc[:, 7, :], 1.0 / TWO_PI, ALU.mult, MAGIC, ALU.add)
            ts(sc[:, 8, :], sc[:, 8, :], MAGIC, ALU.subtract)
            for part in (TP1, TP2, TP3):
                ts(sc[:, 9, :], sc[:, 8, :], -part, ALU.mult)
                add(sc[:, 7, :], sc[:, 7, :], sc[:, 9, :])
            v.tensor_scalar(sc[:, 2, :], sc[:, 7, :], 3.1415925, -3.1415925, ALU.min, ALU.max).then_inc(theta_ready, 1)
            v.tensor_scalar(sc[:, 3, :], sc[:, 7, :], 0.5, None, ALU.mult).then_inc(theta_ready, 1)
            dve.wait_ge(trig_ready, 3)
            mag, sn, half = sc[:, 4, :], sc[:, 5, :], sc[:, 6, :]
            cs = sc[:, 10, :]
            mul(cs, half, half)
            ts(cs, cs, -2.0, ALU.mult, 1.0, ALU.add)
            ar, ai, den, cr, ci, t0, t1 = (sc[:, k, :] for k in (11, 12, 13, 14, 15, 16, 17))
            mul(ar, mag, cs)
            mul(ai, mag, sn)
            mul(den, lre, lre)
            mul(t0, lim, lim)
            add(den, den, t0)
            link(v.reciprocal(den, den))
            ts(ar, ar, 1.0, ALU.subtract)
            mul(t0, ar, lre)
            mul(t1, ai, lim)
            add(cr, t0, t1)
            mul(cr, cr, den)
            mul(t0, ai, lre)
            mul(t1, ar, lim)
            sub(ci, t0, t1)
            mul(ci, ci, den)
            link(v.memset(r3[:, 0:512], 0.0))
            dve.wait_ge(s5_in, 64)
            bb = r3[:, 0:512].rearrange("p (r i h) -> p r i h", r=2, h=32)
            prod = s5tmp[:, 0, 0:128].rearrange("p (i h) -> p i h", h=16)
            wide = lambda col: col.unsqueeze(2).to_broadcast([128, 8, 16])
            for r, (x, y, op) in enumerate(((cr, ci, ALU.subtract), (ci, cr, ALU.add))):
                mul(prod, bsrc[:, 0, :, :], wide(x))
                other = s5tmp[:, 0, 128:256].rearrange("p (i h) -> p i h", h=16)
                mul(other, bsrc[:, 1, :, :], wide(y))
                for half_ in range(2):
                    pr = slice(64 * half_, 64 * half_ + 64)
                    link(v.tensor_tensor(bb[pr, r, :, 16 * half_:16 * half_ + 16], prod[pr], other[pr], op))
            for r in range(2):
                for half_ in range(2):
                    ins = v.tensor_scalar(pools[:, 1, r, :, 64 * half_:64 * half_ + 64], csrc[:, r, :, :],
                                          par[:, half_:half_ + 1], -1.0 if r else 1.0, ALU.mult, ALU.mult)
                    link(ins)
            v.tensor_copy(par[:, 2:3], par[:, 0:1]).then_inc(bc_ready, 1)
            ec, es, t2, t3 = (sc[:, k, :] for k in (18, 19, 20, 21))
            link(v.tensor_copy(ec, cs))
            link(v.tensor_copy(es, sn))
            link(v.memset(cosT[:, :, 0:1], 1.0))
            link(v.memset(sinT[:, :, 0:1], 0.0))
            w = 1
            while w < T:
                ecw, esw = (z.unsqueeze(2).to_broadcast([128, 8, w]) for z in (ec, es))
                ta = s5tmp[:, 0:2, :].rearrange("p a b -> p (a b)")[:, 0:8 * w].rearrange("p (i t) -> p i t", i=8)
                tb = s5tmp[:, 2:4, :].rearrange("p a b -> p (a b)")[:, 0:8 * w].rearrange("p (i t) -> p i t", i=8)
                v.tensor_tensor(ta, cosT[:, :, 0:w], ecw, ALU.mult)
                link(v.tensor_tensor(tb, sinT[:, :, 0:w], esw, ALU.mult))
                sub(cosT[:, :, w:2 * w], ta, tb)
                v.tensor_tensor(ta, cosT[:, :, 0:w], esw, ALU.mult)
                link(v.tensor_tensor(tb, sinT[:, :, 0:w], ecw, ALU.mult))
                add(sinT[:, :, w:2 * w], ta, tb)
                mul(t2, ec, ec)
                mul(t3, es, es)
                mul(es, ec, es)
                sub(ec, t2, t3)
                add(es, es, es)
                w *= 2

            b = wait_full(dve, "adaA")
            v.tensor_tensor(mod[:, 0:18], b[:, 0:18], cols[:, R_ADAB:R_ADAB + 18], ALU.add).then_inc(free_of("adaA"), 1)
            dve.wait_ge(free_of("adaA"), AT["adaA"][1] + 1)
            ts(a1[:, :], mod[:, SCALE1:SCALE1 + 8], 1.0, ALU.add)
            mul(a1[:, :], a1[:, :], cols[:, R_N1:R_N1 + 8])
            for k in range(4):
                b = wait_full(dve, f"xT{k}")
                for c in (2 * k, 2 * k + 1):
                    ins = v.tensor_scalar(hT[:, c, :], b[:, 256 * (c % 2):256 * (c % 2) + 256], a1[:, c:c + 1],
                                          mod[:, SHIFT1 + c:SHIFT1 + c + 1], ALU.mult, ALU.add)
                    if c % 2:
                        ins.then_inc(free_of(f"xT{k}"), 1)
                    else:
                        ins.then_inc(hT_ready, 1)

            e1 = st[:, 40:42]
            link(v.reciprocal(st[:, 42:44], e1))
            mul(st[:, 42:44], st[:, 42:44], e1)
            sub(st[:, 42:44], st[:, 42:44], st[:, 42:44])
            ts(st[:, 44:46], st[:, 42:44], -1.0, ALU.mult, 1.0, ALU.add)
            dve.wait_ge(free_of("pf"), AT["pf"][1] + 1)
            ts(flat(key), flat(key), 1.0, ALU.add)
            link(v.reciprocal(flat(key), flat(key)))
            for m in range(2):
                ts(cum64[:, m, :], key[:, m, :], st[:, 44 + m:45 + m], ALU.mult, st[:, 42 + m:43 + m], ALU.add)
            v.tensor_scalar(flat(key), flat(cum64), -1.0, 1.0, ALU.mult, ALU.add).then_inc(f_ready, 1)
            link(v.memset(flat(keepm), 1.0))
            for c in range(0, 512, 64):
                link(v.memset(flat(keepm)[:, c:c + 1], 0.0))
            dve.wait_ge(logf_ready, 1)
            link(v.tensor_tensor_scan(flat(cum64), flat(keepm), flat(logf), 0.0, ALU.mult, ALU.add))
            link(v.memset(keepm[:, :, 64:256:64], 1.0))
            link(v.tensor_tensor_scan(flat(cumall), flat(keepm), flat(logf), 0.0, ALU.mult, ALU.add))
            dve.wait_ge(qk_sq, 2)
            for k in range(2):
                v.tensor_reduce(st[:, 48 + 8 * k:56 + 8 * k],
                                tmp[:, 512 * k:512 * k + 512].rearrange("p (h d) -> p h d", d=HD), AX.X,
                                ALU.add).then_inc(qk_sq, 1)
            dve.wait_ge(qk_sq, 5)
            link(v.reciprocal(st[:, 48:64], st[:, 48:64]))
            for k, src in enumerate((mq, mk)):
                r8 = st[:, 48 + 8 * k:56 + 8 * k]
                v4 = flat(src).rearrange("p (h d) -> p h d", d=HD)
                v.tensor_tensor(v4, v4, r8.unsqueeze(2).to_broadcast([128, 8, HD]), ALU.mult).then_inc(qknorm_ready, 1)
            ts(st[:, 2:3], cols[:, R_QG:R_QG + 1], HD ** -0.5, ALU.mult)
            v.tensor_copy(st[:, 3:4], cols[:, R_KG:R_KG + 1]).then_inc(qknorm_ready, 1)

            A, B, W, Z, S = (s5tmp[:, k, :] for k in range(5))
            W2, Z2, S2 = W, Z, S
            for i in range(NSTATE_TILES):
                b = wait_full(dve, f"bu{i}")
                cw = cosT[:, i, :].unsqueeze(1).to_broadcast([128, 2, 256])
                sw = sinT[:, i, :].unsqueeze(1).to_broadcast([128, 2, 256])
                three = lambda z: z.rearrange("p (r t) -> p r t", r=2)
                v.tensor_tensor(three(A), three(b[:, :]), cw, ALU.mult)
                v.tensor_tensor(three(B), three(b[:, :]), sw, ALU.mult).then_inc(free_of(f"bu{i}"), 1)
                dve.wait_ge(free_of(f"bu{i}"), AT[f"bu{i}"][1] + 1)
                v.tensor_tensor(W2[:, 0:256], A[:, 0:256], B[:, 256:512], ALU.add)
                link(v.tensor_tensor(W2[:, 256:512], A[:, 256:512], B[:, 0:256], ALU.subtract))
                for r in range(2):
                    ins = v.tensor_tensor_scan(Z2[:, 256 * r:256 * r + 256], mag[:, i:i + 1].to_broadcast([128, 256]),
                                               W2[:, 256 * r:256 * r + 256], 0.0, ALU.mult, ALU.add)
                link(ins)
                v.tensor_tensor(three(A), three(Z2), cw, ALU.mult)
                link(v.tensor_tensor(three(B), three(Z2), sw, ALU.mult))
                if i:
                    dve.wait_ge(s5_state, 2 * i)
                v.tensor_tensor(S2[:, 0:256], A[:, 0:256], B[:, 256:512], ALU.subtract)
                v.tensor_tensor(S2[:, 256:512], A[:, 256:512], B[:, 0:256], ALU.add).then_inc(s5_state, 1)
                dve.wait_ge(s5_state, 2 * i + 1)
            b = wait_full(dve, "sy")
            for m in range(2):
                ins = v.scalar_tensor_tensor(out=S[:, 256 * m:256 * m + 256], in0=uT[:, m, :],
                                             scalar=cols[:, R_D + m:R_D + m + 1], in1=b[:, 256 * m:256 * m + 256],
                                             op0=ALU.mult, op1=ALU.add)
            ins.then_inc(free_of("sy"), 1)
            dve.wait_ge(free_of("sy"), AT["sy"][1] + 1)
            mul(A, S, S)
            ts(A, A, 0.044715, ALU.mult, 1.0, ALU.add)
            v.tensor_tensor(B, A, S, ALU.mult).then_inc(s5_y, 1)
            dve.wait_ge(s5_tanh, 1)
            link(v.scalar_tensor_tensor(out=B, in0=W, scalar=1.0, in1=S, op0=ALU.add, op1=ALU.mult))
            v.tensor_scalar(flat(uT), B, 0.5, None, ALU.mult).then_inc(s5_ready, 1)

            for h in range(HEADS):
                b = wait_full(dve, f"sc{h}")
                if h >= 2:
                    dve.wait_ge(bank_full[AT[f"pT{h - 2}"][0]], AT[f"pT{h - 2}"][1] + 1)
                pr = prob[:, h % 2, :]
                v.tensor_tensor(pr[:, 0:128], b[:, 0:128], causal[:, :], ALU.add)
                v.tensor_copy(pr[:, 128:256], b[:, 128:256])
                ins = v.tensor_tensor(pr[:, 256:384], b[:, 256:384], causal[:, :], ALU.add)
                ins.then_inc(free_of(f"sc{h}"), 1)
                dve.wait_ge(free_of(f"sc{h}"), AT[f"sc{h}"][1] + 1)
                for tt in range(TT):
                    lo, nn = (0, 128) if tt == 0 else (128, 256)
                    v.tensor_reduce(st[:, 8 + 2 * h + tt:9 + 2 * h + tt], pr[:, lo:lo + nn], AX.X, ALU.max,
                                    negate=True).then_inc(sm_max, 1)
                dve.wait_ge(sm_exp, 2 * h + 2)
                link(v.reciprocal(st[:, 24 + 2 * h:26 + 2 * h], st[:, 16 + 2 * h:18 + 2 * h]))
                for tt in range(TT):
                    lo, nn = (0, 128) if tt == 0 else (128, 256)
                    v.tensor_scalar(pr[:, lo:lo + nn], pr[:, lo:lo + nn], st[:, 24 + 2 * h + tt:25 + 2 * h + tt], None,
                                    ALU.mult).then_inc(prob_ready, 1)

            def take_scores(k):
                for half_, g in enumerate("ab"):
                    name = f"L{0 if k == 0 else LEVELS[k - 1]}{g}"
                    b = wait_full(dve, name)
                    dst = score_h[:, 4 * half_:4 * half_ + 4, :]
                    src = b[:, :].rearrange("p (n t) -> p n t", n=4)
                    if k == 0:
                        ins = v.tensor_copy(dst, src)
                    else:
                        ins = v.copy_predicated(dst, level_mask[:, k - 1, :].unsqueeze(1).to_broadcast([128, 4, 128]), src)
                    ins.then_inc(free_of(name), 1)

            for k, lv in enumerate(LEVELS):
                src = cum64 if lv <= 32 else cumall
                cv = flat(src).rearrange("p (n r s) -> p n r s", r=2, s=lv)
                ev = expo.rearrange("p (n r s) -> p n r s", r=2, s=lv)
                ref = cv[:, :, 0, lv - 1:lv].to_broadcast([128, 256 // lv, lv])
                if k:
                    dve.wait_ge(lv_ready, 2 * k)
                v.tensor_tensor(ev[:, :, 0, :], ref, cv[:, :, 0, :], ALU.subtract).then_inc(lv_arg, 1)
                v.tensor_tensor(ev[:, :, 1, :], cv[:, :, 1, :], ref, ALU.subtract).then_inc(lv_arg, 1)
                if k == 0:
                    take_scores(0)
                dve.wait_ge(lv_exp, k + 1)
                if k:
                    g = f"L{LEVELS[k - 1]}b"
                    dve.wait_ge(bank_full[AT[g][0]], AT[g][1] + 1)
                v.tensor_tensor(flat(qe), flat(qT), expo, ALU.mult).then_inc(lv_ready, 1)
                v.tensor_tensor(flat(ke), flat(key), expo, ALU.mult).then_inc(lv_ready, 1)
                if k:
                    g = f"L{LEVELS[k - 2] if k > 1 else 0}b"
                    dve.wait_ge(free_of(g), AT[g][1] + 1)
                    take_scores(k)
            for odd, g in enumerate("ab"):
                b = wait_full(dve, f"L128{g}")
                v.tensor_copy(score_x[:, 2 * odd:2 * odd + 2, :],
                              b[:, 0:256].rearrange("p (n t) -> p n t", n=2)).then_inc(free_of(f"L128{g}"), 1)
            dve.wait_ge(free_of("L64b"), AT["L64b"][1] + 1)
            v.tensor_tensor(score_h, score_h, upto[:, :].unsqueeze(1).to_broadcast([128, 8, 128]),
                            ALU.mult).then_inc(score_ready, 1)
            b = wait_full(dve, "adaB")
            v.tensor_tensor(mod[:, 18:48], b[:, 0:30], cols[:, R_ADAB + 18:R_ADAB + 48],
                            ALU.add).then_inc(free_of("adaB"), 1)
            dve.wait_ge(free_of("adaB"), AT["adaB"][1] + 1)
            v.tensor_scalar(a2[:, :], mod[:, SCALE2:SCALE2 + 8], 1.0, None, ALU.add).then_inc(mod_ready, 1)
            dve.wait_ge(mod_ready, 1)
            v.tensor_tensor(a2[:, :], a2[:, :], cols[:, R_N2:R_N2 + 8], ALU.mult).then_inc(mod_ready, 1)
            dve.wait_ge(o_sq, 1)
            r8 = st[:, 48:56]
            v.tensor_reduce(r8, tmp[:, 0:512].rearrange("p (h d) -> p h d", d=HD), AX.X, ALU.add).then_inc(o_sq, 1)
            dve.wait_ge(o_sq, 3)
            link(v.reciprocal(r8, r8))
            b = wait_full(dve, "ho")
            o3 = tmp[:, 0:512].rearrange("p (h d) -> p h d", d=HD)
            v.tensor_tensor(o3, b[:, :].rearrange("p (h d) -> p h d", d=HD),
                            r8.unsqueeze(2).to_broadcast([128, 8, HD]), ALU.mult).then_inc(free_of("ho"), 1)
            dve.wait_ge(free_of("ho"), AT["ho"][1] + 1)
            dve.wait_ge(bcast_in, 32)
            mul(o3, o3, hg_gain[:, :].unsqueeze(1).to_broadcast([128, 8, HD]))
            dve.wait_ge(o_silu, 1)
            km = flat(keepm)
            link(v.scalar_tensor_tensor(out=km, in0=km, scalar=1.0, in1=flat(hg), op0=ALU.add, op1=ALU.mult))
            v.scalar_tensor_tensor(out=tmp[:, 0:512], in0=km, scalar=0.5, in1=tmp[:, 0:512], op0=ALU.mult,
                                   op1=ALU.mult).then_inc(o_ready, 1)

            dve.wait_ge(free_of("g11"), AT["g11"][1] + 1)
            for k in range(3):
                g8 = gates[:, 8 * k:8 * k + 8, :].rearrange("p g t -> p (g t)")
                link(v.tensor_scalar(g8, g8, 0.5, 0.5, ALU.mult, ALU.add))
            for j in range(KC):
                if j:
                    dve.wait_ge(merged_ready, j)
                dve.wait_ge(zs_ready, j + 1)
                b = ps[AT[f"za{j}"][0]]
                z = tmp2[:, 256 * (j % 2):256 * (j % 2) + 256]
                link(v.scalar_tensor_tensor(out=z, in0=z, scalar=1.0, in1=b[:, 0:256], op0=ALU.add, op1=ALU.mult))
                v.scalar_tensor_tensor(out=z, in0=z, scalar=0.5, in1=gates[:, j, :], op0=ALU.mult,
                                       op1=ALU.mult).then_inc(free_of(f"za{j}"), 1)
                b = wait_full(dve, f"yb{j}")
                y1, y2 = tmp[:, 512:768], tmp[:, 768:1024]
                v.tensor_tensor(y1, b[:, 0:256], gates[:, 8 + j, :], ALU.mult)
                v.tensor_tensor(y2, b[:, 256:512], gates[:, 16 + j, :], ALU.mult).then_inc(free_of(f"yb{j}"), 1)
                dve.wait_ge(free_of(f"yb{j}"), AT[f"yb{j}"][1] + 1)
                add(y1, y1, y2)
                v.tensor_tensor(merged[:, j, :], y1, z, ALU.add).then_inc(merged_ready, 1)
            dve.wait_ge(x_again, 16)
            for tt in range(TT):
                for h in range(2):
                    cs_ = slice(512 * h, 512 * h + 512)
                    b = wait_full(dve, f"wo{tt}{h}")
                    dve.wait_ge(free_of(f"g1r{h}"), AT[f"g1r{h}"][1] + 1)
                    v.tensor_tensor(tmp2, b[:, :], g1row[:, cs_], ALU.mult).then_inc(free_of(f"wo{tt}{h}"), 1)
                    dve.wait_ge(free_of(f"wo{tt}{h}"), AT[f"wo{tt}{h}"][1] + 1)
                    v.tensor_tensor(x1[:, tt, cs_], x1[:, tt, cs_], tmp2, ALU.add).then_inc(x1_ready, 1)
                    dve.wait_ge(x1_ready, 2 * tt + h + 1)
            dve.wait_ge(x1_sq, 3)
            link(v.reciprocal(st[:, 34:36], st[:, 34:36]))
            for tt in range(TT):
                for r in ("a2r1", "b2r1"):
                    dve.wait_ge(free_of(r), AT[r][1] + 1)
                for r in ("a2r0", "b2r0"):
                    dve.wait_ge(free_of(r), AT[r][1] + 1)
                link(v.scalar_tensor_tensor(out=tmp[:, :], in0=x1[:, tt, :], scalar=st[:, 34 + tt:35 + tt],
                                            in1=a2row, op0=ALU.mult, op1=ALU.mult))
                nat = lambda z: z.rearrange("t (p c) -> t p c", c=KC)
                v.tensor_tensor(hp[:, tt, :].rearrange("t (c p) -> t p c", c=KC), nat(tmp[:, :]), nat(b2row),
                                ALU.add).then_inc(h2_ready, 1)
                dve.wait_ge(h2_ready, tt + 1)
            v.memset(pos_all[:, :, :], -1.0)
            link(v.memset(w_all[:, :, :], 0.0))
            dve.wait_ge(r_exp, 1)
            flat_e = lambda z: z.rearrange("p m e -> p (m e)")
            ts(flat_e(s_r), flat_e(s_r), 1.0, ALU.add)
            v.reciprocal(flat_e(s_r), flat_e(s_r)).then_inc(free_of("rt"), 1)
            dve.wait_ge(free_of("rt"), AT["rt"][1] + 1)
            add(b_r, s_r, bias_row[:, :].unsqueeze(1).to_broadcast([128, 2, E]))
            for tt in range(TT):
                link(v.max(top8[:, tt, :], b_r[:, tt, :]))
                link(v.max_index(idx8[:, tt, :], top8[:, tt, :], b_r[:, tt, :]))
            link(v.tensor_copy(idxf[:, :, :], idx8[:, :, :]))
            for tt in range(TT):
                link(v.tensor_tensor(onehot[:, tt, :, :], iota_e[:, :].unsqueeze(2).to_broadcast([128, E, TOP]),
                                     idxf[:, tt, 0:TOP].unsqueeze(1).to_broadcast([128, E, TOP]), ALU.is_equal))
            v.tensor_reduce(flat_e(m_r), tmp[:, 0:768].rearrange("p (e k) -> p e k", k=TOP), AX.X,
                            ALU.add).then_inc(mask_ready, 1)
            dve.wait_ge(mask_ready, 1)
            mul(w_r, s_r, m_r)
            link(v.tensor_reduce(st[:, 36:38], w_r, AX.X, ALU.add))
            link(v.reciprocal(st[:, 36:38], st[:, 36:38]))
            for tt in range(TT):
                ts(w_r[:, tt, :], w_r[:, tt, :], st[:, 36 + tt:37 + tt], ALU.mult, ROUTED_SCALE, ALU.mult)
            for rd in range(MAX_ROUNDS):
                link(v.tensor_copy(w_all[:, :, E * rd:E * rd + E], w_r))
            b = wait_full(dve, "ps")
            p2 = lambda z: z.rearrange("p (m e) -> p m e", m=2)
            link(v.scalar_tensor_tensor(out=b_r, in0=p2(b[:, 0:128]), scalar=1.0, in1=m_r, op0=ALU.add, op1=ALU.mult))
            for rd in range(MAX_ROUNDS):
                link(v.tensor_scalar(pos_all[:, :, E * rd:E * rd + E], b_r, -1.0 - SLOTS * rd, None, ALU.add))
            v.tensor_reduce(st[:, 38:39], b[:, 128:192], AX.X, ALU.max).then_inc(free_of("ps"), 1)
            dve.wait_ge(free_of("ps"), AT["ps"][1] + 1)
            ts(st[:, 39:40], st[:, 38:39], float(SLOTS), ALU.is_gt, 1.0, ALU.add)
            for rd in range(2, MAX_ROUNDS):
                link(v.scalar_tensor_tensor(out=st[:, 39:40], in0=st[:, 38:39], scalar=float(SLOTS * rd),
                                            in1=st[:, 39:40], op0=ALU.is_gt, op1=ALU.add))
            v.tensor_copy(rounds_i[:, :], st[:, 39:40]).then_inc(rounds_ready, 1)
            dve.wait_ge(rounds_ready, 1)

            def select_pair(pair, buf):
                four = lambda z, e0: z[:, :, bass.ds(e0, 2)].unsqueeze(3).to_broadcast([128, 2, 2, SLOTS])
                sl = sel[buf].rearrange("p m (x s) -> p m x s", x=2)
                sw_ = selw[buf].rearrange("p m (x s) -> p m x s", x=2)
                for tt in range(TT):
                    io = iota_e[:, 0:SLOTS].unsqueeze(1).to_broadcast([128, 2, SLOTS])
                    ins = v.tensor_tensor(sl[:, tt, :, :], io, four(pos_all, pair * 2)[:, tt, :, :], ALU.is_equal)
                    ins.then_inc(sel_ready, 1)
                return sl, sw_, four

            def weigh_pair(pair, buf, count):
                sl, sw_, four = select_pair(pair, buf)
                dve.wait_ge(sel_ready, count)
                for tt in range(TT):
                    v.tensor_tensor(sw_[:, tt, :, :], sl[:, tt, :, :], four(w_all, pair * 2)[:, tt, :, :],
                                    ALU.mult).then_inc(sel_ready, 1)

            weigh_pair(0, 0, 2)
            for tt in range(TT):
                dve.wait_ge(part_a, tt + 1)
                dve.wait_ge(free_of("hT3"), AT["hT3"][1] + 1)
                sub(hp[:, tt, :], hp[:, tt, :], parts[0][:, tt, :])
                link(v.tensor_copy(parts[1][:, tt, :], hp[:, tt, :]))
                sub(hp[:, tt, :], hp[:, tt, :], parts[1][:, tt, :])
                v.tensor_copy(parts[2][:, tt, :], hp[:, tt, :]).then_inc(part_ready, 1)
            b = wait_full(dve, "sh1")
            dve.wait_ge(free_of("sh0"), AT["sh0"][1] + 1)
            v.tensor_tensor(hidS.rearrange("p c t -> p (c t)"), silS.rearrange("p c t -> p (c t)"), b[:, :],
                            ALU.mult).then_inc(free_of("sh1"), 1)
            n_rounds = dve.value_load(rounds_i[0:1, 0:1], min_val=1, max_val=MAX_ROUNDS)
            with dve.Fori(0, n_rounds * (E // 4)) as i:
                for k in range(2):
                    p = i * 2 + k
                    dve.wait_ge(g_done, 2 * p + 2)
                    dve.wait_ge(swt_done, p + 1)
                    weigh_pair(p + 1, 1 - k, 4 * p + 6)
                    dve.wait_ge(swt_done, p + 2)
                    v.tensor_copy(swt, ps[4][:, 0:256]).then_inc(swt_full, 1)
                    for x, bank in enumerate((6, 5)):
                        dve.wait_ge(silu_done, 2 * p + x + 1)
                        v.tensor_tensor(hid[:, x, :, :].rearrange("p j s -> p (j s)"),
                                        sil[:, x, :, :].rearrange("p j s -> p (j s)"), ps[bank][:, 128:256],
                                        ALU.mult).then_inc(hid_full, 1)
                    dve.wait_ge(y_done, 2 * p + 2)
                    v.tensor_copy(ysb[:, 512:1024], ps[6][:, :]).then_inc(y1_full, 1)
            dve.wait_ge(acc_done, n_rounds * (E // 2))
            for q in range(4):
                tt, h = divmod(q, 2)
                cs_ = slice(512 * h, 512 * h + 512)
                v.tensor_tensor(xs[:, tt, cs_], ps[q][:, :], g2row[:, cs_], ALU.mult).then_inc(route_ready, 1)
                dve.wait_ge(route_ready, q + 1)
                v.tensor_tensor(xs[:, tt, cs_], xs[:, tt, cs_], x1[:, tt, cs_], ALU.add).then_inc(outs_ready, 1)

        @block.tensor
        def _(pe):
            def begin(name):
                b, cnt = AT[name]
                if cnt:
                    pe.wait_ge(bank_free[b], cnt)
                return ps[b]

            def end(name, ins):
                ins.then_inc(bank_full[AT[name][0]], 1)

            def block_of(blk):
                slot, cnt = landed[blk]
                pe.wait_ge(w_full[slot], cnt)
                return ring[slot]

            def view(w, width):
                return w[:, 0:KC * width].rearrange("p (c n) -> p c n", c=KC)

            pe.wait_ge(consts, 1)
            pe.wait_ge(small_in, 16 * 14)
            pe.wait_ge(rows_ready, 1)
            b = begin("vt")
            end("vt", pe.transpose(b[:, 0:R_END], rows[0:R_END, :], ident[0:R_END, 0:R_END]))

            pe.wait_ge(cond_ready, 2)

            def ada_block(name, blk, first):
                w = view(block_of(blk), BLK)
                b = ps[AT[name][0]]
                for j in range(BLK // 128):
                    col = blk[1] * (BLK // 128) + j - first
                    for c in range(KC):
                        ins = pe.matmul(b[:, col:col + 1], w[:, c, 128 * j:128 * j + 128], cond[:, c:c + 1],
                                        start=(c == 0), stop=(c == KC - 1))
                return ins

            begin("adaA")
            for m in ADA_A:
                ins = ada_block("adaA", ("ada", m), 0)
                if m < 2:
                    ins.then_inc(w_free, 1)
            end("adaA", ins)
            for k in range(4):
                b = begin(f"xT{k}")
                pe.wait_ge(xn_ready, 2)
                for c in (2 * k, 2 * k + 1):
                    for tt in range(TT):
                        lo = 256 * (c % 2) + 128 * tt
                        ins = pe.transpose(b[:, lo:lo + 128], xs[:, tt, 128 * c:128 * c + 128], ident[:, :])
                end(f"xT{k}", ins)
            pe.wait_ge(bc_ready, 1)
            for r, g in enumerate(("bT", "cT")):
                b = begin(g)
                for m in range(4):
                    ins = pe.transpose(b[:, 128 * m:128 * m + 128], pools[:, r, m // 2, m % 2, :], ident[:, :])
                end(g, ins)

            for k in range(4):
                pe.wait_ge(free_of(f"xT{k}"), AT[f"xT{k}"][1] + 1)
            pe.wait_ge(hT_ready, 4)

            def cols_of(b, lo, w, j):
                for c in range(KC):
                    ins = pe.matmul(b[:, lo:lo + 256], w[:, c, 128 * j:128 * j + 128], hT[:, c, :],
                                    start=(c == 0), stop=(c == KC - 1))
                return ins

            def tokens_of(b, lo, tt, w, first, width):
                for c in range(KC):
                    ins = pe.matmul(b[:, lo:lo + width], hT[:, c, 128 * tt:128 * tt + 128],
                                    w[:, c, first:first + width], start=(c == 0), stop=(c == KC - 1))
                return ins

            w = view(block_of(("in", 0)), BLK)
            for k, g in enumerate(("pu", "pq", "pf")):
                b = begin(g)
                for m in range(2):
                    ins = cols_of(b, 256 * m, w, 2 * k + m)
                end(g, ins)
            w = view(block_of(("in", 1)), BLK)
            for tt in range(TT):
                b = begin(f"vg{tt}")
                ins = tokens_of(b, 0, tt, w, 0, 512)
                end(f"vg{tt}", ins)
            b = begin("mq")
            for tt in range(TT):
                ins = tokens_of(b, 256 * tt, tt, w, 512, 256)
            end("mq", ins)
            w = view(block_of(("in", 2)), 512)
            for tt in range(TT):
                b = begin(f"kv{tt}")
                ins = tokens_of(b, 0, tt, w, 0, 512)
                end(f"kv{tt}", ins)

            def gate_tile(k):
                b = begin(f"g{k}")
                for m in range(2):
                    t = 2 * k + m
                    w = view(block_of(("in", 3 + t // 6)), BLK)
                    ins = cols_of(b, 256 * m, w, t % 6)
                end(f"g{k}", ins)

            def bu(i):
                if i == 0:
                    pe.wait_ge(free_of("cT"), AT["cT"][1] + 1)
                    pe.wait_ge(free_of("bT"), AT["bT"][1] + 1)
                    pe.wait_ge(free_of("pu"), AT["pu"][1] + 1)
                b = begin(f"bu{i}")
                q, r = divmod(i, 4)
                for m in range(2):
                    ins = pe.matmul(b[:, 256 * m:256 * m + 256], bt[32 * r:32 * r + 32, 2 * m + q, :],
                                    uT[32 * r:32 * r + 32, q, :], start=True, stop=True, tile_position=(32 * r, 0))
                end(f"bu{i}", ins)

            def s5_out(i):
                q, r = divmod(i, 4)
                pe.wait_ge(s5_state, 2 * i + 1)
                b = ps[AT["sy"][0]]
                for m in range(2):
                    ins = pe.matmul(b[32 * r:32 * r + 32, 256 * q:256 * q + 256], ct[:, 2 * m + q, 32 * r:32 * r + 32],
                                    s5tmp[:, 4, 256 * m:256 * m + 256], start=(m == 0), stop=(m == 1))
                if i < 7:
                    ins.then_inc(s5_state, 1)
                else:
                    end("sy", ins)

            def turn_qk(src, g):
                pe.wait_ge(qknorm_ready, 2)
                b = begin(g)
                for c in range(2):
                    for tt in range(TT):
                        ins = pe.transpose(b[:, 256 * c + 128 * tt:256 * c + 128 * tt + 128],
                                           src[:, tt, 128 * c:128 * c + 128], ident[:, :])
                end(g, ins)

            def scores(h):
                if h == 0:
                    for g in ("qT", "kT"):
                        pe.wait_ge(free_of(g), AT[g][1] + 1)
                b = begin(f"sc{h}")
                pr, c = slice(64 * (h % 2), 64 * (h % 2) + 64), h // 2
                pe.matmul(b[:, 0:128], qn[pr, c, 0:128], kn[pr, c, 0:128], start=True, stop=True)
                ins = pe.matmul(b[:, 128:384], qn[pr, c, 128:256], kn[pr, c, 0:256], start=True, stop=True)
                end(f"sc{h}", ins)

            def turn_probs(h):
                pe.wait_ge(prob_ready, 2 * h + 2)
                b = begin(f"pT{h}")
                for m in range(3):
                    ins = pe.transpose(b[:, 128 * m:128 * m + 128], prob[:, h % 2, 128 * m:128 * m + 128], ident[:, :])
                end(f"pT{h}", ins)

            def attend():
                b = begin("mo")
                for h in range(HEADS):
                    pe.wait_ge(free_of(f"pT{h}"), AT[f"pT{h}"][1] + 1)
                for g in ("kv0", "kv1"):
                    pe.wait_ge(free_of(g), AT[g][1] + 1)
                for h in range(HEADS):
                    po, c = slice(64 * (h % 2), 64 * (h % 2) + 64), 256 * (h // 2)
                    hd = slice(HD * h, HD * h + HD)
                    pe.matmul(b[po, c:c + 128], mv[:, 0, hd], probT[:, h, 0:128], start=True, stop=True)
                    pe.matmul(b[po, c + 128:c + 256], mv[:, 0, hd], probT[:, h, 128:256], start=True, stop=False)
                    ins = pe.matmul(b[po, c + 128:c + 256], mv[:, 1, hd], probT[:, h, 256:384], start=False, stop=True)
                end("mo", ins)

            def level(k):
                lv = 0 if k == 0 else LEVELS[k - 1]
                q_, k_ = (qT, key) if k == 0 else (qe, ke)
                if k == 0:
                    pe.wait_ge(f_ready, 1)
                    pe.wait_ge(free_of("pq"), AT["pq"][1] + 1)
                else:
                    pe.wait_ge(lv_ready, 2 * k)
                for odd, g in enumerate("ab"):
                    b = begin(f"L{lv}{g}")
                    pr = slice(64 * odd, 64 * odd + 64)
                    pairs = [(c, tt, tt) for c in range(2) for tt in range(TT)] if lv < 128 else [(0, 0, 1), (1, 0, 1)]
                    for m, (c, ks, qs) in enumerate(pairs):
                        ins = pe.matmul(b[:, 128 * m:128 * m + 128], k_[pr, c, 128 * ks:128 * ks + 128],
                                        q_[pr, c, 128 * qs:128 * qs + 128], start=True, stop=True)
                    end(f"L{lv}{g}", ins)

            for i in range(8):
                bu(i)
                if i == 1:
                    begin("sy")
                if i >= 1:
                    s5_out(i - 1)
                if i < 6:
                    gate_tile(i)
            turn_qk(mq, "qT")
            turn_qk(mk, "kT")
            gate_tile(6)
            scores(0)
            scores(1)
            s5_out(7)
            gate_tile(7)
            scores(2)
            scores(3)
            gate_tile(8)
            turn_probs(0)
            turn_probs(1)
            gate_tile(9)
            turn_probs(2)
            turn_probs(3)
            attend()
            gate_tile(10)
            level(0)
            gate_tile(11)
            for k in range(1, len(LEVELS)):
                level(k)
            level(len(LEVELS))
            begin("adaB")
            for m in range(3, 8):
                ins = ada_block("adaB", ("ada", m), 18)
                if m < 7:
                    ins.then_inc(w_free, 1)
            end("adaB", ins)
            pe.wait_ge(score_ready, 1)
            pe.wait_ge(free_of("L128b"), AT["L128b"][1] + 1)
            pe.wait_ge(vals_ready, 2)
            b = begin("ho")
            for h in range(HEADS):
                hd = slice(HD * h, HD * h + HD)
                o0, o1 = b[:, HD * h:HD * h + HD], b[:, 256 + HD * h:256 + HD * h + HD]
                n0, nx = 4 * (h % 2) + 2 * (h // 2), 2 * (h % 2) + h // 2
                pe.matmul(o0, score_h[:, n0, :], hi[:, 0, hd], start=True, stop=True)
                pe.matmul(o1, score_x[:, nx, :], hi[:, 0, hd], start=True, stop=False)
                ins = pe.matmul(o1, score_h[:, n0 + 1, :], hi[:, 1, hd], start=False, stop=True)
            end("ho", ins)
            pe.wait_ge(o_ready, 1)
            b = begin("hoT")
            for c in range(2):
                for tt in range(TT):
                    ins = pe.transpose(b[:, 256 * c + 128 * tt:256 * c + 128 * tt + 128],
                                       tmp[:, 256 * tt + 128 * c:256 * tt + 128 * c + 128], ident[:, :])
            end("hoT", ins)
            glu = block_of(("glu", 0))[:, 0:4096].rearrange("p (c n) -> p c n", c=2)
            wo = block_of(("wo", 0))
            who = wo[:, 0:2048].rearrange("p (c n) -> p c n", c=2)
            wmo = wo[:, 2048:4096].rearrange("p (c n) -> p c n", c=2)
            pe.wait_ge(s5_ready, 1)
            pe.wait_ge(free_of("hoT"), AT["hoT"][1] + 1)
            pe.wait_ge(free_of("mo"), AT["mo"][1] + 1)
            for j in range(KC):
                for g, pair in ((f"za{j}", ((glu, j, uT), (glu, 8 + j, uT))), (f"yb{j}", ((who, j, ogT), (wmo, j, mo)))):
                    b = begin(g)
                    for m, (w, jj, x) in enumerate(pair):
                        for c in range(2):
                            ins = pe.matmul(b[:, 256 * m:256 * m + 256], w[:, c, 128 * jj:128 * jj + 128], x[:, c, :],
                                            start=(c == 0), stop=(c == 1))
                    end(g, ins)

            def rows_from(r, k):
                for h in range(2):
                    b = begin(f"{r}{h}")
                    for c in range(4):
                        pe.wait_ge(diag_ready, 8 * k + 4 * h + c + 1)
                        ins = pe.matmul(b[:, 128 * c:128 * c + 128], ones[:, :], diag[:, 4 * h + c, :],
                                        start=True, stop=True)
                    end(f"{r}{h}", ins)

            rows_from("g1r", 0)
            rows_from("a2r", 1)
            rows_from("b2r", 2)
            pe.wait_ge(merged_ready, KC)
            for tt in range(TT):
                for h in range(2):
                    w = block_of(("out", h))[:, 0:4096].rearrange("p (c n) -> p c n", c=KC)
                    b = begin(f"wo{tt}{h}")
                    for c in range(KC):
                        ins = pe.matmul(b[:, :], merged[:, c, 128 * tt:128 * tt + 128], w[:, c, :],
                                        start=(c == 0), stop=(c == KC - 1))
                    end(f"wo{tt}{h}", ins)
            rows_from("g2r", 3)
            for k in range(4):
                b = begin(f"hT{k}")
                pe.wait_ge(h2_ready, 2)
                for c in (2 * k, 2 * k + 1):
                    for tt in range(TT):
                        lo = 256 * (c % 2) + 128 * tt
                        ins = pe.transpose(b[:, lo:lo + 128], hp[:, tt, 128 * c:128 * c + 128], ident[:, :])
                end(f"hT{k}", ins)
            pe.wait_ge(router_in, 16)
            for k in range(4):
                pe.wait_ge(free_of(f"hT{k}"), AT[f"hT{k}"][1] + 1)
            b = begin("rt")
            for tt in range(TT):
                for c in range(KC):
                    ins = pe.matmul(b[:, E * tt:E * tt + E], h2T[:, c, 128 * tt:128 * tt + 128], router[:, c, :],
                                    start=(c == 0), stop=(c == KC - 1))
            end("rt", ins)
            w = block_of(("shared", 0))

            def shared_up(g, base):
                b = begin(g)
                for j in range(2):
                    wv = w[:, base:base + 2048].rearrange("p (c n) -> p c n", c=KC)
                    for c in range(KC):
                        ins = pe.matmul(b[:, 256 * j:256 * j + 256], wv[:, c, 128 * j:128 * j + 128], h2T[:, c, :],
                                        start=(c == 0), stop=(c == KC - 1))
                end(g, ins)

            def prefix():
                b = begin("ps")
                pe.wait_ge(mask_ready, 1)
                pe.wait_ge(consts, 5)
                pe.matmul(b[:, 0:E], before[:, :], m_r[:, 0, :], start=True, stop=True)
                pe.matmul(b[:, E:2 * E], ones[:, :], m_r[:, 0, :], start=True, stop=False)
                pe.matmul(b[:, E:2 * E], before[:, :], m_r[:, 1, :], start=False, stop=True)
                pe.matmul(b[:, 2 * E:3 * E], ones[:, :], m_r[:, 0, :], start=True, stop=False)
                end("ps", pe.matmul(b[:, 2 * E:3 * E], ones[:, :], m_r[:, 1, :], start=False, stop=True))

            shared_up("sh0", 0)
            prefix()
            shared_up("sh1", 2048)
            pe.wait_ge(free_of("sh1"), AT["sh1"][1] + 1)
            for q in range(8):
                pe.wait_ge(bank_free[q], LAST_FREE[q])
            sd = w[:, 4096:6144].rearrange("p (c n) -> p c n", c=2)
            for q in range(4):
                tt, h = divmod(q, 2)
                for j in range(2):
                    ins = pe.matmul(ps[q][:, :], hidS[:, j, 128 * tt:128 * tt + 128], sd[:, j, 512 * h:512 * h + 512],
                                    start=(j == 0), stop=False, skip_group_check=True)
            ins.then_inc(acc_init, 1)

            def gather_half(h, buf):
                for cc in range(4):
                    c = 4 * h + cc
                    for m, (tt, part) in enumerate([(tt, part) for tt in range(TT) for part in range(3)]):
                        ins = pe.matmul(ps[4][:, 128 * cc:128 * cc + 128], parts[part][:, tt, 128 * c:128 * c + 128],
                                        sel[buf][:, tt, :], start=(m == 0), stop=(m == 5))
                ins.then_inc(g_done, 1)

            def gate_up(k, x, buf, bank):
                for m in range(2):
                    wv = ring[2 * k + x][:, 2048 * m:2048 * m + 2048].rearrange("p (c n) -> p c n", c=KC)
                    for j in range(2):
                        lo = 128 * m + SLOTS * j
                        for c in range(KC):
                            ins = pe.matmul(ps[bank][:, lo:lo + SLOTS], wv[:, c, 128 * j:128 * j + 128],
                                            xe[buf][:, c, SLOTS * x:SLOTS * x + SLOTS],
                                            start=(c == 0), stop=(c == KC - 1))
                        if m == 1 and j == 1:
                            ins.then_inc(gu_done, 1)

            def down_half(k, h, bank):
                for x in range(2):
                    wv = ring[2 * k + x][:, 4096:6144].rearrange("p (c n) -> p c n", c=2)
                    for j in range(2):
                        ins = pe.matmul(ps[bank][64 * x:64 * x + 64, :], hid[:, x, j, :],
                                        wv[:, j, 512 * h:512 * h + 512], start=(j == 0), stop=(j == 1))
                ins.then_inc(y_done, 1)

            def scatter_half(h):
                for tt in range(TT):
                    ins = pe.matmul(ps[2 * tt + h][:, :], swt[:, 128 * tt:128 * tt + 128], ysb[:, 512 * h:512 * h + 512],
                                    start=False, stop=False, skip_group_check=True)
                return ins

            pe.wait_ge(part_ready, 2)
            pe.wait_ge(sel_ready, 4)
            gather_half(0, 0)
            pe.wait_ge(xe_full, 1)
            gather_half(1, 0)
            pe.sem_inc(y0_full, 1)
            pe.sem_inc(y1_full, 1)
            pe.sem_inc(hid_full, 2)
            pe.sem_inc(swt_done, 1)
            pe.wait_ge(rounds_ready, 1)
            n_rounds = pe.value_load(rounds_i[0:1, 0:1], min_val=1, max_val=MAX_ROUNDS)
            with pe.Fori(0, n_rounds * (E // 4)) as i:
                for k in range(2):
                    p = i * 2 + k
                    pe.wait_ge(gu_full[2 * k], 32 * i + 32)
                    pe.wait_ge(y1_full, p + 1)
                    pe.wait_ge(xe_full, 2 * p + 2)
                    gate_up(k, 0, k, 6)
                    pe.wait_ge(sel_ready, 4 * p + 4)
                    for tt in range(TT):
                        ins = pe.transpose(ps[4][:, 128 * tt:128 * tt + 128], selw[k][:, tt, :], ident[:, :])
                    ins.then_inc(swt_done, 1)
                    pe.wait_ge(gu_full[2 * k + 1], 32 * i + 32)
                    pe.wait_ge(hid_full, 2 * p + 2)
                    gate_up(k, 1, k, 5)
                    pe.wait_ge(sel_ready, 4 * p + 6)
                    pe.wait_ge(swt_full, p + 1)
                    gather_half(0, 1 - k)
                    pe.wait_ge(dn_full[2 * k], 16 * i + 16)
                    pe.wait_ge(dn_full[2 * k + 1], 16 * i + 16)
                    pe.wait_ge(y0_full, p + 1)
                    pe.wait_ge(hid_full, 2 * p + 4)
                    down_half(k, 0, 7)
                    down_half(k, 1, 6)
                    pe.wait_ge(xe_full, 2 * p + 3)
                    gather_half(1, 1 - k)
                    pe.wait_ge(y0_full, p + 2)
                    scatter_half(0)
                    pe.wait_ge(y1_full, p + 2)
                    scatter_half(1).then_inc(acc_done, 1)


LAST_GROUP = {("ada", 2): "adaA", ("in", 0): "pf", ("in", 1): "mq", ("in", 2): "kv1", ("ada", 7): "adaB",
              ("glu", 0): "yb7", ("wo", 0): "yb7", ("out", 0): "wo11", ("out", 1): "wo11"}
LAST_GROUP.update({("in", 3 + _n): f"g{3 * _n + 2}" for _n in range(4)})

LAST_FREE = [0] * 8
for _name, (_b, _n) in AT.items():
    LAST_FREE[_b] = max(LAST_FREE[_b], _n + 1)

_INS = ["x", "c", "ada_w", "ada_b", "norm1_g", "w_in", "ssm_log_dt", "ssm_lambda_re", "ssm_lambda_im",
        "ssm_b_re", "ssm_b_im", "ssm_c_re", "ssm_c_im", "ssm_d", "ssm_w_glu", "hgrn_lb_logits",
        "hgrn_norm_g", "hgrn_w_o", "moba_q_norm_g", "moba_k_norm_g", "moba_w_o", "w_out", "norm2_g",
        "router_w", "router_bias", "exp_w_gate", "exp_w_up", "exp_w_down", "shared_w_gate",
        "shared_w_up", "shared_w_down"]


def kernel(**inputs):
    import numpy as _np
    import concourse.bacc as _bacc
    from concourse.bass_utils import run_bass_kernel_spmd as _run

    nc = _bacc.Bacc("TRN2", target_bir_lowering=False, num_devices=1)
    arrays, aps = {}, {}
    for name in _INS:
        v = _np.ascontiguousarray(inputs[name])
        arrays[f"in_{name}"] = v
        aps[name] = nc.dram_tensor(f"in_{name}", v.shape, mybir.dt.from_np(v.dtype), kind="ExternalInput").ap()
    out = nc.dram_tensor("out_0", (1, T, D), F32, kind="ExternalOutput").ap()
    build(nc, aps, out)
    r = _run(nc, [arrays], core_ids=[0])
    return r.results[0]["out_0"]
```

```python
import math
from contextlib import ExitStack

import concourse.bass as bass
from concourse import mybir

F32 = mybir.dt.float32
BF16 = mybir.dt.bfloat16
I32 = mybir.dt.int32
U8 = mybir.dt.uint8
U32 = mybir.dt.uint32
ALU = mybir.AluOpType
ACT = mybir.ActivationFunctionType
AX = mybir.AxisListType

D = 1024
T = 256
PT = 128
TT = T // PT
KC = D // 128
HEADS = 4
HD = 64
NSTATE_TILES = 8
E = 64
FE = 256
SLOTS = 64
MAX_ROUNDS = T // SLOTS
TOP = 6
WSLOTS = 4
WCOLS = 6144
BLK = WCOLS // KC
EPS = 1e-6
ROUTED_SCALE = 2.5
MAGIC = 12582912.0
TWO_PI = 2 * math.pi
TP1 = 6.28125
TP2 = 0.0019350051879882812
TP3 = TWO_PI - TP1 - TP2
NEG = -1e30

R_C, R_N1, R_N2, R_ADAB = 0, 8, 16, 24
R_D, R_LB, R_QG, R_KG = 72, 74, 76, 77
R_LRE, R_LIM, R_LDT, R_END = 80, 88, 96, 104
SHIFT1, SCALE1, GATE1, SHIFT2, SCALE2, GATE2 = 0, 8, 16, 24, 32, 40

ACOLS = 512
ADA_HEAD = [0, 1, 2, 3]
ADA_TAIL = [8, 9, 6, 7, 4, 5, 10, 11]
ADA = ADA_HEAD + ADA_TAIL
BLOCKS = [("ada", n) for n in ADA_HEAD] + [("in", n) for n in range(3)]
for _n in range(4):
    BLOCKS += [("in", 3 + _n), ("ada", ADA_TAIL[2 * _n]), ("ada", ADA_TAIL[2 * _n + 1])]
BLOCKS += [("glu", 0), ("wo", 0), ("out", 0), ("out", 1), ("shared", 0)]
assert len(BLOCKS) % WSLOTS == 0
ROWS_AFTER = {1: 8, 3: 9, 8: 6, 10: 7, 14: 4, 16: 5, 20: 10, 22: 11}
COLS_AFTER = {t + 1: n for t, n in ROWS_AFTER.items()}

GROUPS = ["vt", "ar0", "ar1", "xT0", "xT1", "ar2", "xT2", "ar3", "adaA", "xT3", "bT", "cT",
          "pu", "pq", "pf", "vg0", "vg1", "mq", "kv0", "kv1"]


def tile_groups(t):
    return ([f"g{t}"] + ([f"ac{COLS_AFTER[t]}"] if t in COLS_AFTER else [])
            + ([f"ar{ROWS_AFTER[t]}"] if t in ROWS_AFTER else []))


LEVELS = [1, 2, 4, 8, 16, 32, 64, 128]
for i in range(8):
    GROUPS += [f"bu{i}"] + tile_groups(i)
    if i == 5:
        GROUPS += ["qT", "kT"]
GROUPS += tile_groups(8) + ["sc0", "sc1"] + tile_groups(9) + ["sc2", "sc3"] + tile_groups(10)
GROUPS += ["pT0", "pT1"] + tile_groups(11) + ["pT2", "pT3", "mo"] + tile_groups(12) + ["L0a", "L0b"]
for k, b in enumerate(LEVELS):
    GROUPS += tile_groups(13 + k) + [f"L{b}a", f"L{b}b"]
GROUPS += tile_groups(21) + tile_groups(22) + ["ho"] + tile_groups(23) + ["g1r0", "g1r1", "hoT"]
for j in range(KC):
    GROUPS += [f"za{j}", f"yb{j}"] + (["g2r0", "g2r1"] if j == 5 else [])
GROUPS += ["wo00", "wo01", "wo10", "wo11"]
GROUPS += [f"hT{i}" for i in range(4)] + ["rt", "sh0", "ps", "sh1"]
ROTATE = 7
AT = {name: (n % ROTATE, n // ROTATE) for n, name in enumerate(GROUPS)}
AT["sy"] = (ROTATE, 0)


def build(nc, a, out):
    ctx = ExitStack()
    with ctx:
        def sb(name, shape, dt=F32):
            return ctx.enter_context(nc.sbuf_tensor(name, shape, dt))

        def sem(name):
            return ctx.enter_context(nc.semaphore(name))

        ring = [sb(f"ring{n}", [128, WCOLS]) for n in range(WSLOTS)]
        ident = sb("ident", [128, 128])
        ones = sb("ones", [128, 128])
        before = sb("before", [128, 128])
        upto = sb("upto", [128, 128])
        causal = sb("causal", [128, 128])
        level_mask = sb("level_mask", [128, 7, 128], U8)
        iota_e = sb("iota_e", [128, E])
        rows = sb("rows", [128, 128])
        log_dt = sb("log_dt", [128, 2])
        eps = sb("eps", [128, 1])
        cols = sb("cols", [128, R_END])
        cond = sb("cond", [128, KC, 32])
        mod = sb("mod", [128, 48])
        a1 = sb("a1", [128, KC])
        a2 = sb("a2", [128, KC])
        perm = sb("perm", [128, 3, KC])
        bias_row = sb("bias_row", [128, E])
        hg_gain = sb("hg_gain", [128, HD])
        st = sb("st", [128, 64])
        sc = sb("sc", [128, 24, NSTATE_TILES])
        r3 = sb("r3", [128, 1536])
        pools = r3[:, 0:1024].rearrange("p (k r q x) -> p k r q x", k=2, r=2, q=2)
        bsrc = r3[:, 1024:1280].rearrange("p (r i h) -> p r i h", r=2, i=NSTATE_TILES)
        csrc = r3[:, 1280:1536].rearrange("p (r m s) -> p r m s", r=2, m=2)
        bt = sb("bt", [128, 4, 128])
        ct = sb("ct", [128, 4, 128])
        par = sb("par", [128, 4])
        par_i = sb("par_i", [128, 2], I32)
        rounds_i = sb("rounds_i", [128, 1], I32)

        xs = sb("xs", [128, TT, D])
        hT = sb("hT", [128, KC, T])
        merged = hT
        act = sb("act", [128, 24 * 256])
        r1 = sb("r1", [128, 24 * 256])
        r2 = sb("r2", [128, 26 * 256])
        gates = r1[:, :].rearrange("p (g t) -> p g t", g=24)

        row_i, col_i, xor_i = [act[:, 128 * n:128 * (n + 1)].bitcast(I32) for n in range(3)]

        def two(n):
            return act[:, 512 * n:512 * (n + 1)].rearrange("p (m t) -> p m t", m=2)

        uT, qT, key, logf, cum64, cumall, hi, hg, mq, mk, mv, keepm = [two(n) for n in range(12)]
        ogT = logf
        arow = [act[:, 1024 + ACOLS * n:1024 + ACOLS * (n + 1)] for n in range(4)]
        flat = lambda v: v.rearrange("p m t -> p (m t)")
        cosT = r2[:, 0:2048].rearrange("p (i t) -> p i t", i=8)
        sinT = r2[:, 2048:4096].rearrange("p (i t) -> p i t", i=8)
        s5tmp = r2[:, 4096:6656].rearrange("p (n t) -> p n t", n=5)
        expo = r2[:, 0:512]
        qe = r2[:, 512:1024].rearrange("p (m t) -> p m t", m=2)
        ke = r2[:, 1024:1536].rearrange("p (m t) -> p m t", m=2)
        score_h = r2[:, 1536:2560].rearrange("p (n t) -> p n t", n=8)
        score_x = r2[:, 2560:3072].rearrange("p (n t) -> p n t", n=4)
        x1 = r2[:, 4096:6144].rearrange("p (m t) -> p m t", m=2)
        prob = act[:, 4096:4864].rearrange("p (h s) -> p h s", h=2)
        probT = r3[:, :].rearrange("p (h s) -> p h s", h=HEADS)
        qn, kn, mo = [xs[:, 0, 512 * n:512 * n + 512].rearrange("p (m t) -> p m t", m=2) if n < 2
                      else xs[:, 1, 0:512].rearrange("p (m t) -> p m t", m=2) for n in range(3)]
        tmp = sb("tmp", [128, 1024])
        tmp2 = xs[:, 1, 512:1024]
        g1row, g2row = act[:, 2048:3072], act[:, 3072:4096]
        diag = r2[:, 0:1024].rearrange("p (c t) -> p c t", c=8)
        hp = xs
        parts = [r1[:, 1024 * n:1024 * (n + 1)].bitcast(BF16).rearrange("p (m t) -> p m t", m=2) for n in range(3)]
        h2T = r1[:, 3072:5120].rearrange("p (c t) -> p c t", c=8)
        hidS = hT[:, 0:2, :]
        silS = hT[:, 2:4, :]
        xe = hT[:, 4:8, :].rearrange("p c t -> p (c t)").rearrange("p (c s) -> p c s", c=8)
        ysb = r1[:, 5120:6144]
        sel = [act[:, 4096 + 128 * n:4224 + 128 * n].bitcast(BF16).rearrange("p (m s) -> p m s", m=2) for n in range(2)]
        selw = [act[:, 4352 + 256 * n:4608 + 256 * n].rearrange("p (m s) -> p m s", m=2) for n in range(2)]
        swt = act[:, 4864:5120]
        hid = act[:, 5120:5376].rearrange("p (j s) -> p j s", j=2)
        sil = act[:, 5376:5632]
        hid_t = act[:, 5632:5888]
        ro = act[:, 0:512]
        router = act[:, 512:1024].rearrange("p (c e) -> p c e", c=KC)
        s_r, b_r, m_r = [ro[:, 128 * n:128 * n + 128].rearrange("p (m e) -> p m e", m=2) for n in range(3)]
        w_r = ro[:, 384:512].rearrange("p (m e) -> p m e", m=2)
        onehot = tmp[:, 0:768].rearrange("p (m e k) -> p m e k", m=2, k=TOP)
        top8 = sb("top8", [128, 2, 8])
        idx8 = sb("idx8", [128, 2, 8], U32)
        idxf = sb("idxf", [128, 2, 8])
        NPOS = MAX_ROUNDS * E + 2
        pos_all, w_all = [r3[:, 2 * NPOS * n:2 * NPOS * (n + 1)].rearrange("p (m e) -> p m e", m=2) for n in range(2)]

        ps = [ctx.enter_context(nc.psum_tensor(f"bank{n}", [128, 512], F32)) for n in range(8)]

        w_full = [sem(f"w_full{n}") for n in range(WSLOTS)]
        w_free = sem("w_free")
        gu_full = [sem(f"gu_full{n}") for n in range(WSLOTS)]
        dn_full = [sem(f"dn_full{n}") for n in range(WSLOTS)]
        bank_full = [sem(f"bank_full{n}") for n in range(8)]
        bank_free = [sem(f"bank_free{n}") for n in range(8)]
        consts = sem("consts")
        small_in = sem("small_in")
        rows_ready = sem("rows_ready")
        x_in = sem("x_in")
        s5_in = sem("s5_in")
        bcast_in = sem("bcast_in")
        router_in = sem("router_in")
        x_again = sem("x_again")
        dve_seq, act_seq, pool_seq = sem("dve_seq"), sem("act_seq"), sem("pool_seq")
        perm_in, arow_ready, cond_zero = sem("perm_in"), sem("arow_ready"), sem("cond_zero")
        cond_ready, rowsq, xn_ready = sem("cond_ready"), sem("rowsq"), sem("xn_ready")
        theta_ready, trig_ready = sem("theta_ready"), sem("trig_ready")
        bc_ready = sem("bc_ready")
        bct_ready = sem("bct_ready")
        hT_ready, u_ready, f_exp, f_ready, logf_ready = (sem(n) for n in
                                                         ("hT_ready", "u_ready", "f_exp", "f_ready", "logf_ready"))
        vals_ready, qknorm_ready, qkT_ready = sem("vals_ready"), sem("qknorm_ready"), sem("qkT_ready")
        s5_state, s5_y, s5_tanh, s5_ready = sem("s5_state"), sem("s5_y"), sem("s5_tanh"), sem("s5_ready")
        sm_max, sm_exp, prob_ready, probT_ready, mo_ready = (sem(n) for n in
                                                             ("sm_max", "sm_exp", "prob_ready", "probT_ready", "mo_ready"))
        lv_arg, lv_exp, lv_ready, score_ready = (sem(n) for n in ("lv_arg", "lv_exp", "lv_ready", "score_ready"))
        o_sq, o_silu, o_ready = (sem(n) for n in ("o_sq", "o_silu", "o_ready"))
        qk_sq = sem("qk_sq")
        gate_ready, zs_ready, merged_ready = sem("gate_ready"), sem("zs_ready"), sem("merged_ready")
        mod_ready, diag_ready, row_ready = sem("mod_ready"), sem("diag_ready"), sem("row_ready")
        x1_ready, x1_sq, h2_ready, part_ready, h2T_ready = (sem(n) for n in
                                                            ("x1_ready", "x1_sq", "h2_ready", "part_ready", "h2T_ready"))
        part_a = sem("part_a")
        r_exp, mask_ready, route_ready, rounds_ready = (sem(n) for n in
                                                        ("r_exp", "mask_ready", "route_ready", "rounds_ready"))
        sh_silu, sh_hid, acc_init = sem("sh_silu"), sem("sh_hid"), sem("acc_init")
        sel_ready, g_done, xe_full, swt_done, swt_full = (sem(n) for n in
                                                          ("sel_ready", "g_done", "xe_full", "swt_done", "swt_full"))
        gu_done, silu_done, hid_made, hid_turned, hid_full, y_done, y0_full, y1_full, acc_done = (
            sem(n) for n in ("gu_done", "silu_done", "hid_made", "hid_turned", "hid_full", "y_done", "y0_full", "y1_full", "acc_done"))
        outs_ready, stored = sem("outs_ready"), sem("stored")

        block = ctx.enter_context(nc.Block())

        n_dma = {"wo": 2, "shared": 3}
        landed, seen = {}, [0] * WSLOTS
        for s, blk in enumerate(BLOCKS):
            seen[s % WSLOTS] += 16 * n_dma.get(blk[0], 1)
            landed[blk] = (s % WSLOTS, seen[s % WSLOTS])

        def wait_full(eng, name):
            b, n = AT[name]
            eng.wait_ge(bank_full[b], n + 1)
            return ps[b]

        def free_of(name):
            return bank_free[AT[name][0]]

        @block.sync
        def _(sp):
            def w_view(w, lo, n):
                return w[:, lo:lo + n].rearrange("(c p) n -> p c n", p=128)

            def used(blk):
                if blk == ("shared", 0):
                    sp.wait_ge(acc_init, 1)
                elif blk in LAST_GROUP:
                    b, cnt = AT[LAST_GROUP[blk]]
                    sp.wait_ge(bank_full[b], cnt + 1)
                else:
                    sp.wait_ge(bank_full[AT[f"ar{blk[1]}"][0]], AT[f"ar{blk[1]}"][1] + 1)

            sp.dma_start(xs[:, :, :], a["x"][0].rearrange("(m p) d -> p m d", p=PT)).then_inc(x_in, 16)
            ada, win, wout = a["ada_w"][0], a["w_in"][0], a["w_out"][0]
            for s, (kind, n) in enumerate(BLOCKS):
                slot = s % WSLOTS
                if s >= WSLOTS:
                    used(BLOCKS[s - WSLOTS])
                if s == 2:
                    sp.wait_ge(small_in, 16 * 14)
                dst = ring[slot]
                if kind in ("ada", "in"):
                    w = ada if kind == "ada" else win
                    width = ACOLS if kind == "ada" or n == 2 else BLK
                    lo = ACOLS * n if kind == "ada" else (BLK * n if n <= 2 else 2048 + BLK * (n - 3))
                    sp.dma_start(dst[:, 0:KC * width].rearrange("p (c n) -> p c n", c=KC),
                                 w_view(w, lo, width)).then_inc(w_full[slot], 16)
                elif kind == "glu":
                    sp.dma_start(dst[:, 0:4096].rearrange("p (c n) -> p c n", c=2),
                                 w_view(a["ssm_w_glu"][0], 0, 2 * D)).then_inc(w_full[slot], 16)
                elif kind == "wo":
                    for k, w in enumerate(("hgrn_w_o", "moba_w_o")):
                        sp.dma_start(dst[:, 2048 * k:2048 * (k + 1)].rearrange("p (c n) -> p c n", c=2),
                                     w_view(a[w][0], 0, D)).then_inc(w_full[slot], 16)
                elif kind == "out":
                    sp.dma_start(dst[:, 0:4096].rearrange("p (c n) -> p c n", c=KC),
                                 w_view(wout, 512 * n, 512)).then_inc(w_full[slot], 16)
                else:
                    for k, w in enumerate(("shared_w_gate", "shared_w_up")):
                        sp.dma_start(dst[:, 2048 * k:2048 * (k + 1)].rearrange("p (c n) -> p c n", c=KC),
                                     a[w][0].rearrange("(p c) n -> p c n", c=KC)).then_inc(w_full[slot], 16)
                    sp.dma_start(dst[:, 4096:6144].rearrange("p (c n) -> p c n", c=2),
                                 w_view(a["shared_w_down"][0], 0, D)).then_inc(w_full[slot], 16)

            gate_w = a["exp_w_gate"][0].rearrange("e (p c) n -> p e (c n)", c=KC)
            up_w = a["exp_w_up"][0].rearrange("e (p c) n -> p e (c n)", c=KC)
            down_w = a["exp_w_down"][0].rearrange("e (c p) n -> p e c n", p=128)

            def load_gate_up(k, e):
                sp.dma_start(ring[k][:, 0:2048].unsqueeze(1), gate_w[:, bass.ds(e, 1), :]).then_inc(gu_full[k], 16)
                sp.dma_start(ring[k][:, 2048:4096].unsqueeze(1), up_w[:, bass.ds(e, 1), :]).then_inc(gu_full[k], 16)

            def load_down(k, e):
                sp.dma_start(ring[k][:, 4096:6144].rearrange("p (e c n) -> p e c n", e=1, c=2),
                             down_w[:, bass.ds(e, 1), :, :]).then_inc(dn_full[k], 16)

            for k in range(WSLOTS):
                used(BLOCKS[len(BLOCKS) - WSLOTS + k])
                load_gate_up(k, k)
                load_down(k, k)

            def load_four(turn, first):
                for k in range(WSLOTS):
                    if k % 2 == 0:
                        sp.wait_ge(gu_done, 2 * turn - 1 + k // 2)
                    load_gate_up(k, first + k)
                    if k % 2 == 0:
                        sp.wait_ge(y_done, 4 * turn - 2 + k)
                    load_down(k, first + k)

            with sp.Fori(1, E // WSLOTS) as i:
                load_four(i, i * WSLOTS)
            sp.wait_ge(rounds_ready, 1)
            n_rounds = sp.value_load(rounds_i[0:1, 0:1], min_val=1, max_val=MAX_ROUNDS)
            with sp.If(n_rounds > 1):
                with sp.Fori(1, n_rounds) as rd:
                    with sp.Fori(0, E // WSLOTS) as i:
                        load_four(rd * (E // WSLOTS) + i, i * WSLOTS)
            for q in range(4):
                tt, h = divmod(q, 2)
                sp.wait_ge(outs_ready, q + 1)
                sp.dma_start(out[0, tt * PT:(tt + 1) * PT, 512 * h:512 * (h + 1)],
                             xs[:, tt, 512 * h:512 * (h + 1)]).then_inc(stored, 16)
            sp.wait_ge(stored, 64)
        @block.gpsimd
        def _(pool):
            n = [0]

            def link(ins):
                n[0] += 1
                ins.then_inc(pool_seq, 1)
                pool.wait_ge(pool_seq, n[0])

            link(pool.memset(ident[:, :], 0.0))
            link(pool.affine_select(out=ident[:, :], in_=ident[:, :], compare_op=ALU.not_equal, fill=1.0, base=0,
                                    pattern=[[-1, 128]], channel_multiplier=1))
            link(pool.memset(eps[:, :], EPS))
            pool.memset(ones[:, :], 1.0).then_inc(consts, 1)
            pool.iota(row_i[:, :], pattern=[[0, 128]], base=0, channel_multiplier=1).then_inc(consts, 1)
            pool.iota(col_i[:, :], pattern=[[1, 128]], base=0, channel_multiplier=0).then_inc(consts, 1)
            pool.iota(iota_e[:, :], pattern=[[1, E]], base=0, channel_multiplier=0,
                      allow_small_or_imprecise_dtypes=True).then_inc(consts, 1)
            link(pool.memset(before[:, :], 1.0))
            pool.affine_select(out=before[:, :], in_=before[:, :], compare_op=ALU.is_gt, fill=0.0, base=0,
                               pattern=[[1, 128]], channel_multiplier=-1).then_inc(consts, 1)
            link(pool.memset(upto[:, :], 1.0))
            pool.affine_select(out=upto[:, :], in_=upto[:, :], compare_op=ALU.is_ge, fill=0.0, base=0,
                               pattern=[[1, 128]], channel_multiplier=-1).then_inc(consts, 1)
            link(pool.memset(causal[:, :], 0.0))
            pool.affine_select(out=causal[:, :], in_=causal[:, :], compare_op=ALU.is_ge, fill=NEG, base=0,
                               pattern=[[-1, 128]], channel_multiplier=1).then_inc(consts, 1)
            for k, src in enumerate((a["ada_b"][0][128 * SCALE2:128 * SCALE2 + D], a["ada_b"][0][128 * SHIFT2:128 * SHIFT2 + D],
                                     a["norm2_g"][0])):
                pool.dma_start(perm[:, k, :], src.rearrange("(p c) -> p c", c=KC)).then_inc(perm_in, 16)
            pool.wait_ge(s5_ready, 1)
            pool.dma_start(x1, a["x"][0].rearrange("(m p) d -> p m d", p=PT)).then_inc(x_again, 16)
            pool.wait_ge(perm_in, 48)
            pool.wait_ge(free_of("ac9"), AT["ac9"][1] + 1)
            for h, g in enumerate(("ac8", "ac9")):
                pool.wait_ge(free_of(g), AT[g][1] + 1)
            link(pool.tensor_tensor(a2[:, :], mod[:, SCALE2:SCALE2 + 8], perm[:, 0, :], ALU.add))
            link(pool.tensor_scalar(out=a2[:, :], in0=a2[:, :], scalar1=1.0, scalar2=None, op0=ALU.add))
            pool.tensor_tensor(a2[:, :], a2[:, :], perm[:, 2, :], ALU.mult).then_inc(mod_ready, 1)
            for src, bias, gs in ((SHIFT2, perm[:, 1, :], ("ac6", "ac7")),
                                  (GATE1, cols[:, R_ADAB + GATE1:R_ADAB + GATE1 + 8], ("ac4", "ac5")),
                                  (GATE2, cols[:, R_ADAB + GATE2:R_ADAB + GATE2 + 8], ("ac10", "ac11"))):
                for g in gs:
                    pool.wait_ge(free_of(g), AT[g][1] + 1)
                pool.tensor_tensor(mod[:, src:src + 8], mod[:, src:src + 8], bias, ALU.add).then_inc(mod_ready, 1)
            for k, lo in enumerate((GATE1, GATE2)):
                if k == 0:
                    pool.wait_ge(mod_ready, 4)
                    pool.wait_ge(score_ready, 1)
                else:
                    pool.wait_ge(bank_full[AT["g1r1"][0]], AT["g1r1"][1] + 1)
                for c in range(KC):
                    pool.tensor_scalar(out=diag[:, c, :], in0=ident[:, :], scalar1=mod[:, lo + c:lo + c + 1],
                                       scalar2=None, op0=ALU.mult).then_inc(diag_ready, 1)
            pool.wait_ge(merged_ready, KC)
            pool.dma_start(router, a["router_w"][0].rearrange("(p c) n -> p c n", c=KC)).then_inc(router_in, 16)

        @block.scalar
        def _(act_e):
            e = nc.scalar
            n = [0]

            def link(ins):
                n[0] += 1
                ins.then_inc(act_seq, 1)
                act_e.wait_ge(act_seq, n[0])

            def vec(name):
                v = a[name][0]
                return v

            def small(lo, cnt, src):
                e.dma_start(rows[lo:lo + cnt, :], src).then_inc(small_in, 16)

            row = lambda v: v.rearrange("(r p) -> r p", p=128)
            small(R_C, 8, row(a["c"][0]))
            small(R_ADAB, 48, row(a["ada_b"][0]))
            small(R_N1, 8, row(a["norm1_g"][0]))
            small(R_N2, 8, row(a["norm2_g"][0]))
            small(R_D, 2, row(a["ssm_d"][0]))
            small(R_LB, 2, row(a["hgrn_lb_logits"][0]))
            for r, nm in ((R_QG, "moba_q_norm_g"), (R_KG, "moba_k_norm_g")):
                for k in range(2):
                    e.dma_start(rows[r:r + 1, 64 * k:64 * k + 64], a[nm][0:1, :]).then_inc(small_in, 16)
            e.dma_start(rows[78:80, :], row(a["ssm_d"][0])).then_inc(small_in, 16)
            small(R_LRE, 8, a["ssm_lambda_re"][0].rearrange("(i g) p -> i (g p)", g=2))
            small(R_LIM, 8, a["ssm_lambda_im"][0].rearrange("(i g) p -> i (g p)", g=2))
            e.dma_start(log_dt[R_LDT:R_LDT + 8, :],
                        a["ssm_log_dt"][0].rearrange("(i g) -> i g", g=2)).then_inc(small_in, 16)
            for k, (bn, cn) in enumerate((("ssm_b_re", "ssm_c_re"), ("ssm_b_im", "ssm_c_im"))):
                e.dma_start(bsrc[:, k, :, :], a[bn][0].rearrange("g p h -> (g p) h").rearrange("(i q) h -> q i h", q=128)
                            ).then_inc(s5_in, 16)
                e.dma_start(csrc[:, k, :, :], a[cn][0].rearrange("g h p -> (g h) p").rearrange("(m q) p -> q m p", q=128)
                            ).then_inc(s5_in, 16)
            e.dma_start(bias_row[:, :], a["router_bias"][0:1, :].to_broadcast([128, E])).then_inc(bcast_in, 16)
            e.dma_start(hg_gain[:, :], a["hgrn_norm_g"][0:1, :].to_broadcast([128, HD])).then_inc(bcast_in, 16)

            act_e.wait_ge(x_in, 16)
            for tt in range(TT):
                if tt:
                    act_e.wait_ge(rowsq, tt)
                e.activation(tmp[:, :], xs[:, tt, :], ACT.Square, accum_out=st[:, tt:tt + 1]).then_inc(rowsq, 1)
            act_e.wait_ge(rowsq, 2)
            act_e.wait_ge(consts, 1)
            e.activation(st[:, 4:6], st[:, 0:2], ACT.Sqrt, bias=eps[:, :], scale=1.0 / D).then_inc(rowsq, 1)
            act_e.wait_ge(cond_ready, 1)
            act_e.wait_ge(cond_zero, 1)
            e.activation(cond[:, :, 0:1], cols[:, R_C:R_C + 8].unsqueeze(2), ACT.Silu).then_inc(cond_ready, 1)
            link(e.activation(sc[:, 0, :], cols[:, R_LDT:R_LDT + 8], ACT.Exp))
            e.activation(st[:, 40:42], cols[:, R_LB:R_LB + 2], ACT.Exp, bias=0.0).then_inc(theta_ready, 1)
            def take_rows(n, dst):
                b = wait_full(act_e, f"ar{n}")
                e.activation(dst, b[:, :], ACT.Copy).then_inc(free_of(f"ar{n}"), 1)

            for n in ADA_HEAD[0:2]:
                take_rows(n, arow[n])
            act_e.wait_ge(theta_ready, 3)
            e.activation(sc[:, 4, :], sc[:, 1, :], ACT.Exp).then_inc(trig_ready, 1)
            e.activation(sc[:, 5, :], sc[:, 2, :], ACT.Sin).then_inc(trig_ready, 1)
            e.activation(sc[:, 6, :], sc[:, 3, :], ACT.Sin).then_inc(trig_ready, 1)
            for n in ADA_HEAD[2:4]:
                take_rows(n, arow[n])
            for g, dst in (("bT", bt), ("cT", ct)):
                b = wait_full(act_e, g)
                e.activation(dst[:, :, :].rearrange("p a b -> p (a b)"), b[:, :], ACT.Copy).then_inc(free_of(g), 1)
            b = wait_full(act_e, "pu")
            e.activation(flat(uT), b[:, :], ACT.Copy).then_inc(free_of("pu"), 1)
            b = wait_full(act_e, "pq")
            e.activation(flat(qT), b[:, :], ACT.Copy).then_inc(free_of("pq"), 1)
            b = wait_full(act_e, "pf")
            e.activation(flat(key), b[:, :], ACT.Exp, scale=-1.0).then_inc(free_of("pf"), 1)
            act_e.wait_ge(f_ready, 1)
            e.activation(flat(logf), flat(cum64), ACT.Ln).then_inc(logf_ready, 1)
            for tt in range(TT):
                b = wait_full(act_e, f"vg{tt}")
                e.activation(hi[:, tt, :], b[:, 0:256], ACT.Copy).then_inc(vals_ready, 1)
                e.activation(hg[:, tt, :], b[:, 256:512], ACT.Copy).then_inc(free_of(f"vg{tt}"), 1)
            b = wait_full(act_e, "mq")
            e.activation(flat(mq), b[:, :], ACT.Copy).then_inc(free_of("mq"), 1)
            for tt in range(TT):
                b = wait_full(act_e, f"kv{tt}")
                e.activation(mk[:, tt, :], b[:, 0:256], ACT.Copy).then_inc(vals_ready, 1)
                e.activation(mv[:, tt, :], b[:, 256:512], ACT.Copy).then_inc(free_of(f"kv{tt}"), 1)
            act_e.wait_ge(free_of("mq"), AT["mq"][1] + 1)
            act_e.wait_ge(vals_ready, 4)
            act_e.wait_ge(rowsq, 2)
            e.activation(tmp[:, 0:512], flat(mq), ACT.Square).then_inc(qk_sq, 1)
            e.activation(tmp[:, 512:1024], flat(mk), ACT.Square).then_inc(qk_sq, 1)
            act_e.wait_ge(qk_sq, 4)
            e.activation(st[:, 48:64], st[:, 48:64], ACT.Sqrt, bias=eps[:, :], scale=1.0 / HD).then_inc(qk_sq, 1)

            def gate_tile(t):
                b = wait_full(act_e, f"g{t}")
                e.activation(gates[:, t, :], b[:, 0:256], ACT.Tanh, scale=0.5).then_inc(free_of(f"g{t}"), 1)
                if t in COLS_AFTER:
                    nn = COLS_AFTER[t]
                    b = wait_full(act_e, f"ac{nn}")
                    if nn in (6, 7, 8, 9):
                        pr, lo = slice(64 * (nn % 2), 64 * (nn % 2) + 64), SHIFT2 if nn < 8 else SCALE2
                        e.activation(mod[pr, lo:lo + 8], b[pr, 0:8], ACT.Copy).then_inc(free_of(f"ac{nn}"), 1)
                    else:
                        e.activation(mod[:, 4 * nn:4 * nn + 4], b[:, 0:4], ACT.Copy).then_inc(free_of(f"ac{nn}"), 1)
                if t in ROWS_AFTER:
                    take_rows(ROWS_AFTER[t], tmp2)

            def softmax(h):
                act_e.wait_ge(sm_max, 2 * h + 2)
                for tt in range(TT):
                    lo, nn = (0, 128) if tt == 0 else (128, 256)
                    e.activation(prob[:, h % 2, lo:lo + nn], prob[:, h % 2, lo:lo + nn], ACT.Exp,
                                 bias=st[:, 8 + 2 * h + tt:9 + 2 * h + tt],
                                 accum_out=st[:, 16 + 2 * h + tt:17 + 2 * h + tt]).then_inc(sm_exp, 1)

            def level_exp(k):
                act_e.wait_ge(lv_arg, 2 * (k + 1))
                e.activation(expo, expo, ACT.Exp).then_inc(lv_exp, 1)

            def turned_qk():
                act_e.wait_ge(qknorm_ready, 3)
                for g, dst, col in (("qT", qn, 2), ("kT", kn, 3)):
                    b = wait_full(act_e, g)
                    e.activation(flat(dst), b[:, :], ACT.Copy, scale=st[:, col:col + 1]).then_inc(free_of(g), 1)

            def turned_probs(h):
                b = wait_full(act_e, f"pT{h}")
                e.activation(probT[:, h, :], b[:, 0:384], ACT.Copy).then_inc(free_of(f"pT{h}"), 1)

            for i in range(8):
                gate_tile(i)
                if i == 5:
                    turned_qk()
            gate_tile(8)
            act_e.wait_ge(s5_y, 1)
            e.activation(s5tmp[:, 2, :], s5tmp[:, 1, :], ACT.Tanh, scale=math.sqrt(2 / math.pi)).then_inc(s5_tanh, 1)
            gate_tile(9)
            softmax(0)
            softmax(1)
            gate_tile(10)
            turned_probs(0)
            turned_probs(1)
            softmax(2)
            gate_tile(11)
            softmax(3)
            turned_probs(2)
            turned_probs(3)
            b = wait_full(act_e, "mo")
            e.activation(flat(mo), b[:, :], ACT.Copy).then_inc(free_of("mo"), 1)
            gate_tile(12)
            for k in range(len(LEVELS)):
                level_exp(k)
                gate_tile(13 + k)
            gate_tile(21)
            gate_tile(22)
            act_e.wait_ge(free_of("vg1"), AT["vg1"][1] + 1)
            e.activation(keepm.rearrange("p m t -> p (m t)"), flat(hg), ACT.Tanh, scale=0.5).then_inc(o_silu, 1)
            b = wait_full(act_e, "ho")
            act_e.wait_ge(qk_sq, 5)
            e.activation(tmp[:, 0:512], b[:, :], ACT.Square).then_inc(o_sq, 1)
            act_e.wait_ge(o_sq, 2)
            e.activation(st[:, 48:56], st[:, 48:56], ACT.Sqrt, bias=eps[:, :], scale=1.0 / HD).then_inc(o_sq, 1)
            gate_tile(23)

            def take_row(r, dst):
                for h in range(2):
                    b = wait_full(act_e, f"{r}{h}")
                    e.activation(dst[:, 512 * h:512 * h + 512], b[:, :], ACT.Copy).then_inc(free_of(f"{r}{h}"), 1)

            take_row("g1r", g1row)
            b = wait_full(act_e, "hoT")
            e.activation(flat(ogT), b[:, :], ACT.Copy).then_inc(free_of("hoT"), 1)
            for j in range(KC):
                b = wait_full(act_e, f"za{j}")
                if j >= 2:
                    act_e.wait_ge(merged_ready, j - 1)
                e.activation(tmp2[:, 256 * (j % 2):256 * (j % 2) + 256], b[:, 256:512], ACT.Tanh,
                             scale=0.5).then_inc(zs_ready, 1)
                if j == 5:
                    take_row("g2r", g2row)
            for tt in range(TT):
                act_e.wait_ge(x1_ready, 2 * (tt + 1))
                if tt:
                    act_e.wait_ge(x1_sq, tt)
                e.activation(tmp[:, :], x1[:, tt, :], ACT.Square, accum_out=st[:, 32 + tt:33 + tt]).then_inc(x1_sq, 1)
            act_e.wait_ge(x1_sq, 2)
            e.activation(st[:, 34:36], st[:, 32:34], ACT.Sqrt, bias=eps[:, :], scale=1.0 / D).then_inc(x1_sq, 1)
            for tt in range(TT):
                act_e.wait_ge(h2_ready, tt + 1)
                e.activation(parts[0][:, tt, :], hp[:, tt, :], ACT.Copy).then_inc(part_a, 1)
            act_e.wait_ge(mod_ready, 4)
            for k in (0, 2):
                b = wait_full(act_e, f"hT{k}")
                for c in (2 * k, 2 * k + 1):
                    lo = 256 * (c % 2)
                    ins = e.activation(h2T[:, c, :], b[:, lo:lo + 256], ACT.Identity,
                                       bias=mod[:, SHIFT2 + c:SHIFT2 + c + 1], scale=a2[:, c:c + 1])
                ins.then_inc(free_of(f"hT{k}"), 1)
            b = wait_full(act_e, "rt")
            e.activation(s_r.rearrange("p m e -> p (m e)"), b[:, 0:128], ACT.Exp, scale=-1.0).then_inc(r_exp, 1)
            b = wait_full(act_e, "sh0")
            e.activation(silS.rearrange("p c t -> p (c t)"), b[:, :], ACT.Silu).then_inc(free_of("sh0"), 1)

            def take_half(pair, h):
                act_e.wait_ge(g_done, 2 * pair + h + 1)
                for cc in range(4):
                    c = 4 * h + cc
                    ins = e.activation(xe[:, c, :], ps[4 + h][:, 128 * cc:128 * cc + 128], ACT.Identity,
                                       bias=mod[:, SHIFT2 + c:SHIFT2 + c + 1], scale=a2[:, c:c + 1])
                ins.then_inc(xe_full, 1)

            take_half(0, 0)
            take_half(0, 1)
            act_e.wait_ge(rounds_ready, 1)
            n_rounds = act_e.value_load(rounds_i[0:1, 0:1], min_val=1, max_val=MAX_ROUNDS)
            with act_e.Fori(0, n_rounds * (E // 2)) as p:
                act_e.wait_ge(gu_done, p + 1)
                act_e.wait_ge(hid_made, p + 1)
                e.activation(sil, ps[5][:, 0:FE], ACT.Silu).then_inc(silu_done, 1)
                take_half(p + 1, 0)
                take_half(p + 1, 1)
                act_e.wait_ge(y_done, 2 * p + 1)
                act_e.wait_ge(acc_done, p + 1)
                e.activation(ysb[:, 0:512], ps[7][:, :], ACT.Copy).then_inc(y0_full, 1)

        @block.vector
        def _(dve):
            v = nc.vector
            n = [0]

            def link(ins):
                n[0] += 1
                ins.then_inc(dve_seq, 1)
                dve.wait_ge(dve_seq, n[0])

            def mul(o, x, y):
                link(v.tensor_tensor(o, x, y, ALU.mult))

            def add(o, x, y):
                link(v.tensor_tensor(o, x, y, ALU.add))

            def sub(o, x, y):
                link(v.tensor_tensor(o, x, y, ALU.subtract))

            def ts(o, x, s1, op0, s2=None, op1=None):
                link(v.tensor_scalar(o, x, s1, s2, op0, op1) if op1 is not None
                     else v.tensor_scalar(o, x, s1, None, op0))

            v.memset(cond[:, :, :], 0.0).then_inc(cond_zero, 1)
            dve.wait_ge(rowsq, 3)
            link(v.reciprocal(st[:, 6:8], st[:, 4:6]))
            for tt in range(TT):
                v.tensor_scalar(xs[:, tt, :], xs[:, tt, :], st[:, 6 + tt:7 + tt], None, ALU.mult).then_inc(xn_ready, 1)
            dve.wait_ge(small_in, 16 * 14)
            v.tensor_copy(rows[R_LDT:R_LDT + 8, :].rearrange("i (g p) -> i g p", g=2),
                          log_dt[R_LDT:R_LDT + 8, :].unsqueeze(2).to_broadcast([8, 2, 64])).then_inc(rows_ready, 1)
            b = wait_full(dve, "vt")
            v.tensor_copy(cols[:, :], b[:, 0:R_END]).then_inc(cond_ready, 1)
            dve.wait_ge(cond_ready, 1)
            v.tensor_copy(par[:, 0:1], cols[:, 0:1]).then_inc(free_of("vt"), 1)
            dve.wait_ge(consts, 7)
            link(v.tensor_tensor(xor_i[:, :], row_i[:, :], col_i[:, :], ALU.bitwise_xor))
            for k, lv in enumerate(LEVELS[:-1]):
                link(v.tensor_scalar(level_mask[:, k, :], xor_i[:, :], float(lv), None, ALU.is_ge))
            link(v.tensor_scalar(par_i[:, 0:1], row_i[:, 0:1], 4, 1, ALU.logical_shift_right, ALU.bitwise_and))
            link(v.tensor_copy(par[:, 1:2], par_i[:, 0:1]))
            ts(par[:, 0:1], par[:, 1:2], -1.0, ALU.mult, 1.0, ALU.add)

            lre, lim = cols[:, R_LRE:R_LRE + 8], cols[:, R_LIM:R_LIM + 8]
            dve.wait_ge(theta_ready, 1)
            mul(sc[:, 1, :], lre, sc[:, 0, :])
            mul(sc[:, 7, :], lim, sc[:, 0, :])
            ts(sc[:, 8, :], sc[:, 7, :], 1.0 / TWO_PI, ALU.mult, MAGIC, ALU.add)
            ts(sc[:, 8, :], sc[:, 8, :], MAGIC, ALU.subtract)
            for part in (TP1, TP2, TP3):
                ts(sc[:, 9, :], sc[:, 8, :], -part, ALU.mult)
                add(sc[:, 7, :], sc[:, 7, :], sc[:, 9, :])
            v.tensor_scalar(sc[:, 2, :], sc[:, 7, :], 3.1415925, -3.1415925, ALU.min, ALU.max).then_inc(theta_ready, 1)
            v.tensor_scalar(sc[:, 3, :], sc[:, 7, :], 0.5, None, ALU.mult).then_inc(theta_ready, 1)
            dve.wait_ge(trig_ready, 3)
            mag, sn, half = sc[:, 4, :], sc[:, 5, :], sc[:, 6, :]
            cs = sc[:, 10, :]
            mul(cs, half, half)
            ts(cs, cs, -2.0, ALU.mult, 1.0, ALU.add)
            ar, ai, den, cr, ci, t0, t1 = (sc[:, k, :] for k in (11, 12, 13, 14, 15, 16, 17))
            mul(ar, mag, cs)
            mul(ai, mag, sn)
            mul(den, lre, lre)
            mul(t0, lim, lim)
            add(den, den, t0)
            link(v.reciprocal(den, den))
            ts(ar, ar, 1.0, ALU.subtract)
            mul(t0, ar, lre)
            mul(t1, ai, lim)
            add(cr, t0, t1)
            mul(cr, cr, den)
            mul(t0, ai, lre)
            mul(t1, ar, lim)
            sub(ci, t0, t1)
            mul(ci, ci, den)
            link(v.memset(r3[:, 0:512], 0.0))
            dve.wait_ge(s5_in, 64)
            bb = r3[:, 0:512].rearrange("p (r i h) -> p r i h", r=2, h=32)
            prod = s5tmp[:, 0, 0:128].rearrange("p (i h) -> p i h", h=16)
            wide = lambda col: col.unsqueeze(2).to_broadcast([128, 8, 16])
            for r, (x, y, op) in enumerate(((cr, ci, ALU.subtract), (ci, cr, ALU.add))):
                mul(prod, bsrc[:, 0, :, :], wide(x))
                other = s5tmp[:, 0, 128:256].rearrange("p (i h) -> p i h", h=16)
                mul(other, bsrc[:, 1, :, :], wide(y))
                for half_ in range(2):
                    pr = slice(64 * half_, 64 * half_ + 64)
                    link(v.tensor_tensor(bb[pr, r, :, 16 * half_:16 * half_ + 16], prod[pr], other[pr], op))
            for r in range(2):
                for half_ in range(2):
                    ins = v.tensor_scalar(pools[:, 1, r, :, 64 * half_:64 * half_ + 64], csrc[:, r, :, :],
                                          par[:, half_:half_ + 1], -1.0 if r else 1.0, ALU.mult, ALU.mult)
                    link(ins)
            v.tensor_copy(par[:, 2:3], par[:, 0:1]).then_inc(bc_ready, 1)
            b = wait_full(dve, "adaA")
            v.tensor_tensor(mod[:, 0:16], b[:, 0:16], cols[:, R_ADAB:R_ADAB + 16], ALU.add).then_inc(free_of("adaA"), 1)
            dve.wait_ge(free_of("adaA"), AT["adaA"][1] + 1)
            ts(a1[:, :], mod[:, SCALE1:SCALE1 + 8], 1.0, ALU.add)
            mul(a1[:, :], a1[:, :], cols[:, R_N1:R_N1 + 8])
            for k in range(4):
                b = wait_full(dve, f"xT{k}")
                for c in (2 * k, 2 * k + 1):
                    ins = v.tensor_scalar(hT[:, c, :], b[:, 256 * (c % 2):256 * (c % 2) + 256], a1[:, c:c + 1],
                                          mod[:, SHIFT1 + c:SHIFT1 + c + 1], ALU.mult, ALU.add)
                    if c % 2:
                        ins.then_inc(free_of(f"xT{k}"), 1)
                    else:
                        ins.then_inc(hT_ready, 1)

            ec, es, t2, t3 = (sc[:, k, :] for k in (18, 19, 20, 21))
            link(v.tensor_copy(ec, cs))
            link(v.tensor_copy(es, sn))
            link(v.memset(cosT[:, :, 0:1], 1.0))
            link(v.memset(sinT[:, :, 0:1], 0.0))
            w = 1
            while w < T:
                ecw, esw = (z.unsqueeze(2).to_broadcast([128, 8, w]) for z in (ec, es))
                ta = s5tmp[:, 0:2, :].rearrange("p a b -> p (a b)")[:, 0:8 * w].rearrange("p (i t) -> p i t", i=8)
                tb = s5tmp[:, 2:4, :].rearrange("p a b -> p (a b)")[:, 0:8 * w].rearrange("p (i t) -> p i t", i=8)
                v.tensor_tensor(ta, cosT[:, :, 0:w], ecw, ALU.mult)
                link(v.tensor_tensor(tb, sinT[:, :, 0:w], esw, ALU.mult))
                sub(cosT[:, :, w:2 * w], ta, tb)
                v.tensor_tensor(ta, cosT[:, :, 0:w], esw, ALU.mult)
                link(v.tensor_tensor(tb, sinT[:, :, 0:w], ecw, ALU.mult))
                add(sinT[:, :, w:2 * w], ta, tb)
                mul(t2, ec, ec)
                mul(t3, es, es)
                mul(es, ec, es)
                sub(ec, t2, t3)
                add(es, es, es)
                w *= 2

            e1 = st[:, 40:42]
            link(v.reciprocal(st[:, 42:44], e1))
            mul(st[:, 42:44], st[:, 42:44], e1)
            sub(st[:, 42:44], st[:, 42:44], st[:, 42:44])
            ts(st[:, 44:46], st[:, 42:44], -1.0, ALU.mult, 1.0, ALU.add)
            dve.wait_ge(free_of("pf"), AT["pf"][1] + 1)
            ts(flat(key), flat(key), 1.0, ALU.add)
            link(v.reciprocal(flat(key), flat(key)))
            for m in range(2):
                ts(cum64[:, m, :], key[:, m, :], st[:, 44 + m:45 + m], ALU.mult, st[:, 42 + m:43 + m], ALU.add)
            v.tensor_scalar(flat(key), flat(cum64), -1.0, 1.0, ALU.mult, ALU.add).then_inc(f_ready, 1)
            link(v.memset(flat(keepm), 1.0))
            for c in range(0, 512, 64):
                link(v.memset(flat(keepm)[:, c:c + 1], 0.0))
            dve.wait_ge(logf_ready, 1)
            link(v.tensor_tensor_scan(flat(cum64), flat(keepm), flat(logf), 0.0, ALU.mult, ALU.add))
            link(v.memset(keepm[:, :, 64:256:64], 1.0))
            link(v.tensor_tensor_scan(flat(cumall), flat(keepm), flat(logf), 0.0, ALU.mult, ALU.add))
            dve.wait_ge(qk_sq, 2)
            for k in range(2):
                v.tensor_reduce(st[:, 48 + 8 * k:56 + 8 * k],
                                tmp[:, 512 * k:512 * k + 512].rearrange("p (h d) -> p h d", d=HD), AX.X,
                                ALU.add).then_inc(qk_sq, 1)
            dve.wait_ge(qk_sq, 5)
            link(v.reciprocal(st[:, 48:64], st[:, 48:64]))
            for k, src in enumerate((mq, mk)):
                r8 = st[:, 48 + 8 * k:56 + 8 * k]
                v4 = flat(src).rearrange("p (h d) -> p h d", d=HD)
                v.tensor_tensor(v4, v4, r8.unsqueeze(2).to_broadcast([128, 8, HD]), ALU.mult).then_inc(qknorm_ready, 1)
            ts(st[:, 2:3], cols[:, R_QG:R_QG + 1], HD ** -0.5, ALU.mult)
            v.tensor_copy(st[:, 3:4], cols[:, R_KG:R_KG + 1]).then_inc(qknorm_ready, 1)

            A, B, W, Z, S = (s5tmp[:, k, :] for k in range(5))
            W2, Z2, S2 = W, Z, S
            for i in range(NSTATE_TILES):
                b = wait_full(dve, f"bu{i}")
                cw = cosT[:, i, :].unsqueeze(1).to_broadcast([128, 2, 256])
                sw = sinT[:, i, :].unsqueeze(1).to_broadcast([128, 2, 256])
                three = lambda z: z.rearrange("p (r t) -> p r t", r=2)
                v.tensor_tensor(three(A), three(b[:, :]), cw, ALU.mult)
                v.tensor_tensor(three(B), three(b[:, :]), sw, ALU.mult).then_inc(free_of(f"bu{i}"), 1)
                dve.wait_ge(free_of(f"bu{i}"), AT[f"bu{i}"][1] + 1)
                v.tensor_tensor(W2[:, 0:256], A[:, 0:256], B[:, 256:512], ALU.add)
                link(v.tensor_tensor(W2[:, 256:512], A[:, 256:512], B[:, 0:256], ALU.subtract))
                for r in range(2):
                    ins = v.tensor_tensor_scan(Z2[:, 256 * r:256 * r + 256], mag[:, i:i + 1].to_broadcast([128, 256]),
                                               W2[:, 256 * r:256 * r + 256], 0.0, ALU.mult, ALU.add)
                link(ins)
                v.tensor_tensor(three(A), three(Z2), cw, ALU.mult)
                link(v.tensor_tensor(three(B), three(Z2), sw, ALU.mult))
                if i:
                    dve.wait_ge(s5_state, 2 * i)
                v.tensor_tensor(S2[:, 0:256], A[:, 0:256], B[:, 256:512], ALU.subtract)
                v.tensor_tensor(S2[:, 256:512], A[:, 256:512], B[:, 0:256], ALU.add).then_inc(s5_state, 1)
                dve.wait_ge(s5_state, 2 * i + 1)
            b = wait_full(dve, "sy")
            for m in range(2):
                ins = v.scalar_tensor_tensor(out=S[:, 256 * m:256 * m + 256], in0=uT[:, m, :],
                                             scalar=cols[:, R_D + m:R_D + m + 1], in1=b[:, 256 * m:256 * m + 256],
                                             op0=ALU.mult, op1=ALU.add)
            ins.then_inc(free_of("sy"), 1)
            dve.wait_ge(free_of("sy"), AT["sy"][1] + 1)
            mul(A, S, S)
            ts(A, A, 0.044715, ALU.mult, 1.0, ALU.add)
            v.tensor_tensor(B, A, S, ALU.mult).then_inc(s5_y, 1)
            dve.wait_ge(s5_tanh, 1)
            link(v.scalar_tensor_tensor(out=B, in0=W, scalar=1.0, in1=S, op0=ALU.add, op1=ALU.mult))
            v.tensor_scalar(flat(uT), B, 0.5, None, ALU.mult).then_inc(s5_ready, 1)

            for h in range(HEADS):
                b = wait_full(dve, f"sc{h}")
                if h >= 2:
                    dve.wait_ge(bank_full[AT[f"pT{h - 2}"][0]], AT[f"pT{h - 2}"][1] + 1)
                pr = prob[:, h % 2, :]
                v.tensor_tensor(pr[:, 0:128], b[:, 0:128], causal[:, :], ALU.add)
                v.tensor_copy(pr[:, 128:256], b[:, 128:256])
                ins = v.tensor_tensor(pr[:, 256:384], b[:, 256:384], causal[:, :], ALU.add)
                ins.then_inc(free_of(f"sc{h}"), 1)
                dve.wait_ge(free_of(f"sc{h}"), AT[f"sc{h}"][1] + 1)
                for tt in range(TT):
                    lo, nn = (0, 128) if tt == 0 else (128, 256)
                    v.tensor_reduce(st[:, 8 + 2 * h + tt:9 + 2 * h + tt], pr[:, lo:lo + nn], AX.X, ALU.max,
                                    negate=True).then_inc(sm_max, 1)
                dve.wait_ge(sm_exp, 2 * h + 2)
                link(v.reciprocal(st[:, 24 + 2 * h:26 + 2 * h], st[:, 16 + 2 * h:18 + 2 * h]))
                for tt in range(TT):
                    lo, nn = (0, 128) if tt == 0 else (128, 256)
                    v.tensor_scalar(pr[:, lo:lo + nn], pr[:, lo:lo + nn], st[:, 24 + 2 * h + tt:25 + 2 * h + tt], None,
                                    ALU.mult).then_inc(prob_ready, 1)

            def take_scores(k):
                for half_, g in enumerate("ab"):
                    name = f"L{0 if k == 0 else LEVELS[k - 1]}{g}"
                    b = wait_full(dve, name)
                    dst = score_h[:, 4 * half_:4 * half_ + 4, :]
                    src = b[:, :].rearrange("p (n t) -> p n t", n=4)
                    if k == 0:
                        ins = v.tensor_copy(dst, src)
                    else:
                        ins = v.copy_predicated(dst, level_mask[:, k - 1, :].unsqueeze(1).to_broadcast([128, 4, 128]), src)
                    ins.then_inc(free_of(name), 1)

            for k, lv in enumerate(LEVELS):
                src = cum64 if lv <= 32 else cumall
                cv = flat(src).rearrange("p (n r s) -> p n r s", r=2, s=lv)
                ev = expo.rearrange("p (n r s) -> p n r s", r=2, s=lv)
                ref = cv[:, :, 0, lv - 1:lv].to_broadcast([128, 256 // lv, lv])
                if k:
                    dve.wait_ge(lv_ready, 2 * k)
                v.tensor_tensor(ev[:, :, 0, :], ref, cv[:, :, 0, :], ALU.subtract).then_inc(lv_arg, 1)
                v.tensor_tensor(ev[:, :, 1, :], cv[:, :, 1, :], ref, ALU.subtract).then_inc(lv_arg, 1)
                if k == 0:
                    take_scores(0)
                dve.wait_ge(lv_exp, k + 1)
                if k:
                    g = f"L{LEVELS[k - 1]}b"
                    dve.wait_ge(bank_full[AT[g][0]], AT[g][1] + 1)
                v.tensor_tensor(flat(qe), flat(qT), expo, ALU.mult).then_inc(lv_ready, 1)
                v.tensor_tensor(flat(ke), flat(key), expo, ALU.mult).then_inc(lv_ready, 1)
                if k:
                    g = f"L{LEVELS[k - 2] if k > 1 else 0}b"
                    dve.wait_ge(free_of(g), AT[g][1] + 1)
                    take_scores(k)
            for odd, g in enumerate("ab"):
                b = wait_full(dve, f"L128{g}")
                v.tensor_copy(score_x[:, 2 * odd:2 * odd + 2, :],
                              b[:, 0:256].rearrange("p (n t) -> p n t", n=2)).then_inc(free_of(f"L128{g}"), 1)
            dve.wait_ge(free_of("L64b"), AT["L64b"][1] + 1)
            v.tensor_tensor(score_h, score_h, upto[:, :].unsqueeze(1).to_broadcast([128, 8, 128]),
                            ALU.mult).then_inc(score_ready, 1)
            dve.wait_ge(o_sq, 1)
            r8 = st[:, 48:56]
            v.tensor_reduce(r8, tmp[:, 0:512].rearrange("p (h d) -> p h d", d=HD), AX.X, ALU.add).then_inc(o_sq, 1)
            dve.wait_ge(o_sq, 3)
            link(v.reciprocal(r8, r8))
            b = wait_full(dve, "ho")
            o3 = tmp[:, 0:512].rearrange("p (h d) -> p h d", d=HD)
            v.tensor_tensor(o3, b[:, :].rearrange("p (h d) -> p h d", d=HD),
                            r8.unsqueeze(2).to_broadcast([128, 8, HD]), ALU.mult).then_inc(free_of("ho"), 1)
            dve.wait_ge(free_of("ho"), AT["ho"][1] + 1)
            dve.wait_ge(bcast_in, 32)
            mul(o3, o3, hg_gain[:, :].unsqueeze(1).to_broadcast([128, 8, HD]))
            dve.wait_ge(o_silu, 1)
            km = flat(keepm)
            link(v.scalar_tensor_tensor(out=km, in0=km, scalar=1.0, in1=flat(hg), op0=ALU.add, op1=ALU.mult))
            v.scalar_tensor_tensor(out=tmp[:, 0:512], in0=km, scalar=0.5, in1=tmp[:, 0:512], op0=ALU.mult,
                                   op1=ALU.mult).then_inc(o_ready, 1)

            for t in range(24):
                dve.wait_ge(free_of(f"g{t}"), AT[f"g{t}"][1] + 1)
            for k in range(3):
                g8 = gates[:, 8 * k:8 * k + 8, :].rearrange("p g t -> p (g t)")
                link(v.tensor_scalar(g8, g8, 0.5, 0.5, ALU.mult, ALU.add))
            for j in range(KC):
                if j:
                    dve.wait_ge(merged_ready, j)
                dve.wait_ge(zs_ready, j + 1)
                b = ps[AT[f"za{j}"][0]]
                z = tmp2[:, 256 * (j % 2):256 * (j % 2) + 256]
                link(v.scalar_tensor_tensor(out=z, in0=z, scalar=1.0, in1=b[:, 0:256], op0=ALU.add, op1=ALU.mult))
                v.scalar_tensor_tensor(out=z, in0=z, scalar=0.5, in1=gates[:, j, :], op0=ALU.mult,
                                       op1=ALU.mult).then_inc(free_of(f"za{j}"), 1)
                b = wait_full(dve, f"yb{j}")
                y1, y2 = tmp[:, 512:768], tmp[:, 768:1024]
                v.tensor_tensor(y1, b[:, 0:256], gates[:, 8 + j, :], ALU.mult)
                v.tensor_tensor(y2, b[:, 256:512], gates[:, 16 + j, :], ALU.mult).then_inc(free_of(f"yb{j}"), 1)
                dve.wait_ge(free_of(f"yb{j}"), AT[f"yb{j}"][1] + 1)
                add(y1, y1, y2)
                v.tensor_tensor(merged[:, j, :], y1, z, ALU.add).then_inc(merged_ready, 1)
            dve.wait_ge(x_again, 16)
            for tt in range(TT):
                for h in range(2):
                    cs_ = slice(512 * h, 512 * h + 512)
                    b = wait_full(dve, f"wo{tt}{h}")
                    dve.wait_ge(free_of(f"g1r{h}"), AT[f"g1r{h}"][1] + 1)
                    v.tensor_tensor(tmp2, b[:, :], g1row[:, cs_], ALU.mult).then_inc(free_of(f"wo{tt}{h}"), 1)
                    dve.wait_ge(free_of(f"wo{tt}{h}"), AT[f"wo{tt}{h}"][1] + 1)
                    v.tensor_tensor(x1[:, tt, cs_], x1[:, tt, cs_], tmp2, ALU.add).then_inc(x1_ready, 1)
                    dve.wait_ge(x1_ready, 2 * tt + h + 1)
            dve.wait_ge(x1_sq, 3)
            link(v.reciprocal(st[:, 34:36], st[:, 34:36]))
            for tt in range(TT):
                v.tensor_scalar(hp[:, tt, :].rearrange("t (c p) -> t p c", c=KC),
                                x1[:, tt, :].rearrange("t (p c) -> t p c", c=KC), st[:, 34 + tt:35 + tt], None,
                                ALU.mult).then_inc(h2_ready, 1)
            dve.wait_ge(mod_ready, 4)
            for k in (1, 3):
                b = wait_full(dve, f"hT{k}")
                for c in (2 * k, 2 * k + 1):
                    lo = 256 * (c % 2)
                    ins = v.tensor_scalar(h2T[:, c, :], b[:, lo:lo + 256], a2[:, c:c + 1],
                                          mod[:, SHIFT2 + c:SHIFT2 + c + 1], ALU.mult, ALU.add)
                ins.then_inc(free_of(f"hT{k}"), 1)
            v.memset(pos_all[:, :, :], -1.0)
            link(v.memset(w_all[:, :, :], 0.0))
            dve.wait_ge(r_exp, 1)
            flat_e = lambda z: z.rearrange("p m e -> p (m e)")
            ts(flat_e(s_r), flat_e(s_r), 1.0, ALU.add)
            v.reciprocal(flat_e(s_r), flat_e(s_r)).then_inc(free_of("rt"), 1)
            dve.wait_ge(free_of("rt"), AT["rt"][1] + 1)
            add(b_r, s_r, bias_row[:, :].unsqueeze(1).to_broadcast([128, 2, E]))
            for tt in range(TT):
                link(v.max(top8[:, tt, :], b_r[:, tt, :]))
                link(v.max_index(idx8[:, tt, :], top8[:, tt, :], b_r[:, tt, :]))
            link(v.tensor_copy(idxf[:, :, :], idx8[:, :, :]))
            for tt in range(TT):
                link(v.tensor_tensor(onehot[:, tt, :, :], iota_e[:, :].unsqueeze(2).to_broadcast([128, E, TOP]),
                                     idxf[:, tt, 0:TOP].unsqueeze(1).to_broadcast([128, E, TOP]), ALU.is_equal))
            v.tensor_reduce(flat_e(m_r), tmp[:, 0:768].rearrange("p (e k) -> p e k", k=TOP), AX.X,
                            ALU.add).then_inc(mask_ready, 1)
            dve.wait_ge(mask_ready, 1)
            mul(w_r, s_r, m_r)
            link(v.tensor_reduce(st[:, 36:38], w_r, AX.X, ALU.add))
            link(v.reciprocal(st[:, 36:38], st[:, 36:38]))
            for tt in range(TT):
                ts(w_r[:, tt, :], w_r[:, tt, :], st[:, 36 + tt:37 + tt], ALU.mult, ROUTED_SCALE, ALU.mult)
            for rd in range(MAX_ROUNDS):
                link(v.tensor_copy(w_all[:, :, E * rd:E * rd + E], w_r))
            b = wait_full(dve, "ps")
            p2 = lambda z: z.rearrange("p (m e) -> p m e", m=2)
            link(v.scalar_tensor_tensor(out=b_r, in0=p2(b[:, 0:128]), scalar=1.0, in1=m_r, op0=ALU.add, op1=ALU.mult))
            for rd in range(MAX_ROUNDS):
                link(v.tensor_scalar(pos_all[:, :, E * rd:E * rd + E], b_r, -1.0 - SLOTS * rd, None, ALU.add))
            v.tensor_reduce(st[:, 38:39], b[:, 128:192], AX.X, ALU.max).then_inc(free_of("ps"), 1)
            dve.wait_ge(free_of("ps"), AT["ps"][1] + 1)
            ts(st[:, 39:40], st[:, 38:39], float(SLOTS), ALU.is_gt, 1.0, ALU.add)
            for rd in range(2, MAX_ROUNDS):
                link(v.scalar_tensor_tensor(out=st[:, 39:40], in0=st[:, 38:39], scalar=float(SLOTS * rd),
                                            in1=st[:, 39:40], op0=ALU.is_gt, op1=ALU.add))
            v.tensor_copy(rounds_i[:, :], st[:, 39:40]).then_inc(rounds_ready, 1)
            dve.wait_ge(rounds_ready, 1)

            def select_pair(pair, buf):
                four = lambda z, e0: z[:, :, bass.ds(e0, 2)].unsqueeze(3).to_broadcast([128, 2, 2, SLOTS])
                sl = sel[buf].rearrange("p m (x s) -> p m x s", x=2)
                sw_ = selw[buf].rearrange("p m (x s) -> p m x s", x=2)
                for tt in range(TT):
                    io = iota_e[:, 0:SLOTS].unsqueeze(1).to_broadcast([128, 2, SLOTS])
                    ins = v.tensor_tensor(sl[:, tt, :, :], io, four(pos_all, pair * 2)[:, tt, :, :], ALU.is_equal)
                    ins.then_inc(sel_ready, 1)
                return sl, sw_, four

            def weigh_pair(pair, buf, count):
                sl, sw_, four = select_pair(pair, buf)
                dve.wait_ge(sel_ready, count)
                for tt in range(TT):
                    v.tensor_tensor(sw_[:, tt, :, :], sl[:, tt, :, :], four(w_all, pair * 2)[:, tt, :, :],
                                    ALU.mult).then_inc(sel_ready, 1)

            weigh_pair(0, 0, 2)
            for tt in range(TT):
                dve.wait_ge(part_a, tt + 1)
                dve.wait_ge(free_of("hT3"), AT["hT3"][1] + 1)
                sub(hp[:, tt, :], hp[:, tt, :], parts[0][:, tt, :])
                link(v.tensor_copy(parts[1][:, tt, :], hp[:, tt, :]))
                sub(hp[:, tt, :], hp[:, tt, :], parts[1][:, tt, :])
                v.tensor_copy(parts[2][:, tt, :], hp[:, tt, :]).then_inc(part_ready, 1)
            b = wait_full(dve, "sh1")
            dve.wait_ge(free_of("sh0"), AT["sh0"][1] + 1)
            v.tensor_tensor(hidS.rearrange("p c t -> p (c t)"), silS.rearrange("p c t -> p (c t)"), b[:, :],
                            ALU.mult).then_inc(free_of("sh1"), 1)
            n_rounds = dve.value_load(rounds_i[0:1, 0:1], min_val=1, max_val=MAX_ROUNDS)
            with dve.Fori(0, n_rounds * (E // 4)) as i:
                for k in range(2):
                    p = i * 2 + k
                    dve.wait_ge(g_done, 2 * p + 2)
                    dve.wait_ge(swt_done, p + 1)
                    weigh_pair(p + 1, 1 - k, 4 * p + 6)
                    dve.wait_ge(silu_done, p + 1)
                    dve.wait_ge(hid_turned, p + 1)
                    v.tensor_tensor(hid_t, sil, ps[5][:, FE:2 * FE], ALU.mult).then_inc(hid_made, 1)
                    dve.wait_ge(swt_done, p + 2)
                    v.tensor_copy(swt, ps[7][:, 0:256]).then_inc(swt_full, 1)
                    dve.wait_ge(hid_turned, p + 2)
                    v.tensor_copy(hid.rearrange("p j s -> p (j s)"), ps[6][:, 0:256]).then_inc(hid_full, 1)
                    dve.wait_ge(y_done, 2 * p + 2)
                    v.tensor_copy(ysb[:, 512:1024], ps[6][:, :]).then_inc(y1_full, 1)
            dve.wait_ge(acc_done, n_rounds * (E // 2) + 1)
            for q in range(4):
                tt, h = divmod(q, 2)
                cs_ = slice(512 * h, 512 * h + 512)
                v.tensor_tensor(xs[:, tt, cs_], ps[q][:, :], g2row[:, cs_], ALU.mult).then_inc(route_ready, 1)
                dve.wait_ge(route_ready, q + 1)
                v.tensor_tensor(xs[:, tt, cs_], xs[:, tt, cs_], x1[:, tt, cs_], ALU.add).then_inc(outs_ready, 1)

        @block.tensor
        def _(pe):
            def begin(name):
                b, cnt = AT[name]
                if cnt:
                    pe.wait_ge(bank_free[b], cnt)
                return ps[b]

            def end(name, ins):
                ins.then_inc(bank_full[AT[name][0]], 1)

            def block_of(blk):
                slot, cnt = landed[blk]
                pe.wait_ge(w_full[slot], cnt)
                return ring[slot]

            def view(w, width):
                return w[:, 0:KC * width].rearrange("p (c n) -> p c n", c=KC)

            pe.wait_ge(consts, 1)
            pe.wait_ge(small_in, 16 * 14)
            pe.wait_ge(rows_ready, 1)
            b = begin("vt")
            end("vt", pe.transpose(b[:, 0:R_END], rows[0:R_END, :], ident[0:R_END, 0:R_END]))

            pe.wait_ge(cond_ready, 2)

            def ada_rows(n):
                w = view(block_of(("ada", n)), ACOLS)
                b = begin(f"ar{n}")
                for c in range(KC):
                    q = c % 4
                    ins = pe.matmul(b[32 * q:32 * q + 32, :], cond[:, c, :], w[:, c, :], start=(c < 4), stop=(c >= 4),
                                    skip_group_check=True)
                end(f"ar{n}", ins)

            def ada_cols(n):
                pe.wait_ge(free_of(f"ar{n}"), AT[f"ar{n}"][1] + 1)
                b = begin(f"ac{n}")
                if n in (6, 7, 8, 9):
                    for c in range(KC):
                        ins = pe.matmul(b[64 * (n % 2):64 * (n % 2) + 64, c:c + 1], tmp2[:, c:ACOLS:KC], ones[:, 0:1],
                                        start=True, stop=True)
                else:
                    for c in range(4):
                        ins = pe.matmul(b[:, c:c + 1], tmp2[:, 128 * c:128 * c + 128], ones[:, 0:1],
                                        start=True, stop=True)
                end(f"ac{n}", ins)

            def turn_x(k):
                b = begin(f"xT{k}")
                pe.wait_ge(xn_ready, 2)
                for c in (2 * k, 2 * k + 1):
                    for tt in range(TT):
                        lo = 256 * (c % 2) + 128 * tt
                        ins = pe.transpose(b[:, lo:lo + 128], xs[:, tt, 128 * c:128 * c + 128], ident[:, :])
                end(f"xT{k}", ins)

            ada_rows(0)
            ada_rows(1)
            turn_x(0)
            turn_x(1)
            ada_rows(2)
            turn_x(2)
            ada_rows(3)
            b = begin("adaA")
            for n in ADA_HEAD:
                pe.wait_ge(free_of(f"ar{n}"), AT[f"ar{n}"][1] + 1)
                for c in range(4):
                    ins = pe.matmul(b[:, 4 * n + c:4 * n + c + 1], arow[n][:, 128 * c:128 * c + 128], ones[:, 0:1],
                                    start=True, stop=True)
            end("adaA", ins)
            turn_x(3)
            pe.wait_ge(bc_ready, 1)
            for r, g in enumerate(("bT", "cT")):
                b = begin(g)
                for m in range(4):
                    ins = pe.transpose(b[:, 128 * m:128 * m + 128], pools[:, r, m // 2, m % 2, :], ident[:, :])
                end(g, ins)

            for k in range(4):
                pe.wait_ge(free_of(f"xT{k}"), AT[f"xT{k}"][1] + 1)
            pe.wait_ge(hT_ready, 4)

            def cols_of(b, lo, w, j):
                for c in range(KC):
                    ins = pe.matmul(b[:, lo:lo + 256], w[:, c, 128 * j:128 * j + 128], hT[:, c, :],
                                    start=(c == 0), stop=(c == KC - 1))
                return ins

            def tokens_of(b, lo, tt, w, first, width):
                for c in range(KC):
                    ins = pe.matmul(b[:, lo:lo + width], hT[:, c, 128 * tt:128 * tt + 128],
                                    w[:, c, first:first + width], start=(c == 0), stop=(c == KC - 1))
                return ins

            w = view(block_of(("in", 0)), BLK)
            for k, g in enumerate(("pu", "pq", "pf")):
                b = begin(g)
                for m in range(2):
                    ins = cols_of(b, 256 * m, w, 2 * k + m)
                end(g, ins)
            w = view(block_of(("in", 1)), BLK)
            for tt in range(TT):
                b = begin(f"vg{tt}")
                ins = tokens_of(b, 0, tt, w, 0, 512)
                end(f"vg{tt}", ins)
            b = begin("mq")
            for tt in range(TT):
                ins = tokens_of(b, 256 * tt, tt, w, 512, 256)
            end("mq", ins)
            w = view(block_of(("in", 2)), 512)
            for tt in range(TT):
                b = begin(f"kv{tt}")
                ins = tokens_of(b, 0, tt, w, 0, 512)
                end(f"kv{tt}", ins)

            def gate_tile(t):
                b = begin(f"g{t}")
                w = view(block_of(("in", 3 + t // 6)), BLK)
                end(f"g{t}", cols_of(b, 0, w, t % 6))
                if t in COLS_AFTER:
                    ada_cols(COLS_AFTER[t])
                if t in ROWS_AFTER:
                    ada_rows(ROWS_AFTER[t])

            def bu(i):
                if i == 0:
                    pe.wait_ge(free_of("cT"), AT["cT"][1] + 1)
                    pe.wait_ge(free_of("bT"), AT["bT"][1] + 1)
                    pe.wait_ge(free_of("pu"), AT["pu"][1] + 1)
                b = begin(f"bu{i}")
                q, r = divmod(i, 4)
                for m in range(2):
                    ins = pe.matmul(b[:, 256 * m:256 * m + 256], bt[32 * r:32 * r + 32, 2 * m + q, :],
                                    uT[32 * r:32 * r + 32, q, :], start=True, stop=True, tile_position=(32 * r, 0))
                end(f"bu{i}", ins)

            def s5_out(i):
                q, r = divmod(i, 4)
                pe.wait_ge(s5_state, 2 * i + 1)
                b = ps[AT["sy"][0]]
                for m in range(2):
                    ins = pe.matmul(b[32 * r:32 * r + 32, 256 * q:256 * q + 256], ct[:, 2 * m + q, 32 * r:32 * r + 32],
                                    s5tmp[:, 4, 256 * m:256 * m + 256], start=(m == 0), stop=(m == 1))
                if i < 7:
                    ins.then_inc(s5_state, 1)
                else:
                    end("sy", ins)

            def turn_qk(src, g):
                pe.wait_ge(qknorm_ready, 2)
                b = begin(g)
                for c in range(2):
                    for tt in range(TT):
                        ins = pe.transpose(b[:, 256 * c + 128 * tt:256 * c + 128 * tt + 128],
                                           src[:, tt, 128 * c:128 * c + 128], ident[:, :])
                end(g, ins)

            def scores(h):
                if h == 0:
                    for g in ("qT", "kT"):
                        pe.wait_ge(free_of(g), AT[g][1] + 1)
                b = begin(f"sc{h}")
                pr, c = slice(64 * (h % 2), 64 * (h % 2) + 64), h // 2
                pe.matmul(b[:, 0:128], qn[pr, c, 0:128], kn[pr, c, 0:128], start=True, stop=True)
                ins = pe.matmul(b[:, 128:384], qn[pr, c, 128:256], kn[pr, c, 0:256], start=True, stop=True)
                end(f"sc{h}", ins)

            def turn_probs(h):
                pe.wait_ge(prob_ready, 2 * h + 2)
                b = begin(f"pT{h}")
                for m in range(3):
                    ins = pe.transpose(b[:, 128 * m:128 * m + 128], prob[:, h % 2, 128 * m:128 * m + 128], ident[:, :])
                end(f"pT{h}", ins)

            def attend():
                b = begin("mo")
                for h in range(HEADS):
                    pe.wait_ge(free_of(f"pT{h}"), AT[f"pT{h}"][1] + 1)
                for g in ("kv0", "kv1"):
                    pe.wait_ge(free_of(g), AT[g][1] + 1)
                for h in range(HEADS):
                    po, c = slice(64 * (h % 2), 64 * (h % 2) + 64), 256 * (h // 2)
                    hd = slice(HD * h, HD * h + HD)
                    pe.matmul(b[po, c:c + 128], mv[:, 0, hd], probT[:, h, 0:128], start=True, stop=True)
                    pe.matmul(b[po, c + 128:c + 256], mv[:, 0, hd], probT[:, h, 128:256], start=True, stop=False)
                    ins = pe.matmul(b[po, c + 128:c + 256], mv[:, 1, hd], probT[:, h, 256:384], start=False, stop=True)
                end("mo", ins)

            def level(k):
                lv = 0 if k == 0 else LEVELS[k - 1]
                q_, k_ = (qT, key) if k == 0 else (qe, ke)
                if k == 0:
                    pe.wait_ge(f_ready, 1)
                    pe.wait_ge(free_of("pq"), AT["pq"][1] + 1)
                else:
                    pe.wait_ge(lv_ready, 2 * k)
                for odd, g in enumerate("ab"):
                    b = begin(f"L{lv}{g}")
                    pr = slice(64 * odd, 64 * odd + 64)
                    pairs = [(c, tt, tt) for c in range(2) for tt in range(TT)] if lv < 128 else [(0, 0, 1), (1, 0, 1)]
                    for m, (c, ks, qs) in enumerate(pairs):
                        ins = pe.matmul(b[:, 128 * m:128 * m + 128], k_[pr, c, 128 * ks:128 * ks + 128],
                                        q_[pr, c, 128 * qs:128 * qs + 128], start=True, stop=True)
                    end(f"L{lv}{g}", ins)

            for i in range(8):
                bu(i)
                if i == 1:
                    begin("sy")
                if i >= 1:
                    s5_out(i - 1)
                gate_tile(i)
                if i == 5:
                    turn_qk(mq, "qT")
                    turn_qk(mk, "kT")
            gate_tile(8)
            s5_out(7)
            scores(0)
            scores(1)
            gate_tile(9)
            scores(2)
            scores(3)
            gate_tile(10)
            turn_probs(0)
            turn_probs(1)
            gate_tile(11)
            turn_probs(2)
            turn_probs(3)
            attend()
            gate_tile(12)
            level(0)
            for k in range(len(LEVELS)):
                gate_tile(13 + k)
                level(k + 1)
            gate_tile(21)
            gate_tile(22)
            pe.wait_ge(score_ready, 1)
            pe.wait_ge(free_of("L128b"), AT["L128b"][1] + 1)
            pe.wait_ge(vals_ready, 2)
            b = begin("ho")
            for h in range(HEADS):
                hd = slice(HD * h, HD * h + HD)
                o0, o1 = b[:, HD * h:HD * h + HD], b[:, 256 + HD * h:256 + HD * h + HD]
                n0, nx = 4 * (h % 2) + 2 * (h // 2), 2 * (h % 2) + h // 2
                pe.matmul(o0, score_h[:, n0, :], hi[:, 0, hd], start=True, stop=True)
                pe.matmul(o1, score_x[:, nx, :], hi[:, 0, hd], start=True, stop=False)
                ins = pe.matmul(o1, score_h[:, n0 + 1, :], hi[:, 1, hd], start=False, stop=True)
            end("ho", ins)
            gate_tile(23)

            def rows_from(r, k):
                for h in range(2):
                    b = begin(f"{r}{h}")
                    for c in range(4):
                        pe.wait_ge(diag_ready, 8 * k + 4 * h + c + 1)
                        ins = pe.matmul(b[:, 128 * c:128 * c + 128], ones[:, :], diag[:, 4 * h + c, :],
                                        start=True, stop=True)
                    end(f"{r}{h}", ins)

            rows_from("g1r", 0)
            pe.wait_ge(o_ready, 1)
            b = begin("hoT")
            for c in range(2):
                for tt in range(TT):
                    ins = pe.transpose(b[:, 256 * c + 128 * tt:256 * c + 128 * tt + 128],
                                       tmp[:, 256 * tt + 128 * c:256 * tt + 128 * c + 128], ident[:, :])
            end("hoT", ins)
            glu = block_of(("glu", 0))[:, 0:4096].rearrange("p (c n) -> p c n", c=2)
            wo = block_of(("wo", 0))
            who = wo[:, 0:2048].rearrange("p (c n) -> p c n", c=2)
            wmo = wo[:, 2048:4096].rearrange("p (c n) -> p c n", c=2)
            pe.wait_ge(s5_ready, 1)
            pe.wait_ge(free_of("hoT"), AT["hoT"][1] + 1)
            pe.wait_ge(free_of("mo"), AT["mo"][1] + 1)
            for j in range(KC):
                for g, pair in ((f"za{j}", ((glu, j, uT), (glu, 8 + j, uT))), (f"yb{j}", ((who, j, ogT), (wmo, j, mo)))):
                    b = begin(g)
                    for m, (w, jj, x) in enumerate(pair):
                        for c in range(2):
                            ins = pe.matmul(b[:, 256 * m:256 * m + 256], w[:, c, 128 * jj:128 * jj + 128], x[:, c, :],
                                            start=(c == 0), stop=(c == 1))
                    end(g, ins)
                if j == 5:
                    rows_from("g2r", 1)
            pe.wait_ge(merged_ready, KC)
            for tt in range(TT):
                for h in range(2):
                    w = block_of(("out", h))[:, 0:4096].rearrange("p (c n) -> p c n", c=KC)
                    b = begin(f"wo{tt}{h}")
                    for c in range(KC):
                        ins = pe.matmul(b[:, :], merged[:, c, 128 * tt:128 * tt + 128], w[:, c, :],
                                        start=(c == 0), stop=(c == KC - 1))
                    end(f"wo{tt}{h}", ins)
            for k in range(4):
                b = begin(f"hT{k}")
                pe.wait_ge(h2_ready, 2)
                for c in (2 * k, 2 * k + 1):
                    for tt in range(TT):
                        lo = 256 * (c % 2) + 128 * tt
                        ins = pe.transpose(b[:, lo:lo + 128], hp[:, tt, 128 * c:128 * c + 128], ident[:, :])
                end(f"hT{k}", ins)
            pe.wait_ge(router_in, 16)
            for k in range(4):
                pe.wait_ge(free_of(f"hT{k}"), AT[f"hT{k}"][1] + 1)
            b = begin("rt")
            for tt in range(TT):
                for c in range(KC):
                    ins = pe.matmul(b[:, E * tt:E * tt + E], h2T[:, c, 128 * tt:128 * tt + 128], router[:, c, :],
                                    start=(c == 0), stop=(c == KC - 1))
            end("rt", ins)
            w = block_of(("shared", 0))

            def shared_up(g, base):
                b = begin(g)
                for j in range(2):
                    wv = w[:, base:base + 2048].rearrange("p (c n) -> p c n", c=KC)
                    for c in range(KC):
                        ins = pe.matmul(b[:, 256 * j:256 * j + 256], wv[:, c, 128 * j:128 * j + 128], h2T[:, c, :],
                                        start=(c == 0), stop=(c == KC - 1))
                end(g, ins)

            def prefix():
                b = begin("ps")
                pe.wait_ge(mask_ready, 1)
                pe.wait_ge(consts, 5)
                pe.matmul(b[:, 0:E], before[:, :], m_r[:, 0, :], start=True, stop=True)
                pe.matmul(b[:, E:2 * E], ones[:, :], m_r[:, 0, :], start=True, stop=False)
                pe.matmul(b[:, E:2 * E], before[:, :], m_r[:, 1, :], start=False, stop=True)
                pe.matmul(b[:, 2 * E:3 * E], ones[:, :], m_r[:, 0, :], start=True, stop=False)
                end("ps", pe.matmul(b[:, 2 * E:3 * E], ones[:, :], m_r[:, 1, :], start=False, stop=True))

            shared_up("sh0", 0)
            prefix()
            shared_up("sh1", 2048)
            pe.wait_ge(free_of("sh1"), AT["sh1"][1] + 1)
            for q in range(8):
                pe.wait_ge(bank_free[q], LAST_FREE[q])
            sd = w[:, 4096:6144].rearrange("p (c n) -> p c n", c=2)
            for q in range(4):
                tt, h = divmod(q, 2)
                for j in range(2):
                    ins = pe.matmul(ps[q][:, :], hidS[:, j, 128 * tt:128 * tt + 128], sd[:, j, 512 * h:512 * h + 512],
                                    start=(j == 0), stop=False, skip_group_check=True)
            ins.then_inc(acc_init, 1)

            def gather_half(h, buf):
                for cc in range(4):
                    c = 4 * h + cc
                    for m, (tt, part) in enumerate([(tt, part) for tt in range(TT) for part in range(3)]):
                        ins = pe.matmul(ps[4 + h][:, 128 * cc:128 * cc + 128], parts[part][:, tt, 128 * c:128 * c + 128],
                                        sel[buf][:, tt, :], start=(m == 0), stop=(m == 5))
                ins.then_inc(g_done, 1)

            def gate_up(k):
                for m in range(2):
                    for c in range(KC):
                        for x in range(2):
                            w = ring[2 * k + x][:, 2048 * m + FE * c:2048 * m + FE * c + FE]
                            ins = pe.matmul(ps[5][SLOTS * x:SLOTS * x + SLOTS, FE * m:FE * m + FE],
                                            xe[:, c, SLOTS * x:SLOTS * x + SLOTS], w,
                                            start=(c == 0), stop=(c == KC - 1), skip_group_check=True)
                ins.then_inc(gu_done, 1)

            def down_half(k, h, bank):
                for j in range(2):
                    for x in range(2):
                        w = ring[2 * k + x][:, 4096 + D * j + 512 * h:4096 + D * j + 512 * h + 512]
                        ins = pe.matmul(ps[bank][SLOTS * x:SLOTS * x + SLOTS, :],
                                        hid[:, j, SLOTS * x:SLOTS * x + SLOTS], w,
                                        start=(j == 0), stop=(j == 1), skip_group_check=True)
                ins.then_inc(y_done, 1)

            def scatter_half(h):
                for tt in range(TT):
                    ins = pe.matmul(ps[2 * tt + h][:, :], swt[:, 128 * tt:128 * tt + 128], ysb[:, 512 * h:512 * h + 512],
                                    start=False, stop=False, skip_group_check=True)
                return ins

            pe.wait_ge(part_ready, 2)
            pe.wait_ge(sel_ready, 4)
            gather_half(0, 0)
            pe.wait_ge(xe_full, 1)
            gather_half(1, 0)
            for s in (y0_full, y1_full, hid_made, hid_turned, hid_full, swt_done, acc_done):
                pe.sem_inc(s, 1)
            pe.wait_ge(rounds_ready, 1)
            n_rounds = pe.value_load(rounds_i[0:1, 0:1], min_val=1, max_val=MAX_ROUNDS)
            with pe.Fori(0, n_rounds * (E // 4)) as i:
                for k in range(2):
                    p = i * 2 + k
                    pe.wait_ge(gu_full[2 * k], 32 * i + 32)
                    pe.wait_ge(gu_full[2 * k + 1], 32 * i + 32)
                    pe.wait_ge(xe_full, 2 * p + 2)
                    gate_up(k)
                    pe.wait_ge(sel_ready, 4 * p + 6)
                    gather_half(0, 1 - k)
                    pe.wait_ge(y0_full, p + 1)
                    for tt in range(TT):
                        ins = pe.transpose(ps[7][:, 128 * tt:128 * tt + 128], selw[k][:, tt, :], ident[:, :])
                    ins.then_inc(swt_done, 1)
                    pe.wait_ge(y1_full, p + 1)
                    pe.wait_ge(hid_made, p + 2)
                    for j in range(2):
                        ins = pe.transpose(ps[6][:, 128 * j:128 * j + 128], hid_t[:, 128 * j:128 * j + 128], ident[:, :])
                    ins.then_inc(hid_turned, 1)
                    gather_half(1, 1 - k)
                    pe.wait_ge(dn_full[2 * k], 16 * i + 16)
                    pe.wait_ge(dn_full[2 * k + 1], 16 * i + 16)
                    pe.wait_ge(swt_full, p + 1)
                    pe.wait_ge(hid_full, p + 2)
                    down_half(k, 0, 7)
                    down_half(k, 1, 6)
                    pe.wait_ge(y0_full, p + 2)
                    scatter_half(0)
                    pe.wait_ge(y1_full, p + 2)
                    scatter_half(1).then_inc(acc_done, 1)


LAST_GROUP = {("in", 0): "pf", ("in", 1): "mq", ("in", 2): "kv1",
              ("glu", 0): "yb7", ("wo", 0): "yb7", ("out", 0): "wo11", ("out", 1): "wo11"}
LAST_GROUP.update({("in", 3 + _n): f"g{6 * _n + 5}" for _n in range(4)})

LAST_FREE = [0] * 8
for _name, (_b, _n) in AT.items():
    LAST_FREE[_b] = max(LAST_FREE[_b], _n + 1)

_INS = ["x", "c", "ada_w", "ada_b", "norm1_g", "w_in", "ssm_log_dt", "ssm_lambda_re", "ssm_lambda_im",
        "ssm_b_re", "ssm_b_im", "ssm_c_re", "ssm_c_im", "ssm_d", "ssm_w_glu", "hgrn_lb_logits",
        "hgrn_norm_g", "hgrn_w_o", "moba_q_norm_g", "moba_k_norm_g", "moba_w_o", "w_out", "norm2_g",
        "router_w", "router_bias", "exp_w_gate", "exp_w_up", "exp_w_down", "shared_w_gate",
        "shared_w_up", "shared_w_down"]


def kernel(**inputs):
    import numpy as _np
    import concourse.bacc as _bacc
    from concourse.bass_utils import run_bass_kernel_spmd as _run

    nc = _bacc.Bacc("TRN2", target_bir_lowering=False, num_devices=1)
    arrays, aps = {}, {}
    for name in _INS:
        v = _np.ascontiguousarray(inputs[name])
        arrays[f"in_{name}"] = v
        aps[name] = nc.dram_tensor(f"in_{name}", v.shape, mybir.dt.from_np(v.dtype), kind="ExternalInput").ap()
    out = nc.dram_tensor("out_0", (1, T, D), F32, kind="ExternalOutput").ap()
    build(nc, aps, out)
    r = _run(nc, [arrays], core_ids=[0])
    return r.results[0]["out_0"]
```

```python
import math
from contextlib import ExitStack

import concourse.bass as bass
from concourse import mybir

F32 = mybir.dt.float32
BF16 = mybir.dt.bfloat16
I32 = mybir.dt.int32
U8 = mybir.dt.uint8
U32 = mybir.dt.uint32
ALU = mybir.AluOpType
ACT = mybir.ActivationFunctionType
AX = mybir.AxisListType

D = 1024
T = 256
PT = 128
TT = T // PT
KC = D // 128
HEADS = 4
HD = 64
NSTATE_TILES = 8
E = 64
FE = 256
SLOTS = 64
MAX_ROUNDS = T // SLOTS
TOP = 6
WSLOTS = 4
WCOLS = 6144
BLK = WCOLS // KC
EPS = 1e-6
ROUTED_SCALE = 2.5
MAGIC = 12582912.0
TWO_PI = 2 * math.pi
TP1 = 6.28125
TP2 = 0.0019350051879882812
TP3 = TWO_PI - TP1 - TP2
NEG = -1e30

R_C, R_N1, R_N2, R_ADAB = 0, 8, 16, 24
R_D, R_LB, R_QG, R_KG = 72, 74, 76, 77
R_LRE, R_LIM, R_LDT, R_END = 80, 88, 96, 104
SHIFT1, SCALE1, GATE1, SHIFT2, SCALE2, GATE2 = 0, 8, 16, 24, 32, 40

ACOLS = 512
ADA_HEAD = [0, 1, 2, 3]
ADA_TAIL = [8, 9, 6, 7, 4, 5, 10, 11]
ADA = ADA_HEAD + ADA_TAIL
BLOCKS = [("ada", n) for n in ADA_HEAD] + [("in", n) for n in range(3)]
for _n in range(3):
    BLOCKS += [("in", 3 + _n), ("ada", ADA_TAIL[2 * _n]), ("ada", ADA_TAIL[2 * _n + 1])]
BLOCKS += [("in", 6), ("ada", 10), ("glu", 0), ("wo", 0), ("ada", 11), ("out", 0), ("out", 1)]
ROWS_AFTER = {1: 8, 3: 9, 8: 6, 10: 7, 14: 4, 16: 5, 20: 10}
COLS_AFTER = {t + 1: n for t, n in ROWS_AFTER.items()}

GROUPS = ["ar0", "ar1", "xT0", "xT1", "vt", "ar2", "xT2", "xT3", "ar3",
          "pu", "pq", "pf", "bT", "cT", "vg0", "bu0", "bu1", "vg1", "mq", "bu2", "bu3", "kv0", "kv1"]


def tile_groups(t):
    return ([f"g{t}"] + ([f"ac{COLS_AFTER[t]}"] if t in COLS_AFTER else [])
            + ([f"ar{ROWS_AFTER[t]}"] if t in ROWS_AFTER else []))


LEVELS = [1, 2, 4, 8, 16, 32, 64, 128]
GROUPS += tile_groups(0)
for i in range(4, 8):
    GROUPS += ([f"bu{i}", f"bu{i + 1}"] if i % 2 == 0 else []) + tile_groups(i - 3)
    if i == 5:
        GROUPS += ["qT", "kT"]
GROUPS += tile_groups(5) + ["sc0", "sc1"] + tile_groups(6) + ["sc2", "sc3"] + tile_groups(7)
GROUPS += ["pT0", "pT1"] + tile_groups(8) + tile_groups(9) + ["pT2", "pT3"] + tile_groups(10) + ["mo"]
GROUPS += tile_groups(11) + ["L0a", "L0b"]
for k, b in enumerate(LEVELS):
    GROUPS += tile_groups(12 + k) + [f"L{b}a", f"L{b}b"]
GROUPS += tile_groups(20) + tile_groups(21) + ["ho"] + tile_groups(22) + tile_groups(23) + ["g1r0", "g1r1", "hoT"]
for j in range(KC):
    GROUPS += [f"za{j}", f"yb{j}"] + (["ar11"] if j == 1 else []) + (["ac11"] if j == 3 else [])
GROUPS += ["wo00", "wo01", "wo10", "wo11", "g2r0", "g2r1"]
GROUPS += [f"hT{i}" for i in range(4)] + ["rt", "sh0", "sh1", "ps"]
ROTATE = 7
AT = {name: (n % ROTATE, n // ROTATE) for n, name in enumerate(GROUPS)}
AT["adaA"] = (ROTATE, 0)
AT["sy"] = (ROTATE, 1)


def build(nc, a, out):
    ctx = ExitStack()
    with ctx:
        def sb(name, shape, dt=F32):
            return ctx.enter_context(nc.sbuf_tensor(name, shape, dt))

        def sem(name):
            return ctx.enter_context(nc.semaphore(name))

        ring = [sb(f"ring{n}", [128, WCOLS]) for n in range(WSLOTS)]
        ering = [ring[(len(BLOCKS) + n) % WSLOTS] for n in range(WSLOTS)]
        ident = sb("ident", [128, 128])
        ones = sb("ones", [128, 128])
        before = sb("before", [128, 128])
        upto = sb("upto", [128, 128])
        causal = sb("causal", [128, 128])
        level_mask = sb("level_mask", [128, 7, 128], U8)
        iota_e = sb("iota_e", [128, E])
        rows = sb("rows", [128, 128])
        log_dt = sb("log_dt", [128, 2])
        eps = sb("eps", [128, 1])
        cols = sb("cols", [128, R_END])
        craw = sb("craw", [128, KC])
        cond = sb("cond", [128, KC, 32])
        mod = sb("mod", [128, 48])
        a1 = sb("a1", [128, KC])
        a2 = sb("a2", [128, KC])
        perm = sb("perm", [128, 3, KC])
        bias_row = sb("bias_row", [128, E])
        hg_gain = sb("hg_gain", [128, HD])
        st = sb("st", [128, 64])
        sc = sb("sc", [128, 24, NSTATE_TILES])
        r3 = sb("r3", [128, 1536])
        pools = r3[:, 0:1024].rearrange("p (k r q x) -> p k r q x", k=2, r=2, q=2)
        bsrc = r3[:, 1024:1280].rearrange("p (r i h) -> p r i h", r=2, i=NSTATE_TILES)
        csrc = r3[:, 1280:1536].rearrange("p (r m s) -> p r m s", r=2, m=2)
        bt = sb("bt", [128, 4, 128])
        ct = sb("ct", [128, 4, 128])
        par = sb("par", [128, 4])
        par_i = sb("par_i", [128, 2], I32)
        rounds_i = sb("rounds_i", [128, 1], I32)

        xs = sb("xs", [128, TT, D])
        hT = sb("hT", [128, KC, T])
        merged = hT
        act = sb("act", [128, 24 * 256])
        r1 = sb("r1", [128, 24 * 256])
        r2 = sb("r2", [128, 26 * 256])
        gates = r1[:, :].rearrange("p (g t) -> p g t", g=24)

        row_i, col_i, xor_i = [act[:, 128 * n:128 * (n + 1)].bitcast(I32) for n in range(3)]

        def two(n):
            return act[:, 512 * n:512 * (n + 1)].rearrange("p (m t) -> p m t", m=2)

        uT, qT, key, logf, cum64, cumall, hi, hg, mq, mk, mv, keepm = [two(n) for n in range(12)]
        ogT = logf
        arow_last = act[:, 4096:4608]
        arow = [act[:, 1024 + ACOLS * n:1024 + ACOLS * (n + 1)] for n in range(4)]
        flat = lambda v: v.rearrange("p m t -> p (m t)")
        cosT = r2[:, 0:2048].rearrange("p (i t) -> p i t", i=8)
        sinT = r2[:, 2048:4096].rearrange("p (i t) -> p i t", i=8)
        s5tmp = r2[:, 4096:6656].rearrange("p (n t) -> p n t", n=5)
        expo = r2[:, 0:512]
        qe = r2[:, 512:1024].rearrange("p (m t) -> p m t", m=2)
        ke = r2[:, 1024:1536].rearrange("p (m t) -> p m t", m=2)
        score_h = r2[:, 1536:2560].rearrange("p (n t) -> p n t", n=8)
        score_x = r2[:, 2560:3072].rearrange("p (n t) -> p n t", n=4)
        x1 = r2[:, 4096:6144].rearrange("p (m t) -> p m t", m=2)
        prob = act[:, 4096:4864].rearrange("p (h s) -> p h s", h=2)
        probT = r3[:, :].rearrange("p (h s) -> p h s", h=HEADS)
        qn, kn, mo = [xs[:, 0, 512 * n:512 * n + 512].rearrange("p (m t) -> p m t", m=2) if n < 2
                      else xs[:, 1, 0:512].rearrange("p (m t) -> p m t", m=2) for n in range(3)]
        tmp = sb("tmp", [128, 1024])
        tmp2 = xs[:, 1, 512:1024]
        g1row, g2row = act[:, 2048:3072], act[:, 3072:4096]
        shared_gu = r2[:, 0:4096]
        shared_dn = act[:, 1024:3072]
        diag = r2[:, 0:1024].rearrange("p (c t) -> p c t", c=8)
        hp = xs
        parts = [r1[:, 1024 * n:1024 * (n + 1)].bitcast(BF16).rearrange("p (m t) -> p m t", m=2) for n in range(3)]
        h2T = r1[:, 3072:5120].rearrange("p (c t) -> p c t", c=8)
        hidS = hT[:, 0:2, :]
        silS = hT[:, 2:4, :]
        xe = hT[:, 4:8, :].rearrange("p c t -> p (c t)").rearrange("p (c s) -> p c s", c=8)
        ysb = r1[:, 5120:6144]
        sel = [act[:, 4096 + 128 * n:4224 + 128 * n].bitcast(BF16).rearrange("p (m s) -> p m s", m=2) for n in range(2)]
        selw = [act[:, 4352 + 256 * n:4608 + 256 * n].rearrange("p (m s) -> p m s", m=2) for n in range(2)]
        swt = act[:, 4864:5120]
        hid = act[:, 5120:5376].rearrange("p (j s) -> p j s", j=2)
        sil = act[:, 5376:5632]
        hid_t = act[:, 5632:5888]
        ro = act[:, 0:512]
        router = act[:, 512:1024].rearrange("p (c e) -> p c e", c=KC)
        s_r, b_r, m_r = [ro[:, 128 * n:128 * n + 128].rearrange("p (m e) -> p m e", m=2) for n in range(3)]
        w_r = ro[:, 384:512].rearrange("p (m e) -> p m e", m=2)
        onehot = tmp[:, 0:768].rearrange("p (m e k) -> p m e k", m=2, k=TOP)
        top8 = sb("top8", [128, 2, 8])
        idx8 = sb("idx8", [128, 2, 8], U32)
        idxf = sb("idxf", [128, 2, 8])
        NPOS = MAX_ROUNDS * E + 2
        pos_all, w_all = [r3[:, 2 * NPOS * n:2 * NPOS * (n + 1)].rearrange("p (m e) -> p m e", m=2) for n in range(2)]

        ps = [ctx.enter_context(nc.psum_tensor(f"bank{n}", [128, 512], F32)) for n in range(8)]

        def xhat_half(tt, h):
            return (hp[:, tt, :].rearrange("t (c p) -> t p c", c=KC)[:, 64 * h:64 * h + 64, :],
                    x1[:, tt, 512 * h:512 * h + 512].rearrange("t (p c) -> t p c", c=KC))

        w_full = [sem(f"w_full{n}") for n in range(WSLOTS)]
        gu_full = [sem(f"gu_full{n}") for n in range(WSLOTS)]
        dn_full = [sem(f"dn_full{n}") for n in range(WSLOTS)]
        bank_full = [sem(f"bank_full{n}") for n in range(8)]
        bank_free = [sem(f"bank_free{n}") for n in range(8)]
        consts = sem("consts")
        small_in, rows_ready = (sem(n) for n in (
            "small_in", "rows_ready"))
        x_in, c_in, x_again = (sem(n) for n in (
            "x_in", "c_in", "x_again"))
        in0_half, head_half = (sem(n) for n in (
            "in0_half", "head_half"))
        s5_in, bcast_in, perm_in = (sem(n) for n in (
            "s5_in", "bcast_in", "perm_in"))
        router_in, shared_in, shared_dn_in = (sem(n) for n in (
            "router_in", "shared_in", "shared_dn_in"))
        dve_seq, act_seq, pool_seq = (sem(n) for n in (
            "dve_seq", "act_seq", "pool_seq"))
        cond_zero, cond_ready = (sem(n) for n in (
            "cond_zero", "cond_ready"))
        rowsq, xn_ready = (sem(n) for n in (
            "rowsq", "xn_ready"))
        theta_ready, trig_ready = (sem(n) for n in (
            "theta_ready", "trig_ready"))
        bc_ready = sem("bc_ready")
        hT_ready, f_ready, logf_ready = (sem(n) for n in (
            "hT_ready", "f_ready", "logf_ready"))
        vals_ready, qk_sq, qknorm_ready = (sem(n) for n in (
            "vals_ready", "qk_sq", "qknorm_ready"))
        s5_state, s5_y, s5_tanh, s5_ready = (sem(n) for n in (
            "s5_state", "s5_y", "s5_tanh", "s5_ready"))
        sm_max, sm_exp, prob_ready = (sem(n) for n in (
            "sm_max", "sm_exp", "prob_ready"))
        lv_arg, lv_exp, lv_ready, score_ready = (sem(n) for n in (
            "lv_arg", "lv_exp", "lv_ready", "score_ready"))
        o_sq, o_silu, o_ready = (sem(n) for n in (
            "o_sq", "o_silu", "o_ready"))
        zs_ready, merged_ready = (sem(n) for n in (
            "zs_ready", "merged_ready"))
        mod_ready, diag_ready = (sem(n) for n in (
            "mod_ready", "diag_ready"))
        x1_ready, x1_sq, x1_sum, x1_root, h2_ready = (sem(n) for n in (
            "x1_ready", "x1_sq", "x1_sum", "x1_root", "h2_ready"))
        part_a, part_ready = (sem(n) for n in (
            "part_a", "part_ready"))
        r_exp, mask_ready, rounds_ready = (sem(n) for n in (
            "r_exp", "mask_ready", "rounds_ready"))
        sel_ready, g_done, xe_full, swt_done, swt_full = (sem(n) for n in (
            "sel_ready", "g_done", "xe_full", "swt_done", "swt_full"))
        gu_done, silu_done, hid_made, hid_turned, hid_full = (sem(n) for n in (
            "gu_done", "silu_done", "hid_made", "hid_turned", "hid_full"))
        y_done, y0_full, y1_full = (sem(n) for n in (
            "y_done", "y0_full", "y1_full"))
        acc0_done, acc_done = (sem(n) for n in (
            "acc0_done", "acc_done"))
        route_ready, outs0_ready, outs_ready, stored = (sem(n) for n in (
            "route_ready", "outs0_ready", "outs_ready", "stored"))

        block = ctx.enter_context(nc.Block())

        n_dma = {"wo": 2}
        landed, seen = {}, [0] * WSLOTS
        for s, blk in enumerate(BLOCKS):
            seen[s % WSLOTS] += 16 * n_dma.get(blk[0], 1)
            landed[blk] = (s % WSLOTS, seen[s % WSLOTS])

        def wait_full(eng, name):
            b, n = AT[name]
            eng.wait_ge(bank_full[b], n + 1)
            return ps[b]

        def free_of(name):
            return bank_free[AT[name][0]]

        @block.sync
        def _(sp):
            def w_view(w, lo, n):
                return w[:, lo:lo + n].rearrange("(c p) n -> p c n", p=128)

            def used(blk):
                if blk in LAST_GROUP:
                    b, cnt = AT[LAST_GROUP[blk]]
                    sp.wait_ge(bank_full[b], cnt + 1)
                else:
                    sp.wait_ge(bank_full[AT[f"ar{blk[1]}"][0]], AT[f"ar{blk[1]}"][1] + 1)

            def small(lo, cnt, src):
                sp.dma_start(rows[lo:lo + cnt, :], src).then_inc(small_in, 16)

            def small_inputs():
                row = lambda v: v.rearrange("(r p) -> r p", p=128)
                small(R_C, 8, row(a["c"][0]))
                small(R_ADAB, 48, row(a["ada_b"][0]))
                small(R_N1, 8, row(a["norm1_g"][0]))
                small(R_N2, 8, row(a["norm2_g"][0]))
                small(R_D, 2, row(a["ssm_d"][0]))
                small(R_LB, 2, row(a["hgrn_lb_logits"][0]))
                for r, nm in ((R_QG, "moba_q_norm_g"), (R_KG, "moba_k_norm_g")):
                    for k in range(2):
                        sp.dma_start(rows[r:r + 1, 64 * k:64 * k + 64], a[nm][0:1, :]).then_inc(small_in, 16)
                sp.dma_start(rows[78:80, :], row(a["ssm_d"][0])).then_inc(small_in, 16)
                small(R_LRE, 8, a["ssm_lambda_re"][0].rearrange("(i g) p -> i (g p)", g=2))
                small(R_LIM, 8, a["ssm_lambda_im"][0].rearrange("(i g) p -> i (g p)", g=2))
                sp.dma_start(log_dt[R_LDT:R_LDT + 8, :],
                            a["ssm_log_dt"][0].rearrange("(i g) -> i g", g=2)).then_inc(small_in, 16)

            def s5_inputs():
                for k, (bn, cn) in enumerate((("ssm_b_re", "ssm_c_re"), ("ssm_b_im", "ssm_c_im"))):
                    sp.dma_start(bsrc[:, k, :, :], a[bn][0].rearrange("g p h -> (g p) h").rearrange("(i q) h -> q i h", q=128)
                                ).then_inc(s5_in, 16)
                    sp.dma_start(csrc[:, k, :, :], a[cn][0].rearrange("g h p -> (g h) p").rearrange("(m q) p -> q m p", q=128)
                                ).then_inc(s5_in, 16)
                sp.dma_start(bias_row[:, :], a["router_bias"][0:1, :].to_broadcast([128, E])).then_inc(bcast_in, 16)
                sp.dma_start(hg_gain[:, :], a["hgrn_norm_g"][0:1, :].to_broadcast([128, HD])).then_inc(bcast_in, 16)

            sp.dma_start(craw[:, :], a["c"][0].rearrange("(p c) -> p c", c=KC)).then_inc(c_in, 16)
            sp.dma_start(xs[:, :, :], a["x"][0].rearrange("(m p) d -> p m d", p=PT)).then_inc(x_in, 16)
            ada, win, wout = a["ada_w"][0], a["w_in"][0], a["w_out"][0]
            for s, blk in enumerate(BLOCKS):
                kind, n = blk
                slot = s % WSLOTS
                if s >= WSLOTS:
                    used(BLOCKS[s - WSLOTS])
                if s == 1:
                    small_inputs()
                if (kind, n) == ("in", 1):
                    s5_inputs()
                dst = ring[slot]
                if kind in ("ada", "in"):
                    w = ada if kind == "ada" else win
                    width = ACOLS if kind == "ada" or n == 2 else BLK
                    lo = ACOLS * n if kind == "ada" else (BLK * n if n <= 2 else 2048 + BLK * (n - 3))
                    src = w_view(w, lo, width)
                    if kind == "ada":
                        src = w[:, lo:lo + width].rearrange("(p c) n -> p c n", c=KC)
                    dst = dst[:, 0:KC * width].rearrange("p (c n) -> p c n", c=KC)
                    if (kind, n) == ("in", 0):
                        sp.dma_start(dst[:, :, 0:width // 2], src[:, :, 0:width // 2]).then_inc(in0_half, 16)
                        dst, src = dst[:, :, width // 2:width], src[:, :, width // 2:width]
                    if blk == ("ada", ADA_HEAD[-1]):
                        sp.dma_start(dst[:, 0:4, :], src[:, 0:4, :]).then_inc(head_half, 16)
                        dst, src = dst[:, 4:8, :], src[:, 4:8, :]
                    sp.dma_start(dst, src).then_inc(w_full[slot], 16)
                elif kind == "glu":
                    sp.dma_start(dst[:, 0:4096].rearrange("p (c n) -> p c n", c=2),
                                 w_view(a["ssm_w_glu"][0], 0, 2 * D)).then_inc(w_full[slot], 16)
                elif kind == "wo":
                    for k, w in enumerate(("hgrn_w_o", "moba_w_o")):
                        sp.dma_start(dst[:, 2048 * k:2048 * (k + 1)].rearrange("p (c n) -> p c n", c=2),
                                     w_view(a[w][0], 0, D)).then_inc(w_full[slot], 16)
                else:
                    sp.dma_start(dst[:, 0:4096].rearrange("p (c n) -> p c n", c=KC),
                                 w_view(wout, 512 * n, 512)).then_inc(w_full[slot], 16)
            gate_w = a["exp_w_gate"][0].rearrange("e (p c) n -> p e (c n)", c=KC)
            up_w = a["exp_w_up"][0].rearrange("e (p c) n -> p e (c n)", c=KC)
            down_w = a["exp_w_down"][0].rearrange("e (c p) n -> p e c n", p=128)

            def load_gate_up(k, e):
                sp.dma_start(ering[k][:, 0:2048].unsqueeze(1), gate_w[:, bass.ds(e, 1), :]).then_inc(gu_full[k], 16)
                sp.dma_start(ering[k][:, 2048:4096].unsqueeze(1), up_w[:, bass.ds(e, 1), :]).then_inc(gu_full[k], 16)

            def load_down(k, e):
                sp.dma_start(ering[k][:, 4096:6144].rearrange("p (e c n) -> p e c n", e=1, c=2),
                             down_w[:, bass.ds(e, 1), :, :]).then_inc(dn_full[k], 16)

            for k in range(WSLOTS):
                if k == 2:
                    sp.wait_ge(bank_full[AT["g2r1"][0]], AT["g2r1"][1] + 1)
                    for m, w in enumerate(("shared_w_gate", "shared_w_up")):
                        sp.dma_start(shared_gu[:, 2048 * m:2048 * (m + 1)].rearrange("p (c n) -> p c n", c=KC),
                                     a[w][0].rearrange("(p c) n -> p c n", c=KC)).then_inc(shared_in, 16)
                    sp.wait_ge(x1_ready, 4)
                    sp.dma_start(shared_dn.rearrange("p (c n) -> p c n", c=2),
                                 w_view(a["shared_w_down"][0], 0, D)).then_inc(shared_dn_in, 16)
                used(BLOCKS[len(BLOCKS) - WSLOTS + k])
                load_gate_up(k, k)
                load_down(k, k)

            def load_four(turn, first):
                for k in (0, 2):
                    sp.wait_ge(gu_done, 2 * turn - 1 + k // 2)
                    load_gate_up(k, first + k)
                    load_gate_up(k + 1, first + k + 1)
                    sp.wait_ge(y_done, 4 * turn - 2 + k)
                    load_down(k, first + k)
                    load_down(k + 1, first + k + 1)

            with sp.Fori(1, E // WSLOTS) as i:
                load_four(i, i * WSLOTS)
            sp.wait_ge(rounds_ready, 1)
            n_rounds = sp.value_load(rounds_i[0:1, 0:1], min_val=1, max_val=MAX_ROUNDS)
            with sp.If(n_rounds > 1):
                with sp.Fori(1, n_rounds) as rd:
                    with sp.Fori(0, E // WSLOTS) as i:
                        load_four(rd * (E // WSLOTS) + i, i * WSLOTS)
            for q in range(4):
                h, tt = divmod(q, 2)
                sp.wait_ge((outs0_ready, outs_ready)[h], tt + 1)
                sp.dma_start(out[0, tt * PT:(tt + 1) * PT, 512 * h:512 * (h + 1)],
                             xs[:, tt, 512 * h:512 * (h + 1)]).then_inc(stored, 16)
            sp.wait_ge(stored, 64)
        @block.gpsimd
        def _(pool):
            n = [0]

            def link(ins):
                n[0] += 1
                ins.then_inc(pool_seq, 1)
                pool.wait_ge(pool_seq, n[0])

            link(pool.memset(ident[:, :], 0.0))
            link(pool.affine_select(out=ident[:, :], in_=ident[:, :], compare_op=ALU.not_equal, fill=1.0, base=0,
                                    pattern=[[-1, 128]], channel_multiplier=1))
            link(pool.memset(eps[:, :], EPS))
            pool.memset(ones[:, :], 1.0).then_inc(consts, 1)
            pool.iota(row_i[:, :], pattern=[[0, 128]], base=0, channel_multiplier=1).then_inc(consts, 1)
            pool.iota(col_i[:, :], pattern=[[1, 128]], base=0, channel_multiplier=0).then_inc(consts, 1)
            pool.iota(iota_e[:, :], pattern=[[1, E]], base=0, channel_multiplier=0,
                      allow_small_or_imprecise_dtypes=True).then_inc(consts, 1)
            link(pool.memset(before[:, :], 1.0))
            pool.affine_select(out=before[:, :], in_=before[:, :], compare_op=ALU.is_gt, fill=0.0, base=0,
                               pattern=[[1, 128]], channel_multiplier=-1).then_inc(consts, 1)
            link(pool.memset(upto[:, :], 1.0))
            pool.affine_select(out=upto[:, :], in_=upto[:, :], compare_op=ALU.is_ge, fill=0.0, base=0,
                               pattern=[[1, 128]], channel_multiplier=-1).then_inc(consts, 1)
            link(pool.memset(causal[:, :], 0.0))
            pool.affine_select(out=causal[:, :], in_=causal[:, :], compare_op=ALU.is_ge, fill=NEG, base=0,
                               pattern=[[-1, 128]], channel_multiplier=1).then_inc(consts, 1)
            for k, src in enumerate((a["ada_b"][0][128 * SCALE2:128 * SCALE2 + D], a["ada_b"][0][128 * SHIFT2:128 * SHIFT2 + D],
                                     a["norm2_g"][0])):
                pool.dma_start(perm[:, k, :], src.rearrange("(p c) -> p c", c=KC)).then_inc(perm_in, 16)
            pool.wait_ge(s5_ready, 1)
            pool.dma_start(x1, a["x"][0].rearrange("(m p) d -> p m d", p=PT)).then_inc(x_again, 16)
            pool.wait_ge(perm_in, 48)
            pool.wait_ge(free_of("ac9"), AT["ac9"][1] + 1)
            for h, g in enumerate(("ac8", "ac9")):
                pool.wait_ge(free_of(g), AT[g][1] + 1)
            link(pool.tensor_tensor(a2[:, :], mod[:, SCALE2:SCALE2 + 8], perm[:, 0, :], ALU.add))
            link(pool.tensor_scalar(out=a2[:, :], in0=a2[:, :], scalar1=1.0, scalar2=None, op0=ALU.add))
            pool.tensor_tensor(a2[:, :], a2[:, :], perm[:, 2, :], ALU.mult).then_inc(mod_ready, 1)
            def add_bias(lo, bias, gs):
                for g in gs:
                    pool.wait_ge(free_of(g), AT[g][1] + 1)
                pool.tensor_tensor(mod[:, lo:lo + 8], mod[:, lo:lo + 8], bias, ALU.add).then_inc(mod_ready, 1)

            add_bias(SHIFT2, perm[:, 1, :], ("ac6", "ac7"))
            for k, (lo, gs) in enumerate(((GATE1, ("ac4", "ac5")), (GATE2, ("ac10", "ac11")))):
                add_bias(lo, cols[:, R_ADAB + lo:R_ADAB + lo + 8], gs)
                pool.wait_ge(mod_ready, 3 + k)
                if k == 0:
                    pool.wait_ge(score_ready, 1)
                else:
                    pool.wait_ge(bank_full[AT["g1r1"][0]], AT["g1r1"][1] + 1)
                for c in range(KC):
                    pool.tensor_scalar(out=diag[:, c, :], in0=ident[:, :], scalar1=mod[:, lo + c:lo + c + 1],
                                       scalar2=None, op0=ALU.mult).then_inc(diag_ready, 1)
            pool.wait_ge(merged_ready, KC)
            pool.dma_start(router, a["router_w"][0].rearrange("(p c) n -> p c n", c=KC)).then_inc(router_in, 16)
            for tt in range(TT):
                pool.wait_ge(route_ready, tt + 1)
                pool.tensor_tensor(xs[:, tt, 0:512], xs[:, tt, 0:512], x1[:, tt, 0:512], ALU.add).then_inc(outs0_ready, 1)

        @block.scalar
        def _(act_e):
            e = nc.scalar
            n = [0]

            def link(ins):
                n[0] += 1
                ins.then_inc(act_seq, 1)
                act_e.wait_ge(act_seq, n[0])

            act_e.wait_ge(c_in, 16)
            act_e.wait_ge(cond_zero, 1)
            e.activation(cond[:, :, 0:1], craw[:, :].unsqueeze(2), ACT.Silu).then_inc(cond_zero, 1)
            act_e.wait_ge(x_in, 16)
            for tt in range(TT):
                if tt:
                    act_e.wait_ge(rowsq, tt)
                e.activation(tmp[:, :], xs[:, tt, :], ACT.Square, accum_out=st[:, tt:tt + 1]).then_inc(rowsq, 1)
            act_e.wait_ge(rowsq, 2)
            act_e.wait_ge(consts, 1)
            e.activation(st[:, 4:6], st[:, 0:2], ACT.Sqrt, bias=eps[:, :], scale=1.0 / D).then_inc(rowsq, 1)
            act_e.wait_ge(cond_ready, 1)
            link(e.activation(sc[:, 0, :], cols[:, R_LDT:R_LDT + 8], ACT.Exp))
            e.activation(st[:, 40:42], cols[:, R_LB:R_LB + 2], ACT.Exp, bias=0.0).then_inc(theta_ready, 1)
            def take_rows(n, dst):
                b = wait_full(act_e, f"ar{n}")
                e.activation(dst, b[:, :], ACT.Copy).then_inc(free_of(f"ar{n}"), 1)

            for n in ADA_HEAD:
                take_rows(n, arow[n])
            act_e.wait_ge(theta_ready, 3)
            e.activation(sc[:, 4, :], sc[:, 1, :], ACT.Exp).then_inc(trig_ready, 1)
            e.activation(sc[:, 5, :], sc[:, 2, :], ACT.Sin).then_inc(trig_ready, 1)
            e.activation(sc[:, 6, :], sc[:, 3, :], ACT.Sin).then_inc(trig_ready, 1)
            act_e.wait_ge(hT_ready, 1)
            for k in (0, 2):
                b = wait_full(act_e, f"xT{k}")
                for c in (2 * k, 2 * k + 1):
                    lo = 256 * (c % 2)
                    ins = e.activation(hT[:, c, :], b[:, lo:lo + 256], ACT.Identity,
                                       bias=mod[:, SHIFT1 + c:SHIFT1 + c + 1], scale=a1[:, c:c + 1])
                ins.then_inc(free_of(f"xT{k}"), 1)
            for g, dst in (("bT", bt), ("cT", ct)):
                b = wait_full(act_e, g)
                e.activation(dst[:, :, :].rearrange("p a b -> p (a b)"), b[:, :], ACT.Copy).then_inc(free_of(g), 1)
            b = wait_full(act_e, "pu")
            e.activation(flat(uT), b[:, :], ACT.Copy).then_inc(free_of("pu"), 1)
            b = wait_full(act_e, "pq")
            e.activation(flat(qT), b[:, :], ACT.Copy).then_inc(free_of("pq"), 1)
            b = wait_full(act_e, "pf")
            e.activation(flat(key), b[:, :], ACT.Exp, scale=-1.0).then_inc(free_of("pf"), 1)
            act_e.wait_ge(f_ready, 1)
            e.activation(flat(logf), flat(cum64), ACT.Ln).then_inc(logf_ready, 1)
            for tt in range(TT):
                b = wait_full(act_e, f"vg{tt}")
                e.activation(hi[:, tt, :], b[:, 0:256], ACT.Copy).then_inc(vals_ready, 1)
                e.activation(hg[:, tt, :], b[:, 256:512], ACT.Copy).then_inc(free_of(f"vg{tt}"), 1)
            b = wait_full(act_e, "mq")
            e.activation(flat(mq), b[:, :], ACT.Copy).then_inc(free_of("mq"), 1)
            for tt in range(TT):
                b = wait_full(act_e, f"kv{tt}")
                e.activation(mk[:, tt, :], b[:, 0:256], ACT.Copy).then_inc(vals_ready, 1)
                e.activation(mv[:, tt, :], b[:, 256:512], ACT.Copy).then_inc(free_of(f"kv{tt}"), 1)
            act_e.wait_ge(free_of("mq"), AT["mq"][1] + 1)
            act_e.wait_ge(vals_ready, 4)
            act_e.wait_ge(rowsq, 2)
            e.activation(tmp[:, 0:512], flat(mq), ACT.Square).then_inc(qk_sq, 1)
            e.activation(tmp[:, 512:1024], flat(mk), ACT.Square).then_inc(qk_sq, 1)
            act_e.wait_ge(qk_sq, 4)
            e.activation(st[:, 48:64], st[:, 48:64], ACT.Sqrt, bias=eps[:, :], scale=1.0 / HD).then_inc(qk_sq, 1)

            def take_cols(nn):
                b = wait_full(act_e, f"ac{nn}")
                if nn in (6, 7, 8, 9):
                    pr, lo = slice(64 * (nn % 2), 64 * (nn % 2) + 64), SHIFT2 if nn < 8 else SCALE2
                    e.activation(mod[pr, lo:lo + 8], b[pr, 0:8], ACT.Copy).then_inc(free_of(f"ac{nn}"), 1)
                else:
                    e.activation(mod[:, 4 * nn:4 * nn + 4], b[:, 0:4], ACT.Copy).then_inc(free_of(f"ac{nn}"), 1)

            def gate_tile(t):
                b = wait_full(act_e, f"g{t}")
                e.activation(gates[:, t, :], b[:, 0:256], ACT.Tanh, scale=0.5).then_inc(free_of(f"g{t}"), 1)
                if t in COLS_AFTER:
                    take_cols(COLS_AFTER[t])
                if t in ROWS_AFTER:
                    take_rows(ROWS_AFTER[t], tmp2)

            def softmax(h):
                act_e.wait_ge(sm_max, 2 * h + 2)
                for tt in range(TT):
                    lo, nn = (0, 128) if tt == 0 else (128, 256)
                    e.activation(prob[:, h % 2, lo:lo + nn], prob[:, h % 2, lo:lo + nn], ACT.Exp,
                                 bias=st[:, 8 + 2 * h + tt:9 + 2 * h + tt],
                                 accum_out=st[:, 16 + 2 * h + tt:17 + 2 * h + tt]).then_inc(sm_exp, 1)

            def level_exp(k):
                act_e.wait_ge(lv_arg, 2 * (k + 1))
                e.activation(expo, expo, ACT.Exp).then_inc(lv_exp, 1)

            def turned_qk():
                act_e.wait_ge(qknorm_ready, 3)
                for g, dst, col in (("qT", qn, 2), ("kT", kn, 3)):
                    b = wait_full(act_e, g)
                    e.activation(flat(dst), b[:, :], ACT.Copy, scale=st[:, col:col + 1]).then_inc(free_of(g), 1)

            def turned_probs(h):
                b = wait_full(act_e, f"pT{h}")
                e.activation(probT[:, h, :], b[:, 0:384], ACT.Copy).then_inc(free_of(f"pT{h}"), 1)

            for t in range(5):
                gate_tile(t)
                if t == 2:
                    turned_qk()
            gate_tile(5)
            act_e.wait_ge(s5_y, 1)
            e.activation(s5tmp[:, 2, :], s5tmp[:, 1, :], ACT.Tanh, scale=math.sqrt(2 / math.pi)).then_inc(s5_tanh, 1)
            gate_tile(6)
            softmax(0)
            softmax(1)
            gate_tile(7)
            turned_probs(0)
            turned_probs(1)
            softmax(2)
            gate_tile(8)
            softmax(3)
            gate_tile(9)
            turned_probs(2)
            turned_probs(3)
            gate_tile(10)
            b = wait_full(act_e, "mo")
            e.activation(flat(mo), b[:, :], ACT.Copy).then_inc(free_of("mo"), 1)
            gate_tile(11)
            for k in range(len(LEVELS)):
                level_exp(k)
                gate_tile(12 + k)
            gate_tile(20)
            gate_tile(21)
            act_e.wait_ge(free_of("vg1"), AT["vg1"][1] + 1)
            e.activation(keepm.rearrange("p m t -> p (m t)"), flat(hg), ACT.Tanh, scale=0.5).then_inc(o_silu, 1)
            b = wait_full(act_e, "ho")
            act_e.wait_ge(qk_sq, 5)
            e.activation(tmp[:, 0:512], b[:, :], ACT.Square).then_inc(o_sq, 1)
            act_e.wait_ge(o_sq, 2)
            e.activation(st[:, 48:56], st[:, 48:56], ACT.Sqrt, bias=eps[:, :], scale=1.0 / HD).then_inc(o_sq, 1)
            gate_tile(22)
            gate_tile(23)

            def take_row(r, dst):
                for h in range(2):
                    b = wait_full(act_e, f"{r}{h}")
                    e.activation(dst[:, 512 * h:512 * h + 512], b[:, :], ACT.Copy).then_inc(free_of(f"{r}{h}"), 1)

            take_row("g1r", g1row)
            b = wait_full(act_e, "hoT")
            e.activation(flat(ogT), b[:, :], ACT.Copy).then_inc(free_of("hoT"), 1)
            for j in range(KC):
                b = wait_full(act_e, f"za{j}")
                if j >= 2:
                    act_e.wait_ge(merged_ready, j - 1)
                e.activation(tmp2[:, 256 * (j % 2):256 * (j % 2) + 256], b[:, 256:512], ACT.Tanh,
                             scale=0.5).then_inc(zs_ready, 1)
                if j == 1:
                    take_rows(11, arow_last)
                if j == 3:
                    take_cols(11)
            for tt in range(TT):
                for h in range(2):
                    act_e.wait_ge(x1_ready, 2 * tt + h + 1)
                    if tt or h:
                        act_e.wait_ge(x1_sq, 2 * tt + h)
                    e.activation(ysb[:, 0:512], x1[:, tt, 512 * h:512 * h + 512], ACT.Square,
                                 accum_out=st[:, 32 + 2 * tt + h:33 + 2 * tt + h]).then_inc(x1_sq, 1)
                act_e.wait_ge(x1_sum, 2 * tt + 1)
                e.activation(st[:, 36 + tt:37 + tt], st[:, 36 + tt:37 + tt], ACT.Sqrt, bias=eps[:, :],
                             scale=1.0 / D).then_inc(x1_root, 1)
                act_e.wait_ge(x1_sum, 2 * tt + 2)
                e.activation(xhat_half(tt, 1)[0], xhat_half(tt, 1)[1], ACT.Copy,
                             scale=st[:, 36 + tt:37 + tt]).then_inc(h2_ready, 1)
                if tt == 0:
                    act_e.wait_ge(h2_ready, 2)
                    e.activation(parts[0][:, 0, :], hp[:, 0, :], ACT.Copy).then_inc(part_a, 1)
            act_e.wait_ge(mod_ready, 4)
            for k in (0, 2):
                b = wait_full(act_e, f"hT{k}")
                for c in (2 * k, 2 * k + 1):
                    lo = 256 * (c % 2)
                    ins = e.activation(h2T[:, c, :], b[:, lo:lo + 256], ACT.Identity,
                                       bias=mod[:, SHIFT2 + c:SHIFT2 + c + 1], scale=a2[:, c:c + 1])
                ins.then_inc(free_of(f"hT{k}"), 1)
            take_row("g2r", g2row)
            act_e.wait_ge(h2_ready, 4)
            e.activation(parts[0][:, 1, :], hp[:, 1, :], ACT.Copy).then_inc(part_a, 1)
            b = wait_full(act_e, "rt")
            e.activation(s_r.rearrange("p m e -> p (m e)"), b[:, 0:128], ACT.Exp, scale=-1.0).then_inc(r_exp, 1)
            b = wait_full(act_e, "sh0")
            e.activation(silS.rearrange("p c t -> p (c t)"), b[:, :], ACT.Silu).then_inc(free_of("sh0"), 1)

            def take_half(pair, h):
                act_e.wait_ge(g_done, 2 * pair + h + 1)
                for cc in range(4):
                    c = 4 * h + cc
                    ins = e.activation(xe[:, c, :], ps[4 + h][:, 128 * cc:128 * cc + 128], ACT.Identity,
                                       bias=mod[:, SHIFT2 + c:SHIFT2 + c + 1], scale=a2[:, c:c + 1])
                ins.then_inc(xe_full, 1)

            take_half(0, 0)
            take_half(0, 1)
            act_e.wait_ge(rounds_ready, 1)
            n_rounds = act_e.value_load(rounds_i[0:1, 0:1], min_val=1, max_val=MAX_ROUNDS)
            with act_e.Fori(0, n_rounds * (E // 2)) as p:
                act_e.wait_ge(gu_done, p + 1)
                act_e.wait_ge(hid_made, p + 1)
                e.activation(sil, ps[5][:, 0:FE], ACT.Silu).then_inc(silu_done, 1)
                take_half(p + 1, 0)
                take_half(p + 1, 1)
                act_e.wait_ge(y_done, 2 * p + 1)
                act_e.wait_ge(acc_done, p + 1)
                e.activation(ysb[:, 0:512], ps[7][:, :], ACT.Copy).then_inc(y0_full, 1)

        @block.vector
        def _(dve):
            v = nc.vector
            n = [0]

            def link(ins):
                n[0] += 1
                ins.then_inc(dve_seq, 1)
                dve.wait_ge(dve_seq, n[0])

            def mul(o, x, y):
                link(v.tensor_tensor(o, x, y, ALU.mult))

            def add(o, x, y):
                link(v.tensor_tensor(o, x, y, ALU.add))

            def sub(o, x, y):
                link(v.tensor_tensor(o, x, y, ALU.subtract))

            def ts(o, x, s1, op0, s2=None, op1=None):
                link(v.tensor_scalar(o, x, s1, s2, op0, op1) if op1 is not None
                     else v.tensor_scalar(o, x, s1, None, op0))

            v.memset(cond[:, :, :], 0.0).then_inc(cond_zero, 1)
            dve.wait_ge(rowsq, 3)
            link(v.reciprocal(st[:, 6:8], st[:, 4:6]))
            for tt in range(TT):
                v.tensor_scalar(xs[:, tt, :], xs[:, tt, :], st[:, 6 + tt:7 + tt], None, ALU.mult).then_inc(xn_ready, 1)
            dve.wait_ge(small_in, 16 * 14)
            v.tensor_copy(rows[R_LDT:R_LDT + 8, :].rearrange("i (g p) -> i g p", g=2),
                          log_dt[R_LDT:R_LDT + 8, :].unsqueeze(2).to_broadcast([8, 2, 64])).then_inc(rows_ready, 1)
            b = wait_full(dve, "vt")
            v.tensor_copy(cols[:, :], b[:, 0:R_END]).then_inc(cond_ready, 1)
            dve.wait_ge(cond_ready, 1)
            v.tensor_copy(par[:, 0:1], cols[:, 0:1]).then_inc(free_of("vt"), 1)
            dve.wait_ge(consts, 7)
            link(v.tensor_tensor(xor_i[:, :], row_i[:, :], col_i[:, :], ALU.bitwise_xor))
            for k, lv in enumerate(LEVELS[:-1]):
                link(v.tensor_scalar(level_mask[:, k, :], xor_i[:, :], float(lv), None, ALU.is_ge))
            link(v.tensor_scalar(par_i[:, 0:1], row_i[:, 0:1], 4, 1, ALU.logical_shift_right, ALU.bitwise_and))
            link(v.tensor_copy(par[:, 1:2], par_i[:, 0:1]))
            ts(par[:, 0:1], par[:, 1:2], -1.0, ALU.mult, 1.0, ALU.add)

            lre, lim = cols[:, R_LRE:R_LRE + 8], cols[:, R_LIM:R_LIM + 8]
            dve.wait_ge(theta_ready, 1)
            mul(sc[:, 1, :], lre, sc[:, 0, :])
            mul(sc[:, 7, :], lim, sc[:, 0, :])
            ts(sc[:, 8, :], sc[:, 7, :], 1.0 / TWO_PI, ALU.mult, MAGIC, ALU.add)
            ts(sc[:, 8, :], sc[:, 8, :], MAGIC, ALU.subtract)
            for part in (TP1, TP2, TP3):
                ts(sc[:, 9, :], sc[:, 8, :], -part, ALU.mult)
                add(sc[:, 7, :], sc[:, 7, :], sc[:, 9, :])
            v.tensor_scalar(sc[:, 2, :], sc[:, 7, :], 3.1415925, -3.1415925, ALU.min, ALU.max).then_inc(theta_ready, 1)
            v.tensor_scalar(sc[:, 3, :], sc[:, 7, :], 0.5, None, ALU.mult).then_inc(theta_ready, 1)
            b = wait_full(dve, "adaA")
            v.tensor_tensor(mod[:, 0:16], b[:, 0:16], cols[:, R_ADAB:R_ADAB + 16], ALU.add).then_inc(free_of("adaA"), 1)
            dve.wait_ge(free_of("adaA"), AT["adaA"][1] + 1)
            ts(a1[:, :], mod[:, SCALE1:SCALE1 + 8], 1.0, ALU.add)
            v.tensor_tensor(a1[:, :], a1[:, :], cols[:, R_N1:R_N1 + 8], ALU.mult).then_inc(hT_ready, 1)
            dve.wait_ge(hT_ready, 1)
            for k in (1, 3):
                b = wait_full(dve, f"xT{k}")
                for c in (2 * k, 2 * k + 1):
                    ins = v.tensor_scalar(hT[:, c, :], b[:, 256 * (c % 2):256 * (c % 2) + 256], a1[:, c:c + 1],
                                          mod[:, SHIFT1 + c:SHIFT1 + c + 1], ALU.mult, ALU.add)
                    if c % 2:
                        ins.then_inc(free_of(f"xT{k}"), 1)

            dve.wait_ge(trig_ready, 3)
            mag, sn, half = sc[:, 4, :], sc[:, 5, :], sc[:, 6, :]
            cs = sc[:, 10, :]
            mul(cs, half, half)
            ts(cs, cs, -2.0, ALU.mult, 1.0, ALU.add)
            ar, ai, den, cr, ci, t0, t1 = (sc[:, k, :] for k in (11, 12, 13, 14, 15, 16, 17))
            mul(ar, mag, cs)
            mul(ai, mag, sn)
            mul(den, lre, lre)
            mul(t0, lim, lim)
            add(den, den, t0)
            link(v.reciprocal(den, den))
            ts(ar, ar, 1.0, ALU.subtract)
            mul(t0, ar, lre)
            mul(t1, ai, lim)
            add(cr, t0, t1)
            mul(cr, cr, den)
            mul(t0, ai, lre)
            mul(t1, ar, lim)
            sub(ci, t0, t1)
            mul(ci, ci, den)
            link(v.memset(r3[:, 0:512], 0.0))
            dve.wait_ge(s5_in, 64)
            bb = r3[:, 0:512].rearrange("p (r i h) -> p r i h", r=2, h=32)
            prod = s5tmp[:, 0, 0:128].rearrange("p (i h) -> p i h", h=16)
            wide = lambda col: col.unsqueeze(2).to_broadcast([128, 8, 16])
            for r, (x, y, op) in enumerate(((cr, ci, ALU.subtract), (ci, cr, ALU.add))):
                mul(prod, bsrc[:, 0, :, :], wide(x))
                other = s5tmp[:, 0, 128:256].rearrange("p (i h) -> p i h", h=16)
                mul(other, bsrc[:, 1, :, :], wide(y))
                for half_ in range(2):
                    pr = slice(64 * half_, 64 * half_ + 64)
                    link(v.tensor_tensor(bb[pr, r, :, 16 * half_:16 * half_ + 16], prod[pr], other[pr], op))
            for r in range(2):
                for half_ in range(2):
                    ins = v.tensor_scalar(pools[:, 1, r, :, 64 * half_:64 * half_ + 64], csrc[:, r, :, :],
                                          par[:, half_:half_ + 1], -1.0 if r else 1.0, ALU.mult, ALU.mult)
                    link(ins)
            v.tensor_copy(par[:, 2:3], par[:, 0:1]).then_inc(bc_ready, 1)
            ec, es, t2, t3 = (sc[:, k, :] for k in (18, 19, 20, 21))
            link(v.tensor_copy(ec, cs))
            link(v.tensor_copy(es, sn))
            link(v.memset(cosT[:, :, 0:1], 1.0))
            link(v.memset(sinT[:, :, 0:1], 0.0))
            w = 1
            while w < T:
                ecw, esw = (z.unsqueeze(2).to_broadcast([128, 8, w]) for z in (ec, es))
                ta = s5tmp[:, 0:2, :].rearrange("p a b -> p (a b)")[:, 0:8 * w].rearrange("p (i t) -> p i t", i=8)
                tb = s5tmp[:, 2:4, :].rearrange("p a b -> p (a b)")[:, 0:8 * w].rearrange("p (i t) -> p i t", i=8)
                v.tensor_tensor(ta, cosT[:, :, 0:w], ecw, ALU.mult)
                link(v.tensor_tensor(tb, sinT[:, :, 0:w], esw, ALU.mult))
                sub(cosT[:, :, w:2 * w], ta, tb)
                v.tensor_tensor(ta, cosT[:, :, 0:w], esw, ALU.mult)
                link(v.tensor_tensor(tb, sinT[:, :, 0:w], ecw, ALU.mult))
                add(sinT[:, :, w:2 * w], ta, tb)
                mul(t2, ec, ec)
                mul(t3, es, es)
                mul(es, ec, es)
                sub(ec, t2, t3)
                add(es, es, es)
                w *= 2

            e1 = st[:, 40:42]
            link(v.reciprocal(st[:, 42:44], e1))
            mul(st[:, 42:44], st[:, 42:44], e1)
            sub(st[:, 42:44], st[:, 42:44], st[:, 42:44])
            ts(st[:, 44:46], st[:, 42:44], -1.0, ALU.mult, 1.0, ALU.add)
            dve.wait_ge(free_of("pf"), AT["pf"][1] + 1)
            ts(flat(key), flat(key), 1.0, ALU.add)
            link(v.reciprocal(flat(key), flat(key)))
            for m in range(2):
                ts(cum64[:, m, :], key[:, m, :], st[:, 44 + m:45 + m], ALU.mult, st[:, 42 + m:43 + m], ALU.add)
            v.tensor_scalar(flat(key), flat(cum64), -1.0, 1.0, ALU.mult, ALU.add).then_inc(f_ready, 1)
            A, B, W, Z, S = (s5tmp[:, k, :] for k in range(5))
            W2, Z2, S2 = W, Z, S

            def s5_step(i):
                b = wait_full(dve, f"bu{i}")
                cw = cosT[:, i, :].unsqueeze(1).to_broadcast([128, 2, 256])
                sw = sinT[:, i, :].unsqueeze(1).to_broadcast([128, 2, 256])
                three = lambda z: z.rearrange("p (r t) -> p r t", r=2)
                v.tensor_tensor(three(A), three(b[:, :]), cw, ALU.mult)
                v.tensor_tensor(three(B), three(b[:, :]), sw, ALU.mult).then_inc(free_of(f"bu{i}"), 1)
                dve.wait_ge(free_of(f"bu{i}"), AT[f"bu{i}"][1] + 1)
                v.tensor_tensor(W2[:, 0:256], A[:, 0:256], B[:, 256:512], ALU.add)
                link(v.tensor_tensor(W2[:, 256:512], A[:, 256:512], B[:, 0:256], ALU.subtract))
                for r in range(2):
                    ins = v.tensor_tensor_scan(Z2[:, 256 * r:256 * r + 256], mag[:, i:i + 1].to_broadcast([128, 256]),
                                               W2[:, 256 * r:256 * r + 256], 0.0, ALU.mult, ALU.add)
                link(ins)
                v.tensor_tensor(three(A), three(Z2), cw, ALU.mult)
                link(v.tensor_tensor(three(B), three(Z2), sw, ALU.mult))
                if i:
                    dve.wait_ge(s5_state, 2 * i)
                v.tensor_tensor(S2[:, 0:256], A[:, 0:256], B[:, 256:512], ALU.subtract)
                v.tensor_tensor(S2[:, 256:512], A[:, 256:512], B[:, 0:256], ALU.add).then_inc(s5_state, 1)
                dve.wait_ge(s5_state, 2 * i + 1)
            for i in range(4):
                s5_step(i)
            dve.wait_ge(qk_sq, 2)
            for k in range(2):
                v.tensor_reduce(st[:, 48 + 8 * k:56 + 8 * k],
                                tmp[:, 512 * k:512 * k + 512].rearrange("p (h d) -> p h d", d=HD), AX.X,
                                ALU.add).then_inc(qk_sq, 1)
            dve.wait_ge(qk_sq, 5)
            link(v.reciprocal(st[:, 48:64], st[:, 48:64]))
            for k, src in enumerate((mq, mk)):
                r8 = st[:, 48 + 8 * k:56 + 8 * k]
                v4 = flat(src).rearrange("p (h d) -> p h d", d=HD)
                v.tensor_tensor(v4, v4, r8.unsqueeze(2).to_broadcast([128, 8, HD]), ALU.mult).then_inc(qknorm_ready, 1)
            ts(st[:, 2:3], cols[:, R_QG:R_QG + 1], HD ** -0.5, ALU.mult)
            v.tensor_copy(st[:, 3:4], cols[:, R_KG:R_KG + 1]).then_inc(qknorm_ready, 1)

            for i in range(4, NSTATE_TILES):
                s5_step(i)
            b = wait_full(dve, "sy")
            for m in range(2):
                ins = v.scalar_tensor_tensor(out=S[:, 256 * m:256 * m + 256], in0=uT[:, m, :],
                                             scalar=cols[:, R_D + m:R_D + m + 1], in1=b[:, 256 * m:256 * m + 256],
                                             op0=ALU.mult, op1=ALU.add)
            ins.then_inc(free_of("sy"), 1)
            dve.wait_ge(free_of("sy"), AT["sy"][1] + 1)
            mul(A, S, S)
            ts(A, A, 0.044715, ALU.mult, 1.0, ALU.add)
            v.tensor_tensor(B, A, S, ALU.mult).then_inc(s5_y, 1)
            dve.wait_ge(s5_tanh, 1)
            link(v.scalar_tensor_tensor(out=B, in0=W, scalar=1.0, in1=S, op0=ALU.add, op1=ALU.mult))
            v.tensor_scalar(flat(uT), B, 0.5, None, ALU.mult).then_inc(s5_ready, 1)

            for h in range(HEADS):
                b = wait_full(dve, f"sc{h}")
                if h >= 2:
                    dve.wait_ge(bank_full[AT[f"pT{h - 2}"][0]], AT[f"pT{h - 2}"][1] + 1)
                pr = prob[:, h % 2, :]
                v.tensor_tensor(pr[:, 0:128], b[:, 0:128], causal[:, :], ALU.add)
                v.tensor_copy(pr[:, 128:256], b[:, 128:256])
                ins = v.tensor_tensor(pr[:, 256:384], b[:, 256:384], causal[:, :], ALU.add)
                ins.then_inc(free_of(f"sc{h}"), 1)
                dve.wait_ge(free_of(f"sc{h}"), AT[f"sc{h}"][1] + 1)
                for tt in range(TT):
                    lo, nn = (0, 128) if tt == 0 else (128, 256)
                    v.tensor_reduce(st[:, 8 + 2 * h + tt:9 + 2 * h + tt], pr[:, lo:lo + nn], AX.X, ALU.max,
                                    negate=True).then_inc(sm_max, 1)
                dve.wait_ge(sm_exp, 2 * h + 2)
                link(v.reciprocal(st[:, 24 + 2 * h:26 + 2 * h], st[:, 16 + 2 * h:18 + 2 * h]))
                for tt in range(TT):
                    lo, nn = (0, 128) if tt == 0 else (128, 256)
                    v.tensor_scalar(pr[:, lo:lo + nn], pr[:, lo:lo + nn], st[:, 24 + 2 * h + tt:25 + 2 * h + tt], None,
                                    ALU.mult).then_inc(prob_ready, 1)

            link(v.memset(flat(keepm), 1.0))
            for c in range(0, 512, 64):
                link(v.memset(flat(keepm)[:, c:c + 1], 0.0))
            dve.wait_ge(logf_ready, 1)
            link(v.tensor_tensor_scan(flat(cum64), flat(keepm), flat(logf), 0.0, ALU.mult, ALU.add))
            link(v.memset(keepm[:, :, 64:256:64], 1.0))
            link(v.tensor_tensor_scan(flat(cumall), flat(keepm), flat(logf), 0.0, ALU.mult, ALU.add))

            def take_scores(k):
                for half_, g in enumerate("ab"):
                    name = f"L{0 if k == 0 else LEVELS[k - 1]}{g}"
                    b = wait_full(dve, name)
                    dst = score_h[:, 4 * half_:4 * half_ + 4, :]
                    src = b[:, :].rearrange("p (n t) -> p n t", n=4)
                    if k == 0:
                        ins = v.tensor_copy(dst, src)
                    else:
                        ins = v.copy_predicated(dst, level_mask[:, k - 1, :].unsqueeze(1).to_broadcast([128, 4, 128]), src)
                    ins.then_inc(free_of(name), 1)

            for k, lv in enumerate(LEVELS):
                src = cum64 if lv <= 32 else cumall
                cv = flat(src).rearrange("p (n r s) -> p n r s", r=2, s=lv)
                ev = expo.rearrange("p (n r s) -> p n r s", r=2, s=lv)
                ref = cv[:, :, 0, lv - 1:lv].to_broadcast([128, 256 // lv, lv])
                if k:
                    dve.wait_ge(lv_ready, 2 * k)
                v.tensor_tensor(ev[:, :, 0, :], ref, cv[:, :, 0, :], ALU.subtract).then_inc(lv_arg, 1)
                v.tensor_tensor(ev[:, :, 1, :], cv[:, :, 1, :], ref, ALU.subtract).then_inc(lv_arg, 1)
                if k == 0:
                    take_scores(0)
                dve.wait_ge(lv_exp, k + 1)
                if k:
                    g = f"L{LEVELS[k - 1]}b"
                    dve.wait_ge(bank_full[AT[g][0]], AT[g][1] + 1)
                v.tensor_tensor(flat(qe), flat(qT), expo, ALU.mult).then_inc(lv_ready, 1)
                v.tensor_tensor(flat(ke), flat(key), expo, ALU.mult).then_inc(lv_ready, 1)
                if k:
                    g = f"L{LEVELS[k - 2] if k > 1 else 0}b"
                    dve.wait_ge(free_of(g), AT[g][1] + 1)
                    take_scores(k)
            for odd, g in enumerate("ab"):
                b = wait_full(dve, f"L128{g}")
                v.tensor_copy(score_x[:, 2 * odd:2 * odd + 2, :],
                              b[:, 0:256].rearrange("p (n t) -> p n t", n=2)).then_inc(free_of(f"L128{g}"), 1)
            dve.wait_ge(free_of("L64b"), AT["L64b"][1] + 1)
            v.tensor_tensor(score_h, score_h, upto[:, :].unsqueeze(1).to_broadcast([128, 8, 128]),
                            ALU.mult).then_inc(score_ready, 1)
            dve.wait_ge(o_sq, 1)
            r8 = st[:, 48:56]
            v.tensor_reduce(r8, tmp[:, 0:512].rearrange("p (h d) -> p h d", d=HD), AX.X, ALU.add).then_inc(o_sq, 1)
            dve.wait_ge(o_sq, 3)
            link(v.reciprocal(r8, r8))
            b = wait_full(dve, "ho")
            o3 = tmp[:, 0:512].rearrange("p (h d) -> p h d", d=HD)
            v.tensor_tensor(o3, b[:, :].rearrange("p (h d) -> p h d", d=HD),
                            r8.unsqueeze(2).to_broadcast([128, 8, HD]), ALU.mult).then_inc(free_of("ho"), 1)
            dve.wait_ge(free_of("ho"), AT["ho"][1] + 1)
            dve.wait_ge(bcast_in, 32)
            mul(o3, o3, hg_gain[:, :].unsqueeze(1).to_broadcast([128, 8, HD]))
            dve.wait_ge(o_silu, 1)
            km = flat(keepm)
            link(v.scalar_tensor_tensor(out=km, in0=km, scalar=1.0, in1=flat(hg), op0=ALU.add, op1=ALU.mult))
            v.scalar_tensor_tensor(out=tmp[:, 0:512], in0=km, scalar=0.5, in1=tmp[:, 0:512], op0=ALU.mult,
                                   op1=ALU.mult).then_inc(o_ready, 1)

            for t in range(24):
                dve.wait_ge(free_of(f"g{t}"), AT[f"g{t}"][1] + 1)
            for k in range(3):
                g8 = gates[:, 8 * k:8 * k + 8, :].rearrange("p g t -> p (g t)")
                link(v.tensor_scalar(g8, g8, 0.5, 0.5, ALU.mult, ALU.add))
            for j in range(KC):
                if j:
                    dve.wait_ge(merged_ready, j)
                dve.wait_ge(zs_ready, j + 1)
                b = ps[AT[f"za{j}"][0]]
                z = tmp2[:, 256 * (j % 2):256 * (j % 2) + 256]
                link(v.scalar_tensor_tensor(out=z, in0=z, scalar=1.0, in1=b[:, 0:256], op0=ALU.add, op1=ALU.mult))
                v.scalar_tensor_tensor(out=z, in0=z, scalar=0.5, in1=gates[:, j, :], op0=ALU.mult,
                                       op1=ALU.mult).then_inc(free_of(f"za{j}"), 1)
                b = wait_full(dve, f"yb{j}")
                y1, y2 = tmp[:, 512:768], tmp[:, 768:1024]
                v.tensor_tensor(y1, b[:, 0:256], gates[:, 8 + j, :], ALU.mult)
                v.tensor_tensor(y2, b[:, 256:512], gates[:, 16 + j, :], ALU.mult).then_inc(free_of(f"yb{j}"), 1)
                dve.wait_ge(free_of(f"yb{j}"), AT[f"yb{j}"][1] + 1)
                add(y1, y1, y2)
                v.tensor_tensor(merged[:, j, :], y1, z, ALU.add).then_inc(merged_ready, 1)
            def split_parts(tt):
                dve.wait_ge(part_a, tt + 1)
                sub(tmp[:, :], hp[:, tt, :], parts[0][:, tt, :])
                link(v.tensor_copy(parts[1][:, tt, :], tmp[:, :]))
                sub(tmp[:, :], tmp[:, :], parts[1][:, tt, :])
                v.tensor_copy(parts[2][:, tt, :], tmp[:, :]).then_inc(part_ready, 1)
                dve.wait_ge(part_ready, tt + 1)

            dve.wait_ge(x_again, 16)
            for tt in range(TT):
                for h in range(2):
                    cs_ = slice(512 * h, 512 * h + 512)
                    b = wait_full(dve, f"wo{tt}{h}")
                    dve.wait_ge(free_of(f"g1r{h}"), AT[f"g1r{h}"][1] + 1)
                    v.tensor_tensor(tmp2, b[:, :], g1row[:, cs_], ALU.mult).then_inc(free_of(f"wo{tt}{h}"), 1)
                    dve.wait_ge(free_of(f"wo{tt}{h}"), AT[f"wo{tt}{h}"][1] + 1)
                    v.tensor_tensor(x1[:, tt, cs_], x1[:, tt, cs_], tmp2, ALU.add).then_inc(x1_ready, 1)
                    dve.wait_ge(x1_ready, 2 * tt + h + 1)
                dve.wait_ge(x1_sq, 2 * tt + 2)
                root = st[:, 36 + tt:37 + tt]
                v.tensor_tensor(root, st[:, 32 + 2 * tt:33 + 2 * tt], st[:, 33 + 2 * tt:34 + 2 * tt],
                                ALU.add).then_inc(x1_sum, 1)
                dve.wait_ge(x1_root, tt + 1)
                v.reciprocal(root, root).then_inc(x1_sum, 1)
                dve.wait_ge(x1_sum, 2 * tt + 2)
                v.tensor_scalar(xhat_half(tt, 0)[0], xhat_half(tt, 0)[1], root, None, ALU.mult).then_inc(h2_ready, 1)
                if tt == 0:
                    dve.wait_ge(h2_ready, 2)
                    split_parts(0)
            dve.wait_ge(mod_ready, 4)
            for k in (1, 3):
                b = wait_full(dve, f"hT{k}")
                for c in (2 * k, 2 * k + 1):
                    lo = 256 * (c % 2)
                    ins = v.tensor_scalar(h2T[:, c, :], b[:, lo:lo + 256], a2[:, c:c + 1],
                                          mod[:, SHIFT2 + c:SHIFT2 + c + 1], ALU.mult, ALU.add)
                ins.then_inc(free_of(f"hT{k}"), 1)
            split_parts(1)
            v.memset(pos_all[:, :, :], -1.0)
            link(v.memset(w_all[:, :, :], 0.0))
            dve.wait_ge(r_exp, 1)
            flat_e = lambda z: z.rearrange("p m e -> p (m e)")
            ts(flat_e(s_r), flat_e(s_r), 1.0, ALU.add)
            v.reciprocal(flat_e(s_r), flat_e(s_r)).then_inc(free_of("rt"), 1)
            dve.wait_ge(free_of("rt"), AT["rt"][1] + 1)
            add(b_r, s_r, bias_row[:, :].unsqueeze(1).to_broadcast([128, 2, E]))
            for tt in range(TT):
                link(v.max(top8[:, tt, :], b_r[:, tt, :]))
                link(v.max_index(idx8[:, tt, :], top8[:, tt, :], b_r[:, tt, :]))
            link(v.tensor_copy(idxf[:, :, :], idx8[:, :, :]))
            for tt in range(TT):
                link(v.tensor_tensor(onehot[:, tt, :, :], iota_e[:, :].unsqueeze(2).to_broadcast([128, E, TOP]),
                                     idxf[:, tt, 0:TOP].unsqueeze(1).to_broadcast([128, E, TOP]), ALU.is_equal))
            v.tensor_reduce(flat_e(m_r), tmp[:, 0:768].rearrange("p (e k) -> p e k", k=TOP), AX.X,
                            ALU.add).then_inc(mask_ready, 1)
            dve.wait_ge(mask_ready, 1)
            mul(w_r, s_r, m_r)
            link(v.tensor_reduce(st[:, 36:38], w_r, AX.X, ALU.add))
            link(v.reciprocal(st[:, 36:38], st[:, 36:38]))
            for tt in range(TT):
                ts(w_r[:, tt, :], w_r[:, tt, :], st[:, 36 + tt:37 + tt], ALU.mult, ROUTED_SCALE, ALU.mult)
            for rd in range(MAX_ROUNDS):
                link(v.tensor_copy(w_all[:, :, E * rd:E * rd + E], w_r))
            b = wait_full(dve, "ps")
            p2 = lambda z: z.rearrange("p (m e) -> p m e", m=2)
            link(v.scalar_tensor_tensor(out=b_r, in0=p2(b[:, 0:128]), scalar=1.0, in1=m_r, op0=ALU.add, op1=ALU.mult))
            for rd in range(MAX_ROUNDS):
                link(v.tensor_scalar(pos_all[:, :, E * rd:E * rd + E], b_r, -1.0 - SLOTS * rd, None, ALU.add))
            v.tensor_reduce(st[:, 38:39], b[:, 128:192], AX.X, ALU.max).then_inc(free_of("ps"), 1)
            dve.wait_ge(free_of("ps"), AT["ps"][1] + 1)
            ts(st[:, 39:40], st[:, 38:39], float(SLOTS), ALU.is_gt, 1.0, ALU.add)
            for rd in range(2, MAX_ROUNDS):
                link(v.scalar_tensor_tensor(out=st[:, 39:40], in0=st[:, 38:39], scalar=float(SLOTS * rd),
                                            in1=st[:, 39:40], op0=ALU.is_gt, op1=ALU.add))
            v.tensor_copy(rounds_i[:, :], st[:, 39:40]).then_inc(rounds_ready, 1)
            dve.wait_ge(rounds_ready, 1)

            def select_pair(pair, buf):
                four = lambda z, e0: z[:, :, bass.ds(e0, 2)].unsqueeze(3).to_broadcast([128, 2, 2, SLOTS])
                sl = sel[buf].rearrange("p m (x s) -> p m x s", x=2)
                sw_ = selw[buf].rearrange("p m (x s) -> p m x s", x=2)
                for tt in range(TT):
                    io = iota_e[:, 0:SLOTS].unsqueeze(1).to_broadcast([128, 2, SLOTS])
                    ins = v.tensor_tensor(sl[:, tt, :, :], io, four(pos_all, pair * 2)[:, tt, :, :], ALU.is_equal)
                    ins.then_inc(sel_ready, 1)
                return sl, sw_, four

            def weigh_pair(pair, buf, count):
                sl, sw_, four = select_pair(pair, buf)
                dve.wait_ge(sel_ready, count)
                for tt in range(TT):
                    v.tensor_tensor(sw_[:, tt, :, :], sl[:, tt, :, :], four(w_all, pair * 2)[:, tt, :, :],
                                    ALU.mult).then_inc(sel_ready, 1)

            b = wait_full(dve, "sh1")
            dve.wait_ge(free_of("sh0"), AT["sh0"][1] + 1)
            v.tensor_tensor(hidS.rearrange("p c t -> p (c t)"), silS.rearrange("p c t -> p (c t)"), b[:, :],
                            ALU.mult).then_inc(free_of("sh1"), 1)
            weigh_pair(0, 0, 2)
            n_rounds = dve.value_load(rounds_i[0:1, 0:1], min_val=1, max_val=MAX_ROUNDS)
            with dve.Fori(0, n_rounds * (E // 4)) as i:
                for k in range(2):
                    p = i * 2 + k
                    dve.wait_ge(g_done, 2 * p + 2)
                    dve.wait_ge(swt_done, p + 1)
                    weigh_pair(p + 1, 1 - k, 4 * p + 6)
                    dve.wait_ge(silu_done, p + 1)
                    dve.wait_ge(hid_turned, p + 1)
                    v.tensor_tensor(hid_t, sil, ps[5][:, FE:2 * FE], ALU.mult).then_inc(hid_made, 1)
                    dve.wait_ge(swt_done, p + 2)
                    v.tensor_copy(swt, ps[7][:, 0:256]).then_inc(swt_full, 1)
                    dve.wait_ge(hid_turned, p + 2)
                    v.tensor_copy(hid.rearrange("p j s -> p (j s)"), ps[6][:, 0:256]).then_inc(hid_full, 1)
                    dve.wait_ge(y_done, 2 * p + 2)
                    v.tensor_copy(ysb[:, 512:1024], ps[6][:, :]).then_inc(y1_full, 1)
            dve.wait_ge(acc0_done, n_rounds * (E // 2))
            for q in range(4):
                h, tt = divmod(q, 2)
                if q == 2:
                    dve.wait_ge(acc_done, n_rounds * (E // 2) + 1)
                cs_ = slice(512 * h, 512 * h + 512)
                v.tensor_tensor(xs[:, tt, cs_], ps[2 * tt + h][:, :], g2row[:, cs_], ALU.mult).then_inc(route_ready, 1)
            for tt in range(TT):
                dve.wait_ge(route_ready, 3 + tt)
                v.tensor_tensor(xs[:, tt, cs_], xs[:, tt, cs_], x1[:, tt, cs_], ALU.add).then_inc(outs_ready, 1)

        @block.tensor
        def _(pe):
            def begin(name):
                b, cnt = AT[name]
                if cnt:
                    pe.wait_ge(bank_free[b], cnt)
                return ps[b]

            def end(name, ins):
                ins.then_inc(bank_full[AT[name][0]], 1)

            def block_of(blk):
                slot, cnt = landed[blk]
                pe.wait_ge(w_full[slot], cnt)
                return ring[slot]

            def view(w, width):
                return w[:, 0:KC * width].rearrange("p (c n) -> p c n", c=KC)

            pe.wait_ge(cond_zero, 2)

            def ada_rows(n):
                w = view(ring[landed[("ada", n)][0]], ACOLS)
                b = begin(f"ar{n}")
                if n == ADA_HEAD[-1]:
                    pe.wait_ge(head_half, 16)
                else:
                    block_of(("ada", n))
                for c in range(KC):
                    if n == ADA_HEAD[-1] and c == 4:
                        block_of(("ada", n))
                    q = c % 4
                    ins = pe.matmul(b[32 * q:32 * q + 32, :], cond[:, c, :], w[:, c, :], start=(c < 4), stop=(c >= 4),
                                    skip_group_check=True)
                end(f"ar{n}", ins)

            def ada_cols(n):
                pe.wait_ge(free_of(f"ar{n}"), AT[f"ar{n}"][1] + 1)
                b = begin(f"ac{n}")
                rows_of = arow_last if n == 11 else tmp2
                if n in (6, 7, 8, 9):
                    for c in range(KC):
                        ins = pe.matmul(b[64 * (n % 2):64 * (n % 2) + 64, c:c + 1], rows_of[:, c:ACOLS:KC], ones[:, 0:1],
                                        start=True, stop=True)
                else:
                    for c in range(4):
                        ins = pe.matmul(b[:, c:c + 1], rows_of[:, 128 * c:128 * c + 128], ones[:, 0:1],
                                        start=True, stop=True)
                end(f"ac{n}", ins)

            def turn_x(k):
                b = begin(f"xT{k}")
                pe.wait_ge(xn_ready, 2)
                for c in (2 * k, 2 * k + 1):
                    for tt in range(TT):
                        lo = 256 * (c % 2) + 128 * tt
                        ins = pe.transpose(b[:, lo:lo + 128], xs[:, tt, 128 * c:128 * c + 128], ident[:, :])
                end(f"xT{k}", ins)

            def head_cols(n):
                pe.wait_ge(free_of(f"ar{n}"), AT[f"ar{n}"][1] + 1)
                for c in range(4):
                    ins = pe.matmul(ps[AT["adaA"][0]][:, 4 * n + c:4 * n + c + 1], arow[n][:, 128 * c:128 * c + 128],
                                    ones[:, 0:1], start=True, stop=True)
                return ins

            pe.wait_ge(consts, 1)
            ada_rows(0)
            ada_rows(1)
            turn_x(0)
            turn_x(1)
            pe.wait_ge(small_in, 16 * 14)
            pe.wait_ge(rows_ready, 1)
            b = begin("vt")
            end("vt", pe.transpose(b[:, 0:R_END], rows[0:R_END, :], ident[0:R_END, 0:R_END]))
            ada_rows(2)
            turn_x(2)
            turn_x(3)
            begin("adaA")
            for n in (0, 1, 2):
                head_cols(n)
            ada_rows(3)
            end("adaA", head_cols(3))

            for k in range(4):
                pe.wait_ge(free_of(f"xT{k}"), AT[f"xT{k}"][1] + 1)

            def cols_of(b, lo, w, j):
                for c in range(KC):
                    ins = pe.matmul(b[:, lo:lo + 256], w[:, c, 128 * j:128 * j + 128], hT[:, c, :],
                                    start=(c == 0), stop=(c == KC - 1))
                return ins

            def tokens_of(b, lo, tt, w, first, width):
                for c in range(KC):
                    ins = pe.matmul(b[:, lo:lo + width], hT[:, c, 128 * tt:128 * tt + 128],
                                    w[:, c, first:first + width], start=(c == 0), stop=(c == KC - 1))
                return ins

            def bu(*tiles):
                if tiles[0] == 0:
                    pe.wait_ge(free_of("cT"), AT["cT"][1] + 1)
                    pe.wait_ge(free_of("bT"), AT["bT"][1] + 1)
                    pe.wait_ge(free_of("pu"), AT["pu"][1] + 1)
                banks = [begin(f"bu{i}") for i in tiles]
                last = [None] * len(tiles)
                for m in range(2):
                    for k, i in enumerate(tiles):
                        q, r = divmod(i, 4)
                        last[k] = pe.matmul(banks[k][:, 256 * m:256 * m + 256], bt[32 * r:32 * r + 32, 2 * m + q, :],
                                            uT[32 * r:32 * r + 32, q, :], start=True, stop=True,
                                            tile_position=(32 * r, 0))
                for k, i in enumerate(tiles):
                    end(f"bu{i}", last[k])

            def s5_out(i):
                q, r = divmod(i, 4)
                pe.wait_ge(s5_state, 2 * i + 1)
                b = begin("sy")
                for m in range(2):
                    ins = pe.matmul(b[32 * r:32 * r + 32, 256 * q:256 * q + 256], ct[:, 2 * m + q, 32 * r:32 * r + 32],
                                    s5tmp[:, 4, 256 * m:256 * m + 256], start=(m == 0), stop=(m == 1))
                if i < 7:
                    ins.then_inc(s5_state, 1)
                else:
                    end("sy", ins)

            w = view(ring[landed[("in", 0)][0]], BLK)
            pe.wait_ge(in0_half, 16)
            for k, g in enumerate(("pu", "pq", "pf")):
                b = begin(g)
                for m in range(2):
                    if (k, m) == (1, 1):
                        block_of(("in", 0))
                    ins = cols_of(b, 256 * m, w, 2 * k + m)
                end(g, ins)
            pe.wait_ge(bc_ready, 1)
            for r, g in enumerate(("bT", "cT")):
                b = begin(g)
                for m in range(4):
                    ins = pe.transpose(b[:, 128 * m:128 * m + 128], pools[:, r, m // 2, m % 2, :], ident[:, :])
                end(g, ins)

            w = view(block_of(("in", 1)), BLK)
            for tt in range(TT):
                b = begin(f"vg{tt}")
                ins = tokens_of(b, 0, tt, w, 0, 512)
                end(f"vg{tt}", ins)
                if tt == 0:
                    bu(0, 1)
            b = begin("mq")
            for tt in range(TT):
                ins = tokens_of(b, 256 * tt, tt, w, 512, 256)
            end("mq", ins)
            w = view(block_of(("in", 2)), 512)
            for tt in range(TT):
                if tt == 0:
                    bu(2, 3)
                s5_out(tt)
                b = begin(f"kv{tt}")
                ins = tokens_of(b, 0, tt, w, 0, 512)
                end(f"kv{tt}", ins)
            s5_out(2)

            def gate_tile(t):
                b = begin(f"g{t}")
                w = view(block_of(("in", 3 + t // 6)), BLK)
                end(f"g{t}", cols_of(b, 0, w, t % 6))
                if t in COLS_AFTER:
                    ada_cols(COLS_AFTER[t])
                if t in ROWS_AFTER:
                    ada_rows(ROWS_AFTER[t])

            def turn_qk(src, g):
                pe.wait_ge(qknorm_ready, 2)
                b = begin(g)
                for c in range(2):
                    for tt in range(TT):
                        ins = pe.transpose(b[:, 256 * c + 128 * tt:256 * c + 128 * tt + 128],
                                           src[:, tt, 128 * c:128 * c + 128], ident[:, :])
                end(g, ins)

            def scores(h):
                if h == 0:
                    for g in ("qT", "kT"):
                        pe.wait_ge(free_of(g), AT[g][1] + 1)
                b = begin(f"sc{h}")
                pr, c = slice(64 * (h % 2), 64 * (h % 2) + 64), h // 2
                pe.matmul(b[:, 0:128], qn[pr, c, 0:128], kn[pr, c, 0:128], start=True, stop=True)
                ins = pe.matmul(b[:, 128:384], qn[pr, c, 128:256], kn[pr, c, 0:256], start=True, stop=True)
                end(f"sc{h}", ins)

            def turn_probs(h):
                pe.wait_ge(prob_ready, 2 * h + 2)
                b = begin(f"pT{h}")
                for m in range(3):
                    ins = pe.transpose(b[:, 128 * m:128 * m + 128], prob[:, h % 2, 128 * m:128 * m + 128], ident[:, :])
                end(f"pT{h}", ins)

            def attend():
                b = begin("mo")
                for h in range(HEADS):
                    pe.wait_ge(free_of(f"pT{h}"), AT[f"pT{h}"][1] + 1)
                for g in ("kv0", "kv1"):
                    pe.wait_ge(free_of(g), AT[g][1] + 1)
                for h in range(HEADS):
                    po, c = slice(64 * (h % 2), 64 * (h % 2) + 64), 256 * (h // 2)
                    hd = slice(HD * h, HD * h + HD)
                    pe.matmul(b[po, c:c + 128], mv[:, 0, hd], probT[:, h, 0:128], start=True, stop=True)
                    pe.matmul(b[po, c + 128:c + 256], mv[:, 0, hd], probT[:, h, 128:256], start=True, stop=False)
                    ins = pe.matmul(b[po, c + 128:c + 256], mv[:, 1, hd], probT[:, h, 256:384], start=False, stop=True)
                end("mo", ins)

            def level(k):
                lv = 0 if k == 0 else LEVELS[k - 1]
                q_, k_ = (qT, key) if k == 0 else (qe, ke)
                if k == 0:
                    pe.wait_ge(f_ready, 1)
                    pe.wait_ge(free_of("pq"), AT["pq"][1] + 1)
                else:
                    pe.wait_ge(lv_ready, 2 * k)
                pairs = [(c, tt, tt) for c in range(2) for tt in range(TT)] if lv < 128 else [(0, 0, 1), (1, 0, 1)]
                banks = [begin(f"L{lv}{g}") for g in "ab"]
                last = [None, None]
                for m, (c, ks, qs) in enumerate(pairs):
                    for odd in range(2):
                        pr = slice(64 * odd, 64 * odd + 64)
                        last[odd] = pe.matmul(banks[odd][:, 128 * m:128 * m + 128], k_[pr, c, 128 * ks:128 * ks + 128],
                                              q_[pr, c, 128 * qs:128 * qs + 128], start=True, stop=True)
                for odd, g in enumerate("ab"):
                    end(f"L{lv}{g}", last[odd])

            gate_tile(0)
            for i in range(4, 8):
                if i % 2 == 0:
                    bu(i, i + 1)
                s5_out(i - 1)
                gate_tile(i - 3)
                if i == 5:
                    turn_qk(mq, "qT")
                    turn_qk(mk, "kT")
            gate_tile(5)
            s5_out(7)
            scores(0)
            scores(1)
            gate_tile(6)
            scores(2)
            scores(3)
            gate_tile(7)
            turn_probs(0)
            turn_probs(1)
            gate_tile(8)
            gate_tile(9)
            turn_probs(2)
            turn_probs(3)
            gate_tile(10)
            attend()
            gate_tile(11)
            level(0)
            for k in range(len(LEVELS)):
                gate_tile(12 + k)
                level(k + 1)
            gate_tile(20)
            gate_tile(21)
            pe.wait_ge(score_ready, 1)
            pe.wait_ge(free_of("L128b"), AT["L128b"][1] + 1)
            pe.wait_ge(vals_ready, 2)
            b = begin("ho")
            for h in range(HEADS):
                hd = slice(HD * h, HD * h + HD)
                o0, o1 = b[:, HD * h:HD * h + HD], b[:, 256 + HD * h:256 + HD * h + HD]
                n0, nx = 4 * (h % 2) + 2 * (h // 2), 2 * (h % 2) + h // 2
                pe.matmul(o0, score_h[:, n0, :], hi[:, 0, hd], start=True, stop=True)
                pe.matmul(o1, score_x[:, nx, :], hi[:, 0, hd], start=True, stop=False)
                ins = pe.matmul(o1, score_h[:, n0 + 1, :], hi[:, 1, hd], start=False, stop=True)
            end("ho", ins)
            gate_tile(22)
            gate_tile(23)

            def rows_from(r, k):
                for h in range(2):
                    b = begin(f"{r}{h}")
                    for c in range(4):
                        pe.wait_ge(diag_ready, 8 * k + 4 * h + c + 1)
                        ins = pe.matmul(b[:, 128 * c:128 * c + 128], ones[:, :], diag[:, 4 * h + c, :],
                                        start=True, stop=True)
                    end(f"{r}{h}", ins)

            rows_from("g1r", 0)
            pe.wait_ge(o_ready, 1)
            b = begin("hoT")
            for c in range(2):
                for tt in range(TT):
                    ins = pe.transpose(b[:, 256 * c + 128 * tt:256 * c + 128 * tt + 128],
                                       tmp[:, 256 * tt + 128 * c:256 * tt + 128 * c + 128], ident[:, :])
            end("hoT", ins)
            glu = block_of(("glu", 0))[:, 0:4096].rearrange("p (c n) -> p c n", c=2)
            wo = ring[landed[("wo", 0)][0]]
            who = wo[:, 0:2048].rearrange("p (c n) -> p c n", c=2)
            wmo = wo[:, 2048:4096].rearrange("p (c n) -> p c n", c=2)
            pe.wait_ge(s5_ready, 1)
            pe.wait_ge(free_of("hoT"), AT["hoT"][1] + 1)
            pe.wait_ge(free_of("mo"), AT["mo"][1] + 1)
            for j in range(KC):
                for g, pair in ((f"za{j}", ((glu, j, uT), (glu, 8 + j, uT))), (f"yb{j}", ((who, j, ogT), (wmo, j, mo)))):
                    if g == "yb0":
                        block_of(("wo", 0))
                    b = begin(g)
                    for m, (w, jj, x) in enumerate(pair):
                        for c in range(2):
                            ins = pe.matmul(b[:, 256 * m:256 * m + 256], w[:, c, 128 * jj:128 * jj + 128], x[:, c, :],
                                            start=(c == 0), stop=(c == 1))
                    end(g, ins)
                if j == 1:
                    ada_rows(11)
                if j == 3:
                    ada_cols(11)
            for tt in range(TT):
                for h in range(2):
                    w = block_of(("out", h))[:, 0:4096].rearrange("p (c n) -> p c n", c=KC)
                    b = begin(f"wo{tt}{h}")
                    for c in range(KC):
                        if tt == 0 and h == 0:
                            pe.wait_ge(merged_ready, c + 1)
                        ins = pe.matmul(b[:, :], merged[:, c, 128 * tt:128 * tt + 128], w[:, c, :],
                                        start=(c == 0), stop=(c == KC - 1))
                    end(f"wo{tt}{h}", ins)
            rows_from("g2r", 1)
            for tt in range(TT):
                pe.wait_ge(h2_ready, 2 * tt + 2)
                for k in range(4):
                    b = begin(f"hT{k}") if tt == 0 else ps[AT[f"hT{k}"][0]]
                    for c in (2 * k, 2 * k + 1):
                        lo = 256 * (c % 2) + 128 * tt
                        ins = pe.transpose(b[:, lo:lo + 128], hp[:, tt, 128 * c:128 * c + 128], ident[:, :])
                    if tt:
                        end(f"hT{k}", ins)
            pe.wait_ge(router_in, 16)
            for k in range(4):
                pe.wait_ge(free_of(f"hT{k}"), AT[f"hT{k}"][1] + 1)
            b = begin("rt")
            for tt in range(TT):
                for c in range(KC):
                    ins = pe.matmul(b[:, E * tt:E * tt + E], h2T[:, c, 128 * tt:128 * tt + 128], router[:, c, :],
                                    start=(c == 0), stop=(c == KC - 1))
            end("rt", ins)
            pe.wait_ge(shared_in, 32)

            def shared_up(g, base, j):
                b = begin(g) if j == 0 else ps[AT[g][0]]
                wv = shared_gu[:, base:base + 2048].rearrange("p (c n) -> p c n", c=KC)
                for c in range(KC):
                    ins = pe.matmul(b[:, 256 * j:256 * j + 256], wv[:, c, 128 * j:128 * j + 128], h2T[:, c, :],
                                    start=(c == 0), stop=(c == KC - 1))
                if j:
                    end(g, ins)

            def prefix():
                b = begin("ps")
                pe.wait_ge(mask_ready, 1)
                pe.wait_ge(consts, 5)
                pe.matmul(b[:, 0:E], before[:, :], m_r[:, 0, :], start=True, stop=True)
                pe.matmul(b[:, E:2 * E], ones[:, :], m_r[:, 0, :], start=True, stop=False)
                pe.matmul(b[:, E:2 * E], before[:, :], m_r[:, 1, :], start=False, stop=True)
                pe.matmul(b[:, 2 * E:3 * E], ones[:, :], m_r[:, 0, :], start=True, stop=False)
                end("ps", pe.matmul(b[:, 2 * E:3 * E], ones[:, :], m_r[:, 1, :], start=False, stop=True))

            shared_up("sh0", 0, 0)
            shared_up("sh0", 0, 1)
            shared_up("sh1", 2048, 0)
            prefix()
            shared_up("sh1", 2048, 1)
            def gather_half(h, buf):
                for cc in range(4):
                    c = 4 * h + cc
                    for m, (tt, part) in enumerate([(tt, part) for tt in range(TT) for part in range(3)]):
                        ins = pe.matmul(ps[4 + h][:, 128 * cc:128 * cc + 128], parts[part][:, tt, 128 * c:128 * c + 128],
                                        sel[buf][:, tt, :], start=(m == 0), stop=(m == 5))
                ins.then_inc(g_done, 1)

            def gate_up(k):
                for c in range(KC):
                    for x in range(2):
                        w = ering[2 * k + x][:, 0:4096].rearrange("p (m c n) -> p c m n", m=2, c=KC)[:, c, :, :]
                        ins = pe.matmul(ps[5][SLOTS * x:SLOTS * x + SLOTS, :].rearrange("p (m n) -> p m n", m=2),
                                        xe[:, c, SLOTS * x:SLOTS * x + SLOTS], w,
                                        start=(c == 0), stop=(c == KC - 1), skip_group_check=True)
                ins.then_inc(gu_done, 1)

            def down_half(k, h, bank):
                for j in range(2):
                    for x in range(2):
                        w = ering[2 * k + x][:, 4096 + D * j + 512 * h:4096 + D * j + 512 * h + 512]
                        ins = pe.matmul(ps[bank][SLOTS * x:SLOTS * x + SLOTS, :],
                                        hid[:, j, SLOTS * x:SLOTS * x + SLOTS], w,
                                        start=(j == 0), stop=(j == 1), skip_group_check=True)
                ins.then_inc(y_done, 1)

            def scatter_half(h):
                for tt in range(TT):
                    ins = pe.matmul(ps[2 * tt + h][:, :], swt[:, 128 * tt:128 * tt + 128], ysb[:, 512 * h:512 * h + 512],
                                    start=False, stop=False, skip_group_check=True)
                return ins

            pe.wait_ge(shared_dn_in, 16)
            pe.wait_ge(free_of("sh1"), AT["sh1"][1] + 1)
            for q in range(8):
                pe.wait_ge(bank_free[q], LAST_FREE[q])
            sd = shared_dn.rearrange("p (c n) -> p c n", c=2)

            def shared_down(q):
                tt, h = divmod(q, 2)
                for j in range(2):
                    ins = pe.matmul(ps[q][:, :], hidS[:, j, 128 * tt:128 * tt + 128], sd[:, j, 512 * h:512 * h + 512],
                                    start=(j == 0), stop=False, skip_group_check=True)

            shared_down(0)
            shared_down(1)
            pe.wait_ge(part_ready, 2)
            pe.wait_ge(sel_ready, 4)
            gather_half(0, 0)
            gather_half(1, 0)
            shared_down(2)
            shared_down(3)
            for s in (y0_full, y1_full, hid_made, hid_turned, hid_full, swt_done, acc_done):
                pe.sem_inc(s, 1)
            pe.wait_ge(rounds_ready, 1)
            n_rounds = pe.value_load(rounds_i[0:1, 0:1], min_val=1, max_val=MAX_ROUNDS)
            with pe.Fori(0, n_rounds * (E // 4)) as i:
                for k in range(2):
                    p = i * 2 + k
                    pe.wait_ge(gu_full[2 * k], 32 * i + 32)
                    pe.wait_ge(gu_full[2 * k + 1], 32 * i + 32)
                    pe.wait_ge(xe_full, 2 * p + 2)
                    gate_up(k)
                    pe.wait_ge(sel_ready, 4 * p + 6)
                    gather_half(0, 1 - k)
                    pe.wait_ge(y0_full, p + 1)
                    for tt in range(TT):
                        ins = pe.transpose(ps[7][:, 128 * tt:128 * tt + 128], selw[k][:, tt, :], ident[:, :])
                    ins.then_inc(swt_done, 1)
                    pe.wait_ge(y1_full, p + 1)
                    pe.wait_ge(hid_made, p + 2)
                    for j in range(2):
                        ins = pe.transpose(ps[6][:, 128 * j:128 * j + 128], hid_t[:, 128 * j:128 * j + 128], ident[:, :])
                    ins.then_inc(hid_turned, 1)
                    gather_half(1, 1 - k)
                    pe.wait_ge(dn_full[2 * k], 16 * i + 16)
                    pe.wait_ge(dn_full[2 * k + 1], 16 * i + 16)
                    pe.wait_ge(swt_full, p + 1)
                    pe.wait_ge(hid_full, p + 2)
                    down_half(k, 0, 7)
                    down_half(k, 1, 6)
                    pe.wait_ge(y0_full, p + 2)
                    scatter_half(0).then_inc(acc0_done, 1)
                    pe.wait_ge(y1_full, p + 2)
                    scatter_half(1).then_inc(acc_done, 1)


LAST_GROUP = {("in", 0): "pf", ("in", 1): "mq", ("in", 2): "kv1",
              ("glu", 0): "za7", ("wo", 0): "yb7", ("out", 0): "wo11", ("out", 1): "wo11"}
LAST_GROUP.update({("in", 3 + _n): f"g{6 * _n + 5}" for _n in range(4)})

LAST_FREE = [0] * 8
for _name, (_b, _n) in AT.items():
    LAST_FREE[_b] = max(LAST_FREE[_b], _n + 1)

_INS = ["x", "c", "ada_w", "ada_b", "norm1_g", "w_in", "ssm_log_dt", "ssm_lambda_re", "ssm_lambda_im",
        "ssm_b_re", "ssm_b_im", "ssm_c_re", "ssm_c_im", "ssm_d", "ssm_w_glu", "hgrn_lb_logits",
        "hgrn_norm_g", "hgrn_w_o", "moba_q_norm_g", "moba_k_norm_g", "moba_w_o", "w_out", "norm2_g",
        "router_w", "router_bias", "exp_w_gate", "exp_w_up", "exp_w_down", "shared_w_gate",
        "shared_w_up", "shared_w_down"]


def kernel(**inputs):
    import numpy as _np
    import concourse.bacc as _bacc
    from concourse.bass_utils import run_bass_kernel_spmd as _run

    nc = _bacc.Bacc("TRN2", target_bir_lowering=False, num_devices=1)
    arrays, aps = {}, {}
    for name in _INS:
        v = _np.ascontiguousarray(inputs[name])
        arrays[f"in_{name}"] = v
        aps[name] = nc.dram_tensor(f"in_{name}", v.shape, mybir.dt.from_np(v.dtype), kind="ExternalInput").ap()
    out = nc.dram_tensor("out_0", (1, T, D), F32, kind="ExternalOutput").ap()
    build(nc, aps, out)
    r = _run(nc, [arrays], core_ids=[0])
    return r.results[0]["out_0"]
```
